# Optimizing a Trainium2 kernel written in Bass

```python
import math
import jax, jax.numpy as jnp
from jax import lax
import numpy as np

D_MODEL = 1024
BATCH = 1
SEQ = 256
DEPTH = 2

HEAD_DIM = 64
ROPE_THETA = 10000.0
Q_BLOCK = 128
LN_EPS = 1e-5

A_HEADS = 4
A_KV_RANK = 128
A_IDX_HEADS = 4
A_IDX_DIM = 64
A_TOPK_MAX = 256

B_HEADS = 4
B_BLOCK = 256
B_TOPK_BLOCKS = 3

C_HEADS = 8
C_KV_HEADS = 2
C_WINDOW = 128

N_BRANCH = 3
A_W = A_HEADS * HEAD_DIM
B_W = B_HEADS * HEAD_DIM
C_W = C_HEADS * HEAD_DIM
MIX_W = A_W + B_W + C_W

IN_SIZES = (A_W, A_KV_RANK, A_IDX_HEADS * A_IDX_DIM, A_IDX_DIM, A_IDX_HEADS,
            B_W, B_W, B_W,
            C_W, C_KV_HEADS * HEAD_DIM, C_KV_HEADS * HEAD_DIM,
            N_BRANCH * D_MODEL)
N_IN = sum(IN_SIZES)

N_EXPERTS = 16
N_GROUPS = 4
EXPERTS_PER_GROUP = N_EXPERTS // N_GROUPS
TOP_K = 2
D_EXPERT = 512

DN_ALPHA = (2 * DEPTH) ** 0.25
DN_BETA = (8 * DEPTH) ** -0.25


def _split_points(sizes):
    pts, acc = [], 0
    for s in sizes[:-1]:
        acc += s
        pts.append(acc)
    return pts

def layer_norm(x, g, b):
    xf = x.astype(jnp.float32)
    mu = jnp.mean(xf, -1, keepdims=True)
    var = jnp.mean(jnp.square(xf - mu), -1, keepdims=True)
    return ((xf - mu) * lax.rsqrt(var + LN_EPS) * g + b).astype(x.dtype)

def rope_tables(seq_len, dim):
    inv = 1.0 / (ROPE_THETA ** (jnp.arange(0, dim, 2, dtype=jnp.float32) / dim))
    ang = jnp.arange(seq_len, dtype=jnp.float32)[:, None] * inv[None, :]
    return jnp.cos(ang), jnp.sin(ang)

def apply_rope(t, cos, sin):
    t1, t2 = jnp.split(t, 2, axis=-1)
    c = cos[None, :, None, :].astype(t.dtype)
    s = sin[None, :, None, :].astype(t.dtype)
    return jnp.concatenate([t1 * c - t2 * s, t2 * c + t1 * s], axis=-1)

def dsa_attention(q, k, v, iq, ik, iw):
    Bn, S, HA, dh = q.shape
    topk = min(A_TOPK_MAX, S // 4)
    nqb = S // Q_BLOCK
    scale = dh ** -0.5
    key_pos = jnp.arange(S)
    gather = jax.vmap(lambda arr, idx: arr[idx])

    def block(i):
        t0 = i * Q_BLOCK
        qb = lax.dynamic_slice_in_dim(q, t0, Q_BLOCK, 1)
        iqb = lax.dynamic_slice_in_dim(iq, t0, Q_BLOCK, 1)
        iwb = lax.dynamic_slice_in_dim(iw, t0, Q_BLOCK, 1)
        qpos = t0 + jnp.arange(Q_BLOCK)
        dots = jnp.einsum('bqhd,bsd->bqhs', iqb, ik)
        score = jnp.einsum('bqh,bqhs->bqs', iwb, jax.nn.relu(dots)).astype(jnp.float32)
        causal = key_pos[None, :] <= qpos[:, None]
        score = jnp.where(causal[None], score, -jnp.inf)
        _, idx = lax.top_k(score, topk)
        valid = idx <= qpos[None, :, None]
        kg = gather(k, idx)
        vg = gather(v, idx)
        s = jnp.einsum('bqhd,bqkd->bhqk', qb, kg).astype(jnp.float32) * scale
        s = jnp.where(valid[:, None], s, -jnp.inf)
        p = jax.nn.softmax(s, axis=-1).astype(v.dtype)
        return jnp.einsum('bhqk,bqkd->bqhd', p, vg)

    out = lax.map(block, jnp.arange(nqb))
    return out.transpose(1, 0, 2, 3, 4).reshape(Bn, S, HA * dh)

def moba_attention(q, k, v):
    Bn, S, H, dh = q.shape
    nkb = -(-S // B_BLOCK)
    pad = nkb * B_BLOCK - S
    kp = jnp.pad(k, ((0, 0), (0, pad), (0, 0), (0, 0)))
    vp = jnp.pad(v, ((0, 0), (0, pad), (0, 0), (0, 0)))
    kblk = kp.reshape(Bn, nkb, B_BLOCK, H, dh)
    vblk = vp.reshape(Bn, nkb, B_BLOCK, H, dh)
    kmean = jnp.mean(kblk, axis=2)
    kbt = kblk.transpose(0, 3, 1, 2, 4)
    vbt = vblk.transpose(0, 3, 1, 2, 4)
    nsel = min(B_TOPK_BLOCKS, nkb)
    nqb = S // Q_BLOCK
    scale = dh ** -0.5
    gather_bh = jax.vmap(jax.vmap(lambda arr, idx: arr[idx]))
    blk_ids = jnp.arange(nkb)

    def block(i):
        t0 = i * Q_BLOCK
        cur = t0 // B_BLOCK
        qb = lax.dynamic_slice_in_dim(q, t0, Q_BLOCK, 1)
        qpos = t0 + jnp.arange(Q_BLOCK)
        gate = jnp.einsum('bqhd,bnhd->bhqn', qb, kmean).astype(jnp.float32)
        gate = jnp.where(blk_ids < cur, gate, -jnp.inf)
        _, sel = lax.top_k(gate, nsel)
        sel_valid = sel < cur
        kg = gather_bh(kbt, sel)
        vg = gather_bh(vbt, sel)
        s_sel = jnp.einsum('bqhd,bhqnkd->bhqnk', qb, kg).astype(jnp.float32) * scale
        s_sel = jnp.where(sel_valid[..., None], s_sel, -jnp.inf)
        s_sel = s_sel.reshape(Bn, H, Q_BLOCK, nsel * B_BLOCK)
        k_own = lax.dynamic_slice_in_dim(kp, cur * B_BLOCK, B_BLOCK, 1)
        v_own = lax.dynamic_slice_in_dim(vp, cur * B_BLOCK, B_BLOCK, 1)
        own_pos = cur * B_BLOCK + jnp.arange(B_BLOCK)
        s_own = jnp.einsum('bqhd,bkhd->bhqk', qb, k_own).astype(jnp.float32) * scale
        s_own = jnp.where((own_pos[None, :] <= qpos[:, None])[None, None], s_own, -jnp.inf)
        p = jax.nn.softmax(jnp.concatenate([s_own, s_sel], axis=-1), axis=-1).astype(v.dtype)
        p_own = p[..., :B_BLOCK]
        p_sel = p[..., B_BLOCK:].reshape(Bn, H, Q_BLOCK, nsel, B_BLOCK)
        return (jnp.einsum('bhqk,bkhd->bqhd', p_own, v_own)
                + jnp.einsum('bhqnk,bhqnkd->bqhd', p_sel, vg))

    out = lax.map(block, jnp.arange(nqb))
    return out.transpose(1, 0, 2, 3, 4).reshape(Bn, S, H * dh)

def swa_sink_attention(q, k, v, sinks):
    Bn, S, HC, dh = q.shape
    KV = k.shape[2]
    G = HC // KV
    W = C_WINDOW
    nb = S // W
    scale = dh ** -0.5
    qb = q.reshape(Bn, nb, W, KV, G, dh)
    kb = k.reshape(Bn, nb, W, KV, dh)
    vb = v.reshape(Bn, nb, W, KV, dh)
    kband = jnp.concatenate([jnp.pad(kb, ((0, 0), (1, 0), (0, 0), (0, 0), (0, 0)))[:, :-1], kb], axis=2)
    vband = jnp.concatenate([jnp.pad(vb, ((0, 0), (1, 0), (0, 0), (0, 0), (0, 0)))[:, :-1], vb], axis=2)
    s = jnp.einsum('bnqkgd,bnskd->bnkgqs', qb, kband).astype(jnp.float32) * scale
    qrel = jnp.arange(W)[:, None] + W
    krel = jnp.arange(2 * W)[None, :]
    diff = qrel - krel
    kabs = jnp.arange(nb)[:, None, None] * W - W + krel[None]
    mask = (diff >= 0)[None] & (diff < W)[None] & (kabs >= 0)
    s = jnp.where(mask[None, :, None, None], s, -jnp.inf)
    sink = jnp.broadcast_to(sinks.astype(jnp.float32).reshape(1, 1, KV, G, 1, 1), s.shape[:-1] + (1,))
    p = jax.nn.softmax(jnp.concatenate([s, sink], axis=-1), axis=-1)[..., :-1].astype(v.dtype)
    out = jnp.einsum('bnkgqs,bnskd->bnqkgd', p, vband)
    return out.reshape(Bn, S, HC * dh)

def mixer(x, w_in, a_w_uk, a_w_uv, c_sinks, w_branch, w_o, cos, sin):
    Bn, S, _ = x.shape
    h = x @ w_in
    (a_q, a_c, a_iq, a_ik, a_iw, b_q, b_k, b_v, c_q, c_k, c_v, gates) = jnp.split(
        h, _split_points(IN_SIZES), axis=-1)
    heads = lambda t, n: t.reshape(Bn, S, n, -1)
    qa = apply_rope(heads(a_q, A_HEADS), cos, sin)
    ka = apply_rope((a_c @ a_w_uk)[:, :, None, :], cos, sin)[:, :, 0]
    va = a_c @ a_w_uv
    iq = apply_rope(heads(a_iq, A_IDX_HEADS), cos, sin)
    ik = apply_rope(a_ik[:, :, None, :], cos, sin)[:, :, 0]
    o_a = dsa_attention(qa, ka, va, iq, ik, a_iw)
    o_b = moba_attention(apply_rope(heads(b_q, B_HEADS), cos, sin),
                         apply_rope(heads(b_k, B_HEADS), cos, sin),
                         heads(b_v, B_HEADS))
    o_c = swa_sink_attention(apply_rope(heads(c_q, C_HEADS), cos, sin),
                             apply_rope(heads(c_k, C_KV_HEADS), cos, sin),
                             heads(c_v, C_KV_HEADS), c_sinks)
    wa, wb, wc = jnp.split(w_branch, [A_W, A_W + B_W], axis=0)
    ga, gb, gc = jnp.split(jax.nn.sigmoid(gates), N_BRANCH, axis=-1)
    merged = ga * (o_a @ wa) + gb * (o_b @ wb) + gc * (o_c @ wc)
    return merged @ w_o

def moe(x, router_w, router_b, w_gate, w_up, w_down):
    Bn, S, D = x.shape
    xt = x.reshape(-1, D)
    aff = jax.nn.sigmoid((xt @ router_w).astype(jnp.float32))
    sel_score = aff + router_b.astype(jnp.float32)
    grp_score = lax.top_k(sel_score.reshape(-1, N_GROUPS, EXPERTS_PER_GROUP), TOP_K)[0].sum(-1)
    g_star = jnp.argmax(grp_score, axis=-1)
    in_group = (jnp.arange(N_EXPERTS) // EXPERTS_PER_GROUP)[None, :] == g_star[:, None]
    _, top_idx = lax.top_k(jnp.where(in_group, sel_score, -jnp.inf), TOP_K)
    top_aff = jnp.take_along_axis(aff, top_idx, axis=-1)
    wts = top_aff / jnp.sum(top_aff, -1, keepdims=True)
    combine = jnp.sum(jax.nn.one_hot(top_idx, N_EXPERTS, dtype=jnp.float32) * wts[..., None], axis=1)
    combine = combine.astype(x.dtype)
    y = jnp.zeros_like(xt)
    for e in range(N_EXPERTS):
        he = jax.nn.silu(xt @ w_gate[e]) * (xt @ w_up[e])
        y = y + combine[:, e:e + 1] * (he @ w_down[e])
    return y.reshape(Bn, S, D)

def first_inputs(seed: int = 0) -> dict:
    key = jax.random.key(seed)
    ks = jax.random.split(key, 20)
    nrm = lambda k, shape, scale: jax.random.normal(k, shape, jnp.float32) * scale
    w_branch = jnp.concatenate([
        nrm(ks[5], (DEPTH, A_W, D_MODEL), A_W ** -0.5),
        nrm(ks[6], (DEPTH, B_W, D_MODEL), B_W ** -0.5),
        nrm(ks[7], (DEPTH, C_W, D_MODEL), C_W ** -0.5)], axis=1)
    return {
        "x": nrm(ks[0], (BATCH, SEQ, D_MODEL), 1.0),
        "w_in": nrm(ks[1], (DEPTH, D_MODEL, N_IN), D_MODEL ** -0.5),
        "a_w_uk": nrm(ks[2], (DEPTH, A_KV_RANK, HEAD_DIM), A_KV_RANK ** -0.5),
        "a_w_uv": nrm(ks[3], (DEPTH, A_KV_RANK, HEAD_DIM), A_KV_RANK ** -0.5),
        "c_sinks": nrm(ks[4], (DEPTH, C_HEADS), 1.0),
        "w_branch": w_branch,
        "w_o": nrm(ks[8], (DEPTH, D_MODEL, D_MODEL), D_MODEL ** -0.5 * DN_BETA),
        "ln1_g": 1.0 + nrm(ks[9], (DEPTH, D_MODEL), 0.01),
        "ln1_b": nrm(ks[10], (DEPTH, D_MODEL), 0.01),
        "router_w": nrm(ks[11], (D_MODEL, N_EXPERTS), D_MODEL ** -0.5),
        "router_b": nrm(ks[12], (N_EXPERTS,), 0.01),
        "moe_w_gate": nrm(ks[13], (DEPTH, N_EXPERTS, D_MODEL, D_EXPERT), D_MODEL ** -0.5),
        "moe_w_up": nrm(ks[14], (DEPTH, N_EXPERTS, D_MODEL, D_EXPERT), D_MODEL ** -0.5),
        "moe_w_down": nrm(ks[15], (DEPTH, N_EXPERTS, D_EXPERT, D_MODEL), D_EXPERT ** -0.5 * DN_BETA),
        "ln2_g": 1.0 + nrm(ks[16], (DEPTH, D_MODEL), 0.01),
        "ln2_b": nrm(ks[17], (DEPTH, D_MODEL), 0.01),
    }

def first_block(x, w_in, a_w_uk, a_w_uv, c_sinks, w_branch, w_o, ln1_g, ln1_b,
              router_w, router_b, moe_w_gate, moe_w_up, moe_w_down, ln2_g, ln2_b):
    S = x.shape[1]
    cos, sin = rope_tables(S, HEAD_DIM)
    for l in range(DEPTH):
        y = mixer(x, w_in[l], a_w_uk[l], a_w_uv[l], c_sinks[l], w_branch[l], w_o[l], cos, sin)
        x = layer_norm(DN_ALPHA * x + y, ln1_g[l], ln1_b[l])
        y = moe(x, router_w, router_b, moe_w_gate[l], moe_w_up[l], moe_w_down[l])
        x = layer_norm(DN_ALPHA * x + y, ln2_g[l], ln2_b[l])
    return x


CHUNK = 64
N_BRANCHES = 3
BRANCH_WIDTH = 512
SB_HEADS = 8
SB_HEAD_DIM = BRANCH_WIDTH // SB_HEADS
CONV_CHANNELS = BRANCH_WIDTH
CONV_WIDTH = 31
GLA_HEADS = 4
GLA_KEY_DIM = BRANCH_WIDTH // 2
GLA_VALUE_DIM = BRANCH_WIDTH
GLA_HEAD_K = GLA_KEY_DIM // GLA_HEADS
GLA_HEAD_V = GLA_VALUE_DIM // GLA_HEADS
GLA_GATE_RANK = 16
GLA_GATE_TAU = 16.0
D_FF = 2816
NORM_EPS = 1e-6

IN_WIDTHS = (
    BRANCH_WIDTH, BRANCH_WIDTH, BRANCH_WIDTH,
    2 * CONV_CHANNELS,
    GLA_KEY_DIM, GLA_KEY_DIM, GLA_VALUE_DIM,
    GLA_VALUE_DIM,
    GLA_GATE_RANK,
    N_BRANCHES * D_MODEL,
)
IN_WIDTH = sum(IN_WIDTHS)


def rms_norm(x, g):
    xf = x.astype(jnp.float32)
    y = xf * lax.rsqrt(jnp.mean(xf * xf, axis=-1, keepdims=True) + NORM_EPS)
    return (y * g.astype(jnp.float32)).astype(x.dtype)

def swiglu_ffn(h, w_gate, w_up, w_down):
    return (jax.nn.silu(h @ w_gate) * (h @ w_up)) @ w_down

def stick_breaking_attention(q, k, v):
    b, nh, s, dh = q.shape
    nb = s // Q_BLOCK
    q_blocks = q.reshape(b, nh, nb, Q_BLOCK, dh).transpose(2, 0, 1, 3, 4)
    key_pos = jnp.arange(s)
    scale = dh ** -0.5

    def one_block(args):
        q_blk, blk = args
        z = jnp.einsum('bhqd,bhkd->bhqk', q_blk, k).astype(jnp.float32) * scale
        query_pos = blk * Q_BLOCK + jnp.arange(Q_BLOCK)
        earlier = key_pos[None, :] < query_pos[:, None]
        log_keep = jnp.where(earlier, jax.nn.log_sigmoid(-z), 0.0)
        log_stick = lax.cumsum(log_keep, axis=3, reverse=True) - log_keep
        w = jnp.where(earlier, jnp.exp(jax.nn.log_sigmoid(z) + log_stick), 0.0)
        return jnp.einsum('bhqk,bhkd->bhqd', w.astype(v.dtype), v)

    out = lax.map(one_block, (q_blocks, jnp.arange(nb)))
    return out.transpose(1, 2, 0, 3, 4).reshape(b, nh, s, dh)

def conformer_conv(u_glu, conv_w, conv_b, ln_g, ln_b):
    a, g = jnp.split(u_glu, 2, axis=-1)
    u = a * jax.nn.sigmoid(g)
    y = lax.conv_general_dilated(
        u, conv_w[:, None, :], window_strides=(1,),
        padding=[(CONV_WIDTH - 1, 0)],
        dimension_numbers=('NWC', 'WIO', 'NWC'),
        feature_group_count=CONV_CHANNELS) + conv_b
    yf = y.astype(jnp.float32)
    mu = jnp.mean(yf, axis=-1, keepdims=True)
    var = jnp.mean(jnp.square(yf - mu), axis=-1, keepdims=True)
    yn = (yf - mu) * lax.rsqrt(var + NORM_EPS) * ln_g.astype(jnp.float32) + ln_b.astype(jnp.float32)
    return jax.nn.silu(yn).astype(u.dtype)

def gla_chunked(q, k, v, log_alpha):
    b, s, nh, dk = q.shape
    dv = v.shape[-1]
    n = s // CHUNK

    def to_chunks(t):
        return t.reshape(b, n, CHUNK, nh, t.shape[-1]).transpose(1, 0, 2, 3, 4)

    la_c = to_chunks(log_alpha.astype(jnp.float32))
    decay_to_end = lax.cumsum(la_c, axis=2, reverse=True) - la_c
    chunk_decay = jnp.exp(jnp.sum(la_c, axis=2))
    k_dec = to_chunks(k).astype(jnp.float32) * jnp.exp(decay_to_end)
    q_c = to_chunks(q).astype(jnp.float32) * (dk ** -0.5)
    v_c = to_chunks(v).astype(jnp.float32)

    def step(state, xs):
        q_n, k_n, v_n, lam = xs
        state = lam[..., None] * state + jnp.einsum('bchk,bchv->bhkv', k_n, v_n)
        return state, jnp.einsum('bchk,bhkv->bchv', q_n, state)

    state0 = jnp.zeros((b, nh, dk, dv), jnp.float32)
    _, o = lax.scan(step, state0, (q_c, k_dec, v_c, chunk_decay))
    return o.transpose(1, 0, 2, 3, 4).reshape(b, s, nh, dv).astype(v.dtype)

def hybrid_mixer(h, w_in, conv_w, conv_b, conv_ln_g, conv_ln_b,
                 gla_w_alpha, gla_b_alpha, gla_norm_g, w_branch, w_out):
    b, s, _ = h.shape
    proj = h @ w_in
    offsets = [int(o) for o in np.cumsum(IN_WIDTHS)[:-1]]
    (sb_q, sb_k, sb_v, conv_in, gla_q, gla_k, gla_v, gla_r, gla_lr,
     gate_logits) = jnp.split(proj, offsets, axis=-1)

    def heads(t, nh):
        return t.reshape(b, s, nh, -1)

    sb_out = stick_breaking_attention(
        heads(sb_q, SB_HEADS).transpose(0, 2, 1, 3),
        heads(sb_k, SB_HEADS).transpose(0, 2, 1, 3),
        heads(sb_v, SB_HEADS).transpose(0, 2, 1, 3))
    sb_out = sb_out.transpose(0, 2, 1, 3).reshape(b, s, BRANCH_WIDTH)

    conv_out = conformer_conv(conv_in, conv_w, conv_b, conv_ln_g, conv_ln_b)

    log_alpha = jax.nn.log_sigmoid((gla_lr @ gla_w_alpha + gla_b_alpha).astype(jnp.float32)) / GLA_GATE_TAU
    gla_o = gla_chunked(heads(gla_q, GLA_HEADS), heads(gla_k, GLA_HEADS),
                        heads(gla_v, GLA_HEADS), heads(log_alpha, GLA_HEADS))
    gla_o = rms_norm(gla_o, gla_norm_g.reshape(GLA_HEADS, GLA_HEAD_V))
    gla_out = gla_o.reshape(b, s, GLA_VALUE_DIM) * jax.nn.silu(gla_r)

    branches = jnp.stack([sb_out, conv_out, gla_out], axis=2)
    branch_d = jnp.einsum('bsgw,gwd->bsgd', branches, w_branch)
    gates = jax.nn.sigmoid(gate_logits.reshape(b, s, N_BRANCHES, D_MODEL))
    merged = jnp.sum(gates * branch_d, axis=2)
    return merged @ w_out

def second_inputs(seed: int = 0) -> dict:
    key = jax.random.key(seed)
    ks = jax.random.split(key, 20)

    def nrm(k, shape, scale):
        return jax.random.normal(k, shape, jnp.float32) * scale

    L, D = DEPTH, D_MODEL
    return {
        "x": nrm(ks[0], (BATCH, SEQ, D), 1.0),
        "norm_pre": 1.0 + nrm(ks[1], (L, 3, D), 0.05),
        "norm_post": 1.0 + nrm(ks[2], (L, 3, D), 0.05),
        "ffn1_w_gate": nrm(ks[3], (L, D, D_FF), D ** -0.5),
        "ffn1_w_up": nrm(ks[4], (L, D, D_FF), D ** -0.5),
        "ffn1_w_down": nrm(ks[5], (L, D_FF, D), D_FF ** -0.5),
        "ffn2_w_gate": nrm(ks[6], (L, D, D_FF), D ** -0.5),
        "ffn2_w_up": nrm(ks[7], (L, D, D_FF), D ** -0.5),
        "ffn2_w_down": nrm(ks[8], (L, D_FF, D), D_FF ** -0.5),
        "w_in": nrm(ks[9], (L, D, IN_WIDTH), D ** -0.5),
        "conv_w": nrm(ks[10], (L, CONV_WIDTH, CONV_CHANNELS), CONV_WIDTH ** -0.5),
        "conv_b": nrm(ks[11], (L, CONV_CHANNELS), 0.02),
        "conv_ln_g": 1.0 + nrm(ks[12], (L, CONV_CHANNELS), 0.05),
        "conv_ln_b": nrm(ks[13], (L, CONV_CHANNELS), 0.02),
        "gla_w_alpha": nrm(ks[14], (L, GLA_GATE_RANK, GLA_KEY_DIM), GLA_GATE_RANK ** -0.5),
        "gla_b_alpha": nrm(ks[15], (L, GLA_KEY_DIM), 0.02),
        "gla_norm_g": 1.0 + nrm(ks[16], (L, GLA_VALUE_DIM), 0.05),
        "w_branch": nrm(ks[17], (L, N_BRANCHES, BRANCH_WIDTH, D), BRANCH_WIDTH ** -0.5),
        "w_out": nrm(ks[18], (L, D, D), D ** -0.5),
    }

def second_block(x, norm_pre, norm_post, ffn1_w_gate, ffn1_w_up, ffn1_w_down,
              ffn2_w_gate, ffn2_w_up, ffn2_w_down, w_in, conv_w, conv_b,
              conv_ln_g, conv_ln_b, gla_w_alpha, gla_b_alpha, gla_norm_g,
              w_branch, w_out):
    for l in range(DEPTH):
        h = rms_norm(x, norm_pre[l, 0])
        x = x + 0.5 * rms_norm(swiglu_ffn(h, ffn1_w_gate[l], ffn1_w_up[l], ffn1_w_down[l]), norm_post[l, 0])
        h = rms_norm(x, norm_pre[l, 1])
        m = hybrid_mixer(h, w_in[l], conv_w[l], conv_b[l], conv_ln_g[l], conv_ln_b[l],
                         gla_w_alpha[l], gla_b_alpha[l], gla_norm_g[l], w_branch[l], w_out[l])
        x = x + rms_norm(m, norm_post[l, 1])
        h = rms_norm(x, norm_pre[l, 2])
        x = x + 0.5 * rms_norm(swiglu_ffn(h, ffn2_w_gate[l], ffn2_w_up[l], ffn2_w_down[l]), norm_post[l, 2])
    return x


def setup_inputs(seed=0):
    out = dict(first_inputs(seed))
    for name, value in second_inputs(seed + 1).items():
        if name != "x":
            out[name + "_2"] = value
    return out


def reference(
    x, w_in, a_w_uk, a_w_uv, c_sinks, w_branch, w_o, ln1_g, ln1_b, router_w, router_b,
    moe_w_gate, moe_w_up, moe_w_down, ln2_g, ln2_b, norm_pre_2, norm_post_2, ffn1_w_gate_2,
    ffn1_w_up_2, ffn1_w_down_2, ffn2_w_gate_2, ffn2_w_up_2, ffn2_w_down_2, w_in_2, conv_w_2,
    conv_b_2, conv_ln_g_2, conv_ln_b_2, gla_w_alpha_2, gla_b_alpha_2, gla_norm_g_2, w_branch_2,
    w_out_2,
):
    x = first_block(
        x, w_in, a_w_uk, a_w_uv, c_sinks, w_branch, w_o, ln1_g, ln1_b, router_w, router_b,
        moe_w_gate, moe_w_up, moe_w_down, ln2_g, ln2_b,
    )
    return second_block(
        x, norm_pre_2, norm_post_2, ffn1_w_gate_2, ffn1_w_up_2, ffn1_w_down_2, ffn2_w_gate_2,
        ffn2_w_up_2, ffn2_w_down_2, w_in_2, conv_w_2, conv_b_2, conv_ln_g_2, conv_ln_b_2,
        gla_w_alpha_2, gla_b_alpha_2, gla_norm_g_2, w_branch_2, w_out_2,
    )


_drawn_inputs = setup_inputs


def setup_inputs(seed=0):
    import zlib

    import numpy as np

    out = dict(_drawn_inputs(seed))
    spreads = {}
    factors = {'c_sinks': 4.986, 'conv_ln_b_2': 4.765, 'gla_b_alpha_2': 8.0}
    for name, (base, spread) in spreads.items():
        noise = np.random.default_rng([zlib.crc32(name.encode()), seed]).standard_normal(out[name].shape)
        drawn = base * np.exp(spread * noise) if base else spread * noise
        out[name] = __import__('jax').numpy.asarray(drawn.astype(out[name].dtype))
    for name, factor in factors.items():
        out[name] = (out[name] * factor).astype(out[name].dtype)
    return out
```

```python
from contextlib import ExitStack

import concourse.bass as bass
from concourse import mybir

F32 = mybir.dt.float32
F32R = mybir.dt.float32r
I32 = mybir.dt.int32
ALU = mybir.AluOpType
ACT = mybir.ActivationFunctionType
AX = mybir.AxisListType

P = 128
DM = 1024
TT = 2
DEPTH = 2
DH = 64
NEG = -1e30
TAKEN = -3e38
TOPK = 64
LN_EPS, RMS_EPS = 1e-5, 1e-6
ALPHA = (2 * DEPTH) ** 0.25
SCALE = DH ** -0.5
NE, NG, EPG, DE = 16, 4, 4, 512

RING = 3
UNIT = 2048
HALF = UNIT // 2
AHEAD = 5

A_Q, A_C, A_IQ, A_IK, A_IW, B_Q, B_K, B_V, C_Q, C_K, C_V, N_QKV = (
    0, 256, 384, 640, 704, 708, 964, 1220, 1476, 1988, 2116, 2244)
N_GATE = 3 * DM
RB_AQ, RB_IQ, RB_IKKA, RB_BQ, RB_BK, RB_CQ, RB_CK, RB_KAIK, RB_CK2, N_RB = 0, 2, 4, 5, 7, 9, 13, 14, 15, 16

U_LAYER, U_ROUND = 22 + 4 + 4, NE * 6
G_LAYER, G_ROUND = 40, 2 * NE + 4
T_LAYER, T_ROUND = 48, 4 + 6 * NG
S_LAYER, S_ROUND = 10, NG

DFF = 2816
N_IN2 = 7184
S_Q, S_K, S_V, CONV, L_Q, L_K, L_V, L_R, L_LR, GATE2 = 0, 512, 1024, 1536, 2560, 2816, 3072, 3584, 4096, 4112
TAPS = 31
N_PROJ2 = GATE2
PROJ2_ORDER = (3, 4, 0, 1, 5, 2, 6, 7)
FB = DFF // 256
U_FFN, U_MIX2 = 3 * FB, 2 * 8 + 1 + 12 + 6 + 4
U_LAYER2 = 2 * U_FFN + U_MIX2
G_MIX2, G_LAYER2 = 48, 56
T_FFN, T_MIX2 = 4 + 2 * FB, 44
T_LAYER2 = 2 * T_FFN + T_MIX2
S_FFN, S_MIX2 = FB, 4
S_LAYER2 = 2 * S_FFN + S_MIX2
XT_LAYER2 = 22
GATE2_G = (18, 20, 22, 24, 28, 30)


class At:

    def __init__(self, const, *terms):
        self.const, self.terms = const, terms

    def __add__(self, k):
        return At(self.const + k, *self.terms)

    def value(self, scale=1, more=0):
        v = self.const * scale + more
        for reg, step in self.terms:
            v = reg * (step * scale) + v
        return v

    def turn(self, n):
        assert all(step % n == 0 for _, step in self.terms), (self.terms, n)
        return At(self.const // n, *[(reg, step // n) for reg, step in self.terms])

    def slot(self, n):
        return self.const % n


def plan_mixer1():
    t, s, steps = 4 + 2, 0, []
    for j in range(8):
        steps.append(dict(kind="rt", j=j, t=t))
        t += 1
        if j in (2, 5):
            steps.append(dict(kind="gate", n=(2, 5).index(j)))
    for tt in range(TT):
        steps.append(dict(kind="index", tt=tt, s=s))
        s += 1
    n = 0
    for i, (grp, tt) in enumerate([(1, 0), (1, 1), (2, 0), (2, 1), (3, 0), (3, 1), (0, 0), (0, 1)]):
        steps.append(dict(kind="scores", grp=grp, tt=tt, n=i, s=s))
        s += 1
        if i in (1, 3, 5, 7):
            steps.append(dict(kind="gate", n=2 + (i - 1) // 2))
        steps.append(dict(kind="values", grp=grp, tt=tt, n=i, t=t))
        t += 2 + tt
    assert t == 4 + 2 + 8 + 12 + 8 and s == S_LAYER
    return steps, t


PLAN1, T_AFTER_MIX1 = plan_mixer1()


def plan_mixer2():
    t, s, steps = 4 + 2 + 1 + 4, 0, []
    gates = iter(range(6))

    def gate(taps=(0, 0)):
        steps.append(dict(kind="gate", n=next(gates), taps=taps))

    def other(kind, n_t, **more):
        nonlocal t
        steps.append(dict(kind=kind, t=t, **more))
        t += n_t

    after = {(0, 0): (20, 24), (0, 1): (24, 28), (1, 0): (28, 31), (1, 1): (0, 0)}
    for i, (grp, tt) in enumerate([(0, 0), (0, 1), (1, 0), (1, 1)]):
        steps.append(dict(kind="scores", grp=grp, tt=tt, n=i, s=s))
        s += 1
        gate(after[grp, tt])
        other("values", 2 + tt, grp=grp, tt=tt, n=i)
        if i == 2:
            other("conv_back", 2)
    other("alpha", 2)
    other("gla_q", 1)
    gate()
    other("decay", 2)
    gate()
    other("states", 4)
    other("gla_out", 2)
    assert t == 34 and s == S_MIX2
    return steps, t


PLAN2, T_AFTER_MIX2 = plan_mixer2()


def shape_constants():
    import numpy as np

    i = np.arange(P)
    q, k = i[:, None], i[None, :]
    causal = np.where(k <= q, 0.0, NEG)
    band = np.where(k > q, 0.0, NEG)
    earlier = np.where(k < q, 0.0, NEG)
    zero = np.zeros((P, P))
    inv = (np.float32(1.0) / (np.float32(10000.0) ** (np.arange(0, DH, 2, dtype=np.float32) / np.float32(DH)))).astype(np.float32)
    ang = np.arange(TT * P, dtype=np.float32)[:, None] * inv[None, :]
    cos, sin = np.cos(ang).astype(np.float32), np.sin(ang).astype(np.float32)
    rope = np.concatenate([cos, cos, -sin, sin], axis=1).reshape(TT, P, 4 * DH // 2)
    parts = {
        "ident": np.eye(P),
        "mask_causal": np.concatenate([zero, causal], axis=1),
        "mask_window": np.concatenate([band, causal], axis=1),
        "mask_earlier": np.concatenate([zero, earlier], axis=1),
        "rope": np.concatenate([rope[0], rope[1]], axis=1),
        "before": (q < k) * 1.0,
        "ones": np.ones((P, P)),
        "iota": np.broadcast_to(k, (P, P)),
        "first_of16": np.broadcast_to(16 - np.arange(16), (P, 16)),
        "first_of4": np.broadcast_to(4 - np.arange(4), (P, 4)),
        "later_in_chunk": ((q > k) & (q // 64 == k // 64)) * 1.0,
        "chunk_of": (q // 64 == np.arange(2)[None, :]) * 1.0,
    }
    at, n = {}, 0
    for name, a in parts.items():
        at[name] = (n, n + a.shape[1])
        n += a.shape[1]
    return np.concatenate([np.asarray(a, np.float32) for a in parts.values()], axis=1), at


def build(nc, d, const_at, stacks=2):
    d_const, out = d["shape_constants"], d["out_0_dram"]
    n_const = d_const.shape[1]
    with ExitStack() as ctx:
        def sb(name, shape, dt=F32, scope=ctx):
            return scope.enter_context(nc.sbuf_tensor(name, shape, dt))

        def sem(name):
            return ctx.enter_context(nc.semaphore(name))

        g_bank = [ctx.enter_context(nc.psum_tensor(f"g_bank{i}", [P, 512], F32)) for i in range(4)]
        t_bank = [ctx.enter_context(nc.psum_tensor(f"t_bank{i}", [P, 512], F32)) for i in range(2)]
        s_bank = ctx.enter_context(nc.psum_tensor("s_bank", [P, 1024], F32))

        const = sb("const", [P, n_const])
        w_raw = sb("w_raw", [P, RING, UNIT])
        w_hi = sb("w_hi", [P, RING, UNIT], F32R)
        w_lo = sb("w_lo", [P, RING, UNIT], F32R)
        x = sb("x_res", [P, TT, DM])
        xt_hi = sb("xt_hi", [P, 12, TT * P], F32R)
        xt_lo = sb("xt_lo", [P, 12, TT * P], F32R)
        gains = sb("gains", [P, 2, DM])
        stats = sb("stats", [P, TT, 12])
        mean_var = sb("mean_var", [P, TT, 2])
        rstd = sb("rstd", [P, TT])
        rstd_in = sb("rstd_in", [P, TT])
        mean_sq = sb("mean_sq", [P, TT, 2])
        w_ukv = sb("w_ukv", [P, 2 * DH])
        sinks = sb("sinks", [P, 8])
        w_router = sb("w_router", [P, 8, NE])
        wr_hi = sb("wr_hi", [P, 8, NE], F32R)
        wr_lo = sb("wr_lo", [P, 8, NE], F32R)
        b_router = sb("b_router", [P, NE])

        def c(name, a=0, b=None):
            lo, hi = const_at[name]
            return const[:, lo + a:(hi if b is None else lo + b)]

        ident = c("ident")

        mix1 = ctx.enter_context(ExitStack())
        qkv = sb("qkv", [P, TT, N_QKV], scope=mix1)
        gate = sb("gate", [P, TT, N_GATE], scope=mix1)
        rot = sb("rot", [P, TT, 2048], scope=mix1)
        rot_t = sb("rot_t", [P, N_RB, TT * P], scope=mix1)
        kv_lat = sb("kv_lat", [P, TT, 2 * DH], scope=mix1)
        top8 = sb("top8", [P, 8], scope=mix1)
        chosen = sb("chosen", [P, TT, 256], scope=mix1)
        masked = sb("masked", [P, 2, 1024], scope=mix1)
        probs = masked
        relu_dots = masked[:, 0, :].rearrange("p (h k) -> p h k", h=4)
        rope_tmp = masked[:, :, 0:10 * DH].rearrange("p t (h d) -> p t h d", d=DH)
        gated = masked[:, :, 0:512]
        idx_work = masked[:, 1, 0:256]
        probs_t = rot[:, :, DM:DM + 512].rearrange("p k (h q) -> p k h q", h=4)
        lat_t = chosen[:, :, 0:P]
        row_max = sb("row_max", [P, 2, 4], scope=mix1)
        neg_max = sb("neg_max", [P, 2, 4], scope=mix1)
        row_sum = sb("row_sum", [P, 2, 4], scope=mix1)
        sink_exp = sb("sink_exp", [P, 2, 4], scope=mix1)
        inv_sum = sb("inv_sum", [P, 2, 4], scope=mix1)
        attn = rot[:, :, 0:DM]
        merged = rot[:, :, DM:2 * DM]
        mix1.close()

        moe = ctx.enter_context(ExitStack())
        aff = sb("aff", [P, TT, NE], scope=moe)
        sel = sb("sel", [P, TT, NE], scope=moe)
        pair = sb("pair", [P, TT * NG, 6], scope=moe)
        grp_score = sb("grp_score", [P, TT, NG], scope=moe)
        in_grp = sb("in_grp", [P, TT, NG], scope=moe)
        key = sb("key", [P, TT, NE], scope=moe)
        best = sb("best", [P, TT], scope=moe)
        hot1 = sb("hot1", [P, TT, NE], scope=moe)
        hot2 = sb("hot2", [P, TT, NE], scope=moe)
        comb = sb("comb", [P, TT, NE], scope=moe)
        place = sb("place", [P, TT, NG], scope=moe)
        n_grp = sb("n_grp", [P, NG], scope=moe)
        rounds_f = sb("rounds_f", [P, 1], scope=moe)
        rounds_i = sb("rounds_i", [P, 1], I32, scope=moe)
        onehot = sb("onehot", [P, TT, NG, P], scope=moe)
        onehot_t = sb("onehot_t", [P, TT, NG, P], F32R, scope=moe)
        comb_slot = sb("comb_slot", [P, NE], scope=moe)
        xg_hi = sb("xg_hi", [P, 8, P], F32R, scope=moe)
        xg_lo = sb("xg_lo", [P, 8, P], F32R, scope=moe)
        silu_g = sb("silu_g", [P, 2, DE], scope=moe)
        hid = sb("hid", [P, 2, DE], scope=moe)
        hid_t_hi = sb("hid_t_hi", [P, 2, 4, P], F32R, scope=moe)
        hid_t_lo = sb("hid_t_lo", [P, 2, 4, P], F32R, scope=moe)
        y_hi = sb("y_hi", [P, NG, DM], F32R, scope=moe)
        y_lo = sb("y_lo", [P, NG, DM], F32R, scope=moe)
        acc = sb("acc", [P, TT, DM], scope=moe)
        moe.close()

        ffn = ctx.enter_context(ExitStack())
        ffn_y = sb("ffn_y", [P, TT, DM], scope=ffn)
        ffn_junk = sb("ffn_junk", [P, DM], scope=ffn)
        ffn_silu = sb("ffn_silu", [P, TT, 256], scope=ffn)
        ffn_hid = sb("ffn_hid", [P, TT, 256], scope=ffn)
        ffn_t_hi = sb("ffn_t_hi", [P, 2, TT * P], F32R, scope=ffn)
        ffn_t_lo = sb("ffn_t_lo", [P, 2, TT * P], F32R, scope=ffn)
        ffn.close()

        mix2 = ctx.enter_context(ExitStack())
        proj = sb("proj", [P, TT, N_PROJ2], scope=mix2)
        gate2 = sb("gate2", [P, TT, N_GATE], scope=mix2)
        qk_t = sb("qk_t", [P, 8, TT * P], scope=mix2)
        logit = sb("logit", [P, 4, 256], scope=mix2)
        soft = sb("soft", [P, 4, 256], scope=mix2)
        probs_t2 = sb("probs_t2", [P, 2, 4, P], scope=mix2)
        conv_in = sb("conv_in", [P, 4, TAPS - 1 + TT * P], scope=mix2)
        conv_y = sb("conv_y", [P, 4, TT * P], scope=mix2)
        taps = sb("taps", [P, 4, 32], scope=mix2)
        lam = sb("lam", [P, 8], scope=mix2)
        mean_sq8 = sb("mean_sq8", [P, TT, 4], scope=mix2)
        mix_y = gate2[:, :, 0:DM]
        mix_junk = proj[:, 0, 0:DM]
        gla_gain = proj[:, 0, CONV + 512:CONV + 1024]
        b_alpha = proj[:, 1, CONV + 512:CONV + 768]
        w_alpha = proj[0:16, 1, CONV + 768:CONV + 1024]
        conv_row = gains[:, 1, :]
        flat = "p a b -> p (a b)"
        taps_raw = probs_t2[0:32, 0, :, :].rearrange(flat)
        state = qk_t[:, :, :].rearrange("p (c h) n -> p c h n", c=4)
        k_dec = logit[:, :, :].rearrange("p (t c) n -> p t c n", t=TT)
        log_alpha = soft[:, 0:2, :]
        decay = soft[:, 2:4, :]
        log_tmp = probs_t2[:, 0, :, :].rearrange(flat)
        kv_new = probs_t2[:, 1, :, :].rearrange(flat)
        lin_qt = conv_in[:, :, :].rearrange(flat)[:, 0:512].rearrange("p (h n) -> p h n", h=2)
        lr_t = conv_in[:, :, :].rearrange(flat)[0:16, 512:768].rearrange("p (t n) -> p t n", t=TT)
        gla_o = conv_y[:, :, :].rearrange("p (t a) n -> p t (a n)", t=TT)
        merged2 = proj[:, :, 512:512 + DM]
        ATTN2 = (0, 1536, 2048)
        mix2.close()

        const_in, x_in, small_in, gains_in, router_in, x_out = (
            sem(n) for n in ("const_in", "x_in", "small_in", "gains_in", "router_in", "x_out"))
        landed = [sem(f"landed{i}") for i in range(2 * RING)]
        fences = {e: sem(f"fence_{i}") for i, e in enumerate(
            (nc.sync.engine, nc.scalar.engine, nc.vector.engine, nc.tensor.engine, nc.gpsimd.engine))}
        credits = sem("credits")
        hi_ready, lo_ready, w_used = sem("hi_ready"), sem("lo_ready"), sem("w_used")
        g_free = [sem(f"g_free{i}") for i in range(4)]
        t_ready, s_ready, s_free = sem("t_ready"), sem("s_ready"), sem("s_free")
        t_free = [sem(f"t_free{i}") for i in range(2)]
        xt_hi_ready, xt_ready, x_ready = sem("xt_hi_ready"), sem("xt_ready"), sem("x_ready")
        qkv_ready, lat_t_ready, kv_lat_ready, rot_ready, rot_t_ready = (
            sem(n) for n in ("qkv_ready", "lat_t_ready", "kv_lat_ready", "rot_ready", "rot_t_ready"))
        kv_lat_done, returned = sem("kv_lat_done"), sem("returned")
        relu_ready, chosen_ready, max_ready, probs_ready, probs_t_ready, attn_ready = (
            sem(n) for n in ("relu_ready", "chosen_ready", "max_ready", "probs_ready", "probs_t_ready", "attn_ready"))
        gate_ready, merged_ready, var_ready, rstd_ready = (
            sem(n) for n in ("gate_ready", "merged_ready", "var_ready", "rstd_ready"))
        router_split, aff_ready, in_grp_ready, rounds_ready, onehot_ready, onehot_t_ready, comb_slot_ready = (
            sem(n) for n in ("router_split", "aff_ready", "in_grp_ready", "rounds_ready", "onehot_ready",
                             "onehot_t_ready", "comb_slot_ready"))
        xg_hi_ready, xg_ready, silu_ready, hid_ready, hid_hi_ready, hid_t_ready, y_hi_ready, y_ready = (
            sem(n) for n in ("xg_hi_ready", "xg_ready", "silu_ready", "hid_ready", "hid_hi_ready", "hid_t_ready",
                             "y_hi_ready", "y_ready"))

        (square_ready, normed_ready, up_silu_ready, ffn_hid_ready, ffn_hi_ready, ffn_t_ready, proj_ready, conv_u_ready,
         conv_in_ready, taps_ready, qk_t_ready, logit_ready, soft_ready, log_w_ready, stick_ready, probs_t2_ready,
         branch_ready, conv_y_ready, conv_mid_ready, lr_t_ready, alpha_in_ready, alpha_soft_ready, log_alpha_ready,
         gla_q_ready, decay_ready, k_dec_ready, state_ready, merged2_ready, gate2_ready, pad_ready, mixer_in, alpha_in) = (
            sem(n) for n in (
                "square_ready", "normed_ready", "up_silu_ready", "ffn_hid_ready", "ffn_hi_ready", "ffn_t_ready",
                "proj_ready", "conv_u_ready", "conv_in_ready", "taps_ready", "qk_t_ready", "logit_ready", "soft_ready",
                "log_w_ready", "stick_ready", "probs_t2_ready", "branch_ready", "conv_y_ready", "conv_mid_ready",
                "lr_t_ready", "alpha_in_ready", "alpha_soft_ready", "log_alpha_ready", "gla_q_ready", "decay_ready",
                "k_dec_ready", "state_ready", "merged2_ready", "gate2_ready", "pad_ready", "mixer_in", "alpha_in"))
        pre_in, post_in = sem("pre_in"), sem("post_in")

        def half_slot(u, h):
            return (2 * u.const + h) % (2 * RING)

        def half_of(ring, u, h):
            hs = half_slot(u, h)
            return ring[:, hs // 2, (hs % 2) * HALF:(hs % 2 + 1) * HALF]

        def unit_is_used(eng, u):
            eng.wait_ge(w_used, u.value(2, 2 * RING + 2))

        def half_is_split(u, h):
            nc.tensor.wait_ge(lo_ready, u.value(2, 2 * RING + 1 + h))

        def split_hi(u, h):
            place = u + h // 2
            nc.scalar.wait_ge(w_used, u.value(2, 1 + h))
            nc.scalar.wait_ge(landed[half_slot(u, h)], place.turn(RING).value(32, 32))
            nc.scalar.activation(half_of(w_hi, u, h), half_of(w_raw, u, h), ACT.Copy).then_inc(hi_ready, 1)

        def split_lo(u, h):
            nc.vector.wait_ge(hi_ready, u.value(2, 1 + h))
            nc.vector.tensor_tensor(half_of(w_lo, u, h), half_of(w_raw, u, h), half_of(w_hi, u, h).bitcast(F32),
                                    ALU.subtract).then_inc(lo_ready, 1)

        def ahead_of(split):
            def ahead(u, k=0):
                split(u, 2 * k + AHEAD)
                split(u, 2 * k + AHEAD + 1)
            return ahead

        def mm3(dst, a_hi, a_lo, b_hi, b_lo, first, last):
            nc.tensor.matmul(dst, a_hi, b_hi, start=first, stop=False)
            nc.tensor.matmul(dst, a_hi, b_lo, start=False, stop=False)
            return nc.tensor.matmul(dst, a_lo, b_hi, start=False, stop=last)

        def g_wait(f):
            nc.tensor.wait_ge(g_free[f.slot(4)], f.turn(4).value(1, 1))
            return g_bank[f.slot(4)]

        def t_wait(t):
            nc.tensor.wait_ge(t_free[t.slot(2)], t.turn(2).value(1, 1))
            return t_bank[t.slot(2)]

        def pe_block(u, f, n=512):
            for half in range(2):
                uu = u + half
                s = uu.slot(RING)
                for h in range(2):
                    half_is_split(uu, h)
                    for tt in range(TT):
                        bank = g_bank[(f + tt).slot(4)] if half or h else g_wait(f + tt)
                        for k in (2 * h, 2 * h + 1):
                            kk = half * 4 + k
                            last = mm3(bank[:, 0:n], xt_hi[:, kk, tt * P:(tt + 1) * P], xt_lo[:, kk, tt * P:(tt + 1) * P],
                                       w_hi[:, s, k * 512:k * 512 + n], w_lo[:, s, k * 512:k * 512 + n],
                                       kk == 0, kk == 7)
                    last.then_inc(w_used, 1)

        def pe_xt(src, t, quads, ready):
            for i in range(TT * quads):
                tt, kq = divmod(i, quads)
                if kq == 0:
                    ready(nc.tensor, tt)
                bank = t_wait(t + i)
                for j in range(4):
                    last = nc.tensor.transpose(bank[:, j * P:(j + 1) * P], src[:, tt, (4 * kq + j) * P:(4 * kq + j + 1) * P], ident)
                last.then_inc(t_ready, 1)

        def act_xt(t, quads):
            for i in range(TT * quads):
                tt, kq = divmod(i, quads)
                nc.scalar.wait_ge(t_ready, (t + i).value(1, 1))
                nc.scalar.activation(xt_hi[:, 4 * kq:4 * kq + 4, tt * P:(tt + 1) * P],
                                     t_bank[(t + i).slot(2)][:, :].rearrange("p (a b) -> p a b", a=4),
                                     ACT.Copy).then_inc(xt_hi_ready, 1)

        def dve_xt(t, n, quads):
            for i in range(TT * quads):
                tt, kq = divmod(i, quads)
                nc.vector.wait_ge(xt_hi_ready, (n + i).value(1, 1))
                nc.vector.tensor_tensor(xt_lo[:, 4 * kq:4 * kq + 4, tt * P:(tt + 1) * P],
                                        t_bank[(t + i).slot(2)][:, :].rearrange("p (a b) -> p a b", a=4),
                                        xt_hi[:, 4 * kq:4 * kq + 4, tt * P:(tt + 1) * P].bitcast(F32),
                                        ALU.subtract).then_inc(t_free[(t + i).slot(2)], 1)
            nc.vector.drain().then_inc(xt_ready, 1)

        def layer_norm(src, dst, norm, gain, bias, gains_at):
            dve = nc.vector
            dve.drain()
            for tt in range(TT):
                for hf in range(2):
                    dve.bn_stats(stats[:, tt, hf * 6:hf * 6 + 6], src[:, tt, hf * 512:hf * 512 + 512])
            dve.drain()
            for tt in range(TT):
                dve.bn_aggr(mean_var[:, tt, :], stats[:, tt, :])
            dve.drain()
            dve.tensor_scalar(mean_var[:, :, 1:2], mean_var[:, :, 1:2], LN_EPS, None, ALU.add)
            dve.drain()
            dve.reciprocal(rstd[:, :], mean_var[:, :, 1:2].rearrange("p a b -> p (a b)")).then_inc(var_ready, 1)
            dve.wait_ge(rstd_ready, norm.value(1, 1))
            dve.wait_ge(gains_in, gains_at)
            for tt in range(TT):
                dve.tensor_scalar(dst[:, tt, :], src[:, tt, :], mean_var[:, tt, 0:1], rstd[:, tt:tt + 1],
                                  ALU.subtract, ALU.mult)
            dve.drain()
            for tt in range(TT):
                dve.tensor_tensor(dst[:, tt, :], dst[:, tt, :], gain, ALU.mult)
            dve.drain()
            for tt in range(TT):
                last = dve.tensor_tensor(dst[:, tt, :], dst[:, tt, :], bias, ALU.add)
            last.then_inc(x_ready, 1)

        def act_root(norm):
            nc.scalar.wait_ge(var_ready, norm.value(1, 1))
            nc.scalar.activation(rstd[:, :], rstd[:, :], ACT.Sqrt).then_inc(rstd_ready, 1)

        def layer1(l, rho):
            return dict(u=At(0, (l, U_LAYER), (rho, U_ROUND)), g=At(0, (l, G_LAYER), (rho, G_ROUND)),
                        t=At(0, (l, T_LAYER), (rho, T_ROUND)), s=At(0, (l, S_LAYER), (rho, S_ROUND)))

        def s_half(half, kn):
            return s_bank[:, 512 * half:512 * half + 2 * kn].rearrange("p (i k) -> p i k", i=2)

        def layer2(l, rho):
            def at(consts, per):
                return At(DEPTH * consts[0], (rho, consts[1]), (l, per))

            first = dict(u=at((U_LAYER, U_ROUND), U_LAYER2), g=at((G_LAYER, G_ROUND), G_LAYER2),
                         t=at((T_LAYER, T_ROUND), T_LAYER2), s=at((S_LAYER, S_ROUND), S_LAYER2))
            mixer = dict(u=first["u"] + U_FFN, g=first["g"] + 4, t=first["t"] + T_FFN, s=first["s"] + S_FFN)
            second = dict(u=mixer["u"] + U_MIX2, g=mixer["g"] + G_MIX2, t=mixer["t"] + T_MIX2, s=mixer["s"] + S_MIX2)
            return first, mixer, second

        def ffn_fills(f):
            return [[f + (2 * tt + nb) for nb in range(2)] for tt in range(TT)]

        def mix_fills(f):
            return [[f + (44 + 2 * nb + tt) for nb in range(2)] for tt in range(TT)]

        def fence(eng):
            eng.sem_inc(fences[eng.engine], 1)

        def in_round(l, rho):
            at = layer1(l, rho)
            return dict(u=at["u"] + U_LAYER, g=at["g"] + G_LAYER, t=at["t"] + T_LAYER, s=at["s"] + S_LAYER)

        def group_steps(part):
            if part == "start":
                return [("gather", 0), ("gate", 0), ("up", 0)]
            steps = []
            for e in range(1, EPG + 1 if part == "group" else EPG):
                steps += [("gate", e), ("hid_t", e - 1), ("up", e)]
                if e == EPG - 1 and part == "group":
                    steps.append(("gather", 0))
                steps.append(("down", e - 1))
            if part == "last":
                steps += [("hid_t", EPG - 1), ("down", EPG - 1)]
            return steps + [("back", 0)]

        def plus(a, c, g, step):
            return a + (c + g * step) if isinstance(g, int) else At(a.const + c, *a.terms, (g, step))

        def walk(part, at_r, g):
            later = part != "start"
            u, t = plus(at_r["u"], 4 * later, g, 24), plus(at_r["t"], 4 + 2 * later, g, 6)
            for kind, e in group_steps(part):
                if kind in ("gate", "up", "down"):
                    for half in range(2):
                        yield kind, e, half, u
                        u = u + 1
                else:
                    yield kind, e, None, t
                    t = t + {"gather": 2, "hid_t": 1, "back": 0}[kind]

        def all_parts(eng, run):
            run("start", 0)
            with eng.Fori(0, NG - 1) as g:
                run("group", g)
            run("last", NG - 1)

        def expert_fill(at_r, kind, g, e):
            return plus(at_r["g"], 2 * e + (kind == "up"), g, 8)

        def rounds_loop(eng, at_least, value):
            eng.wait_ge(rounds_ready, value)
            fence(eng)
            return eng.value_load(rounds_i[0:1, 0:1], min_val=1, max_val=2)

        block = ctx.enter_context(nc.Block())

        @block.sync
        def _(sp):
            sp.dma_start(const[:, :], d_const).then_inc(const_in, 16)
            sp.dma_start(x[:, :, :], d["x"].rearrange("a (t p) n -> p (a t) n", p=P)).then_inc(x_in, 16)

            def load(u, src, n=512, k=4):
                s = u.slot(RING)
                dst = w_raw[:, s, :].rearrange("p (k n) -> p k n", k=k)[:, :, 0:n]
                for h in range(2):
                    sp.wait_ge(lo_ready, u.value(2, 1 + h))
                    fence(sp)
                    a = h * (k // 2)
                    hs = half_slot(u, h)
                    sp.dma_start(dst[:, a:a + k // 2, :], src[:, a:a + k // 2, :]).then_inc(landed[hs], 16)
                    sp.sem_inc(landed[hs], 16)

            def rows(w, l, k0, n0, n=512, k=4):
                return w[bass.ds(l, 1), k0 * P:(k0 + k) * P, n0:n0 + n].rearrange("a (k p) n -> p (a k) n", p=P)

            rho = sp.alloc_register("rounds_done_sp")
            sp.reg_mov(rho, 0)
            with sp.Fori(0, DEPTH) as l:
                done = sp.snap(rho, min_val=0, max_val=4)
                at = layer1(l, done)
                u = at["u"]
                for blk in range(5):
                    n = min(512, N_QKV - blk * 512)
                    for half in range(2):
                        load(u + (2 * blk + half), rows(d["w_in"], l, 4 * half, blk * 512, n), n)
                for blk in range(6):
                    for half in range(2):
                        load(u + (10 + 2 * blk + half), rows(d["w_in"], l, 4 * half, N_QKV + blk * 512))
                for i, w in ((22, "w_branch"), (26, "w_o")):
                    for blk in range(2):
                        for half in range(2):
                            load(u + (i + 2 * blk + half), rows(d[w], l, 4 * half, blk * 512))
                def round_of_experts(rnd):
                    at_r = in_round(l, rnd)

                    def expert(u, what, ex):
                        src = d[f"moe_w_{what}"].rearrange("l e k n -> (l e) k n")
                        rows_, n, k = (256, DM, 2) if what == "down" else (512, DE, 4)
                        for half in range(2):
                            load(u + half, src[bass.ds(ex, 1), half * rows_:(half + 1) * rows_, :]
                                 .rearrange("a (k p) n -> p (a k) n", p=P), n, k)

                    u = at_r["u"]
                    expert(u, "gate", l * NE)
                    expert(u + 2, "up", l * NE)
                    with sp.Fori(1, NE) as e:
                        ue = At(u.const - 2, *u.terms, (e, 6))
                        expert(ue, "gate", l * NE + e)
                        expert(ue + 2, "up", l * NE + e)
                        expert(ue + 4, "down", l * NE + e - 1)
                    expert(u + (U_ROUND - 2), "down", l * NE + (NE - 1))

                round_of_experts(done)
                R = rounds_loop(sp, 1, l + 1)
                with sp.If(R > 1):
                    round_of_experts(done + 1)
                sp.reg_add(rho, rho, R)
            if stacks == 2:
                done = sp.snap(rho, min_val=0, max_val=4)
                with sp.Fori(0, DEPTH) as l:
                    first, mixer, second = layer2(l, done)

                    def gate_up(u, w, j):
                        for h in range(4):
                            sp.wait_ge(lo_ready, u.value(2, 1 + h))
                            fence(sp)
                            for i, name in enumerate(("gate", "up")):
                                src = d[f"{w}_w_{name}_2"][bass.ds(l, 1), h * 256:(h + 1) * 256, bass.ds(j * 256, 256)]
                                sp.dma_start(half_of(w_raw, u, h).rearrange("p (k n) -> p k n", k=2)[:, :, i * 256:(i + 1) * 256],
                                             src.rearrange("a (k p) n -> p (a k) n", p=P)).then_inc(landed[half_slot(u, h)], 16)

                    def down(u, w, j):
                        src = d[f"{w}_w_down_2"][bass.ds(l, 1), bass.ds(j * 256, 256), :]
                        load(u, src.rearrange("a (k p) n -> p (a k) n", p=P), DM, 2)

                    def feed_forward(u, w):
                        gate_up(u, w, 0)
                        gate_up(u + 2, w, 1)
                        down(u + 4, w, 0)
                        with sp.Fori(2, FB) as j:
                            uj = At(u.const - 1, *u.terms, (j, 3))
                            gate_up(uj, w, j)
                            down(uj + 2, w, j - 1)
                        down(u + (U_FFN - 1), w, FB - 1)

                    feed_forward(first["u"], "ffn1")
                    u = mixer["u"]
                    for i, blk in enumerate(PROJ2_ORDER):
                        for half in range(2):
                            load(u + (2 * i + half), rows(d["w_in_2"], l, 4 * half, blk * 512))
                    load(u + 16, rows(d["w_in_2"], l, 0, L_LR, 16, 8), 16, 8)
                    for blk in range(6):
                        for half in range(2):
                            load(u + (17 + 2 * blk + half), rows(d["w_in_2"], l, 4 * half, GATE2 + blk * 512))
                    for blk in range(2):
                        for br in range(3):
                            src = d["w_branch_2"][bass.ds(l, 1), br, :, blk * 512:(blk + 1) * 512]
                            load(u + (29 + 3 * blk + br), src.rearrange("a (k p) n -> p (a k) n", p=P))
                    for blk in range(2):
                        for half in range(2):
                            load(u + (35 + 2 * blk + half), rows(d["w_out_2"], l, 4 * half, blk * 512))
                    feed_forward(second["u"], "ffn2")
                end = layer2(DEPTH, done)[0]["u"]
                for h in range(AHEAD):
                    sp.wait_ge(lo_ready, end.value(2, 1 + h))
                    sp.sem_inc(landed[half_slot(end, h)], 32)
            sp.wait_ge(x_ready, 2 * DEPTH + 1 + (3 * DEPTH if stacks == 2 else 0))
            sp.dma_start(out.rearrange("a (t p) n -> p (a t) n", p=P), x[:, :, :]).then_inc(x_out, 16)
            sp.wait_ge(x_out, 16)

        @block.gpsimd
        def _(pool):
            pool.dma_start(w_router[:, :, :], d["router_w"].rearrange("(k p) n -> p k n", p=P)).then_inc(router_in, 16)
            pool.dma_start(b_router[:, :], d["router_b"].rearrange("(a n) -> a n", a=1).to_broadcast([P, NE])).then_inc(router_in, 16)
            pool.wait_ge(credits, 3)
            with pool.Fori(0, DEPTH) as l:
                pool.wait_ge(x_ready, 2 * l + 1)
                fence(pool)
                for i, w in enumerate(("ln1_g", "ln1_b")):
                    pool.dma_start(gains[:, i, :], d[w][bass.ds(l, 1), :].to_broadcast([P, DM])).then_inc(gains_in, 16)
                pool.dma_start(sinks[:, :], d["c_sinks"][bass.ds(l, 1), :].to_broadcast([P, 8])).then_inc(small_in, 16)
                for i, w in enumerate(("a_w_uk", "a_w_uv")):
                    pool.dma_start(w_ukv[:, i * DH:(i + 1) * DH], d[w][bass.ds(l, 1), :, :].rearrange("a p n -> p (a n)")).then_inc(small_in, 16)
                pool.wait_ge(x_ready, 2 * l + 2)
                fence(pool)
                for i, w in enumerate(("ln2_g", "ln2_b")):
                    pool.dma_start(gains[:, i, :], d[w][bass.ds(l, 1), :].to_broadcast([P, DM])).then_inc(gains_in, 16)

            if stacks == 2:
                with pool.Fori(0, DEPTH) as l:
                    for i in range(3):
                        pool.wait_ge(normed_ready, 6 * l + (2 * i + 1))
                        if i == 0:
                            pool.wait_ge(x_ready, 2 * DEPTH + 1)
                        fence(pool)
                        pool.dma_start(gains[:, 0, :], d["norm_pre_2"][bass.ds(l, 1), i, :].to_broadcast([P, DM])).then_inc(pre_in, 16)
                        pool.wait_ge(x_ready, 3 * l + (2 * DEPTH + 1 + i))
                        fence(pool)
                        if i == 1:
                            pool.wait_ge(normed_ready, 6 * l + 5)
                            fence(pool)
                            pool.memset(conv_in[:, :, 0:TAPS - 1], 0.0).then_inc(pad_ready, 1)
                            for j, w in enumerate(("conv_ln_g_2", "conv_ln_b_2")):
                                pool.dma_start(conv_row[:, j * 512:(j + 1) * 512],
                                               d[w][bass.ds(l, 1), :].to_broadcast([P, 512])).then_inc(mixer_in, 16)
                            pool.dma_start(taps_raw[0:TAPS, :], d["conv_w_2"][bass.ds(l, 1), :, :].rearrange("a t n -> (a t) n")).then_inc(mixer_in, 16)
                            pool.dma_start(taps_raw[TAPS:TAPS + 1, :], d["conv_b_2"][bass.ds(l, 1), :]).then_inc(mixer_in, 16)
                            pool.wait_ge(conv_u_ready, l + 1)
                            fence(pool)
                            pool.dma_start(gla_gain, d["gla_norm_g_2"][bass.ds(l, 1), :].to_broadcast([P, 512])).then_inc(alpha_in, 16)
                            pool.dma_start(b_alpha, d["gla_b_alpha_2"][bass.ds(l, 1), :].to_broadcast([P, 256])).then_inc(alpha_in, 16)
                            pool.dma_start(w_alpha, d["gla_w_alpha_2"][bass.ds(l, 1), :, :].rearrange("a t n -> (a t) n")).then_inc(alpha_in, 16)
                            pool.wait_ge(conv_mid_ready, l + 1)
                            fence(pool)
                        pool.dma_start(gains[:, 1, :], d["norm_post_2"][bass.ds(l, 1), i, :].to_broadcast([P, DM])).then_inc(post_in, 16)

        @block.scalar
        def _(act):
            act.wait_ge(const_in, 16)
            act.wait_ge(router_in, 32)
            act.wait_ge(credits, 3)
            act.activation(wr_hi[:, :, :], w_router[:, :, :], ACT.Copy).then_inc(router_split, 1)

            ahead = ahead_of(split_hi)
            for h in range(AHEAD):
                split_hi(At(0), h)

            def experts(at_r, rnd):
                def run(part, g):
                    count = plus(At(0, (rnd, 16)), 0, g, 4)
                    for what, e, half, place in walk(part, at_r, g):
                        if half is not None:
                            ahead(place)
                            if what == "gate" and half == 1:
                                b = expert_fill(at_r, what, g, e).slot(4)
                                unit_is_used(act, place)
                                act.wait_ge(hid_ready, count.value(1, 1 + e))
                                act.activation(silu_g[:, e % 2, :], g_bank[b][:, :], ACT.Silu).then_inc(g_free[b], 1)
                                act.drain().then_inc(silu_ready, 1)
                        elif what == "gather":
                            for i in range(2):
                                act.wait_ge(t_ready, (place + i).value(1, 1))
                                act.activation(xg_hi[:, 4 * i:4 * i + 4, :], t_bank[(place + i).slot(2)][:, :].rearrange("p (a b) -> p a b", a=4),
                                               ACT.Copy).then_inc(xg_hi_ready, 1)
                        elif what == "hid_t":
                            act.wait_ge(t_ready, place.value(1, 1))
                            act.activation(hid_t_hi[:, e % 2, :, :], t_bank[place.slot(2)][:, :].rearrange("p (a b) -> p a b", a=4),
                                           ACT.Copy).then_inc(hid_hi_ready, 1)
                        else:
                            act.wait_ge(s_ready, plus(at_r["s"], 0, g, 1).value(1, 1))
                            act.activation(y_hi[:, bass.ds(g, 1), :], s_bank[:, :].unsqueeze(1), ACT.Copy).then_inc(y_hi_ready, 1)

                all_parts(act, run)

            rho = act.alloc_register("rounds_done_act")
            act.reg_mov(rho, 0)
            with act.Fori(0, DEPTH) as l:
                done = act.snap(rho, min_val=0, max_val=4)
                at = layer1(l, done)
                u, f, t = at["u"], at["g"], at["t"]
                act_xt(t, 2)
                for blk in range(5):
                    n = min(512, N_QKV - blk * 512)
                    ahead(u, 2 * blk)
                    ahead(u, 2 * blk + 1)
                    unit_is_used(act, u + (2 * blk + 1))
                    for tt in range(TT):
                        b = (f + (2 * blk + tt)).slot(4)
                        act.activation(qkv[:, tt, blk * 512:blk * 512 + n], g_bank[b][:, 0:n], ACT.Copy).then_inc(g_free[b], 1)
                    act.drain().then_inc(qkv_ready, 1)
                    if blk == 0:
                        for tt in range(TT):
                            act.wait_ge(t_ready, (t + (4 + tt)).value(1, 1))
                            act.activation(lat_t[:, tt, :], t_bank[tt][:, 0:P], ACT.Copy).then_inc(t_free[tt], 1)
                        act.drain().then_inc(lat_t_ready, 1)
                    if blk == 1:
                        for tt in range(TT):
                            b = (f + (10 + tt)).slot(4)
                    if blk == 4:
                        act.wait_ge(kv_lat_done, l + 1)
                        for tt in range(TT):
                            b = (f + (10 + tt)).slot(4)
                            act.activation(kv_lat[:, tt, :], g_bank[b][:, 0:P], ACT.Copy).then_inc(g_free[b], 1)
                        act.drain().then_inc(kv_lat_ready, 1)
                for st in PLAN1:
                    kind = st["kind"]
                    if kind == "rt":
                        tf = t + st["t"]
                        act.wait_ge(t_ready, tf.value(1, 1))
                        act.activation(rot_t[:, 2 * st["j"]:2 * st["j"] + 2, :],
                                       t_bank[tf.slot(2)][:, :].rearrange("p (a b) -> p a b", a=2), ACT.Copy).then_inc(t_free[tf.slot(2)], 1)
                        if st["j"] == 7:
                            act.drain().then_inc(rot_t_ready, 1)
                    elif kind == "gate":
                        n = st["n"]
                        k = 10 + 2 * n
                        ahead(u, k)
                        ahead(u, k + 1)
                        unit_is_used(act, u + (k + 1))
                        for tt in range(TT):
                            b = (f + (12 + 2 * n + tt)).slot(4)
                            act.activation(gate[:, tt, n * 512:(n + 1) * 512], g_bank[b][:, :], ACT.Sigmoid).then_inc(g_free[b], 1)
                        act.drain().then_inc(gate_ready, 1)
                    elif kind == "index":
                        kn = P * (1 + st["tt"])
                        act.wait_ge(s_ready, (at["s"] + st["s"]).value(1, 1))
                        if st["tt"]:
                            act.wait_ge(chosen_ready, 2 * l + 1)
                        for half in range(2):
                            last = act.activation(relu_dots[:, 2 * half:2 * half + 2, 0:kn], s_half(half, kn), ACT.Relu)
                        act.drain().then_inc(relu_ready, 1)
                    elif kind == "scores":
                        kn, i = P * (1 + st["tt"]), st["n"]
                        act.wait_ge(max_ready, 8 * l + (i + 1))
                        pr = probs[:, i % 2, 0:4 * kn].rearrange("p (h k) -> p h k", h=4)
                        sc = masked[:, i % 2, 0:4 * kn].rearrange("p (h k) -> p h k", h=4)
                        for h in range(4):
                            act.activation(pr[:, h, :], sc[:, h, :], ACT.Exp, bias=neg_max[:, i % 2, h:h + 1],
                                           accum_out=row_sum[:, i % 2, h:h + 1])
                        if st["grp"] >= 2:
                            act.activation(sink_exp[:, i % 2, :], sink_exp[:, i % 2, :], ACT.Exp)
                        act.drain().then_inc(probs_ready, 1)
                    elif kind == "values":
                        for kt in range(1 + st["tt"]):
                            tf = t + (st["t"] + kt)
                            act.wait_ge(t_ready, tf.value(1, 1))
                            act.activation(probs_t[:, kt, :, :], t_bank[tf.slot(2)][:, :].rearrange("p (h q) -> p h q", h=4),
                                           ACT.Copy).then_inc(t_free[tf.slot(2)], 1)
                        act.drain().then_inc(probs_t_ready, 1)
                act_xt(t + T_AFTER_MIX1, 2)
                for k in range(4):
                    ahead(u + 22, k)
                act_xt(t + (T_AFTER_MIX1 + 4), 2)
                for k in range(4):
                    ahead(u + 26, k)
                act_root(At(0, (l, 2)))
                act_xt(t + (T_AFTER_MIX1 + 8), 2)
                tf = t + (T_AFTER_MIX1 + 12)
                act.wait_ge(t_ready, tf.value(1, 1))
                act.activation(aff[:, :, :], t_bank[tf.slot(2)][:, 0:TT * NE].rearrange("p (a b) -> p a b", a=TT),
                               ACT.Sigmoid).then_inc(t_free[tf.slot(2)], 1)
                act.drain().then_inc(aff_ready, 1)
                R = rounds_loop(act, 1, l + 1)
                with act.Fori(0, R) as r:
                    at_r = in_round(l, done + r)
                    rnd = done + r
                    for tt in range(TT):
                        tf = at_r["t"] + tt
                        act.wait_ge(t_ready, tf.value(1, 1))
                        act.activation(onehot_t[:, tt, :, :], t_bank[tf.slot(2)][:, :].rearrange("p (a b) -> p a b", a=NG),
                                       ACT.Copy).then_inc(t_free[tf.slot(2)], 1)
                    for i in range(2):
                        tf = at_r["t"] + (2 + i)
                        act.wait_ge(t_ready, tf.value(1, 1))
                        act.activation(comb_slot[:, 8 * i:8 * i + 8], t_bank[tf.slot(2)][:, 0:8], ACT.Copy).then_inc(t_free[tf.slot(2)], 1)
                    act.drain().then_inc(comb_slot_ready, 1)
                    experts(at_r, rnd)
                act.reg_add(rho, rho, R)
                act_root(At(1, (l, 2)))

            if stacks < 2:
                return
            done = act.snap(rho, min_val=0, max_val=4)
            with act.Fori(0, DEPTH) as l:
                first, mixer, second = layer2(l, done)

                def in_root(i, n, junk):
                    act.wait_ge(x_ready, 3 * l + (2 * DEPTH + 1 + i))
                    fence(act)
                    for tt in range(TT):
                        act.activation(junk, x[:, tt, :], ACT.Square, scale=DM ** -0.5, accum_out=mean_sq[:, tt, 0:1])
                        act.drain()
                    act.sem_inc(square_ready, 1)
                    act.wait_ge(var_ready, At(4 + n, (l, 11)).value(1, 1))
                    act.activation(rstd_in[:, :], rstd_in[:, :], ACT.Sqrt)
                    act.drain().then_inc(rstd_ready, 1)

                def out_roots(n, fills, junk, factor):
                    for tt in range(TT):
                        for nb in range(2):
                            act.activation(junk[:, nb * 512:(nb + 1) * 512], g_bank[fills[tt][nb].slot(4)][:, :], ACT.Square,
                                           scale=DM ** -0.5 / factor, accum_out=mean_sq[:, tt, nb:nb + 1])
                            act.drain().then_inc(square_ready, 1)
                    for tt in range(TT):
                        act.wait_ge(var_ready, At(4 + n + tt, (l, 11)).value(1, 1))
                        act.activation(rstd[:, tt:tt + 1], rstd[:, tt:tt + 1], ACT.Sqrt).then_inc(rstd_ready, 1)

                def feed_forward(at, i, n, w):
                    u, f, t = at["u"], at["g"], at["t"]
                    act_xt(t, 2)
                    in_root(i, n, ffn_junk[:, :])

                    def silu(u_up, q):
                        unit_is_used(act, u_up)
                        act.wait_ge(ffn_hid_ready, q.value(1, 1))
                        for tt in range(TT):
                            act.activation(ffn_silu[:, tt, :], s_bank[:, tt * 512:tt * 512 + 256], ACT.Silu, scale=rstd_in[:, tt:tt + 1])
                        act.drain().then_inc(up_silu_ready, 1)

                    def hid_t(tj):
                        for tt in range(TT):
                            tf = tj + tt
                            act.wait_ge(t_ready, tf.value(1, 1))
                            act.activation(ffn_t_hi[:, :, tt * P:(tt + 1) * P], t_bank[tf.slot(2)][:, 0:256].rearrange("p (a b) -> p a b", a=2),
                                           ACT.Copy).then_inc(ffn_hi_ready, 1)

                    q0 = At(w * FB, (l, 2 * FB))
                    ahead(u)
                    ahead(u, 1)
                    silu(u + 1, q0)
                    hid_t(t + 4)
                    ahead(u, 2)
                    ahead(u, 3)
                    silu(u + 3, q0 + 1)
                    ahead(u, 4)
                    hid_t(t + 6)

                    with act.Fori(2, FB) as j:
                        uj, tj, qj = (At(a.const + b, *a.terms, (j, k)) for a, b, k in ((u, -1, 3), (t, 4, 2), (q0, 0, 1)))
                        ahead(uj)
                        ahead(uj, 1)
                        silu(uj + 1, qj)
                        ahead(uj, 2)
                        hid_t(tj)
                    ahead(u, U_FFN - 1)
                    unit_is_used(act, u + (U_FFN - 1))
                    out_roots(n + 1, ffn_fills(f), ffn_junk[:, :], 0.5)

                feed_forward(first, 0, 0, 0)

                u, f, t = mixer["u"], mixer["g"], mixer["t"]
                act_xt(t, 2)
                in_root(1, 3, mix_junk)
                for i, blk in enumerate(PROJ2_ORDER):
                    ahead(u, 2 * i)
                    ahead(u, 2 * i + 1)
                    unit_is_used(act, u + (2 * i + 1))
                    for tt in range(TT):
                        b = (f + (2 * i + tt)).slot(4)
                        act.activation(proj[:, tt, blk * 512:(blk + 1) * 512], g_bank[b][:, :],
                                       {4: ACT.Sigmoid, 7: ACT.Silu}.get(blk, ACT.Copy),
                                       scale=rstd_in[:, tt:tt + 1]).then_inc(g_free[b], 1)
                    act.drain().then_inc(proj_ready, 1)
                    if i == 2:
                        act.wait_ge(t_ready, (t + 4).value(1, 1))
                        act.activation(taps[:, :, :], t_bank[0][:, 0:P].rearrange("p (c t) -> p c t", c=4), ACT.Copy).then_inc(t_free[0], 1)
                        act.drain().then_inc(taps_ready, 1)
                        act.wait_ge(pad_ready, l + 1)
                        for tt in range(TT):
                            tf = t + (5 + tt)
                            act.wait_ge(t_ready, tf.value(1, 1))
                            act.activation(conv_in[:, :, TAPS - 1 + tt * P:TAPS - 1 + (tt + 1) * P],
                                           t_bank[tf.slot(2)][:, :].rearrange("p (c n) -> p c n", c=4), ACT.Copy).then_inc(t_free[tf.slot(2)], 1)
                        act.drain().then_inc(conv_in_ready, 1)
                    if i == 5:
                        for j in range(4):
                            tf = t + (7 + j)
                            act.wait_ge(t_ready, tf.value(1, 1))
                            act.activation(qk_t[:, 2 * j:2 * j + 2, :], t_bank[tf.slot(2)][:, :].rearrange("p (a b) -> p a b", a=2),
                                           ACT.Copy).then_inc(t_free[tf.slot(2)], 1)
                        act.drain().then_inc(qk_t_ready, 1)
                ahead(u, 16)
                unit_is_used(act, u + 16)
                for tt in range(TT):
                    b = (f + (16 + tt)).slot(4)
                    act.activation(proj[:, tt, L_LR:L_LR + 16], g_bank[b][:, 0:16], ACT.Copy,
                                   scale=rstd_in[:, tt:tt + 1]).then_inc(g_free[b], 1)
                act.drain().then_inc(proj_ready, 1)

                def soft_tail(z, tmp):
                    act.activation(tmp, z, ACT.Abs)
                    act.drain()
                    act.activation(tmp, tmp, ACT.Exp, scale=-1.0)
                    act.drain()
                    act.activation(tmp, tmp, ACT.Ln, bias=1.0)

                for st in PLAN2:
                    kind = st["kind"]
                    if kind == "gate":
                        n = st["n"]
                        k = 17 + 2 * n
                        ahead(u, k)
                        ahead(u, k + 1)
                        unit_is_used(act, u + (k + 1))
                        for tt in range(TT):
                            b = (f + (GATE2_G[n] + tt)).slot(4)
                            act.activation(gate2[:, tt, n * 512:(n + 1) * 512], g_bank[b][:, :], ACT.Sigmoid,
                                           scale=rstd_in[:, tt:tt + 1]).then_inc(g_free[b], 1)
                        act.drain().then_inc(gate2_ready, 1)
                    elif kind == "scores":
                        kn = P * (1 + st["tt"])
                        act.wait_ge(logit_ready, 4 * l + (st["n"] + 1))
                        soft_tail(logit[:, :, 0:kn], soft[:, :, 0:kn])
                        act.drain().then_inc(soft_ready, 1)
                        act.wait_ge(log_w_ready, 4 * l + (st["n"] + 1))
                        act.activation(logit[:, :, 0:kn], logit[:, :, 0:kn], ACT.Exp)
                        act.drain().then_inc(stick_ready, 1)
                    elif kind == "values":
                        for kt in range(1 + st["tt"]):
                            tf = t + (st["t"] + kt)
                            act.wait_ge(t_ready, tf.value(1, 1))
                            act.activation(probs_t2[:, kt, :, :], t_bank[tf.slot(2)][:, :].rearrange("p (h q) -> p h q", h=4),
                                           ACT.Copy).then_inc(t_free[tf.slot(2)], 1)
                        act.drain().then_inc(probs_t2_ready, 1)
                    elif kind == "conv_back":
                        act_root(At(4 + 4, (l, 11)))
                        act.wait_ge(conv_mid_ready, l + 1)
                        act.activation(proj[:, :, ATTN2[1]:ATTN2[1] + 512], proj[:, :, ATTN2[1]:ATTN2[1] + 512], ACT.Silu)
                        act.drain().then_inc(branch_ready, 1)
                    elif kind == "alpha":
                        for tt in range(TT):
                            tf = t + (st["t"] + tt)
                            act.wait_ge(t_ready, tf.value(1, 1))
                            act.activation(lr_t[:, tt, :], t_bank[tf.slot(2)][0:16, 0:P], ACT.Copy).then_inc(t_free[tf.slot(2)], 1)
                        act.drain().then_inc(lr_t_ready, 1)
                        act.wait_ge(alpha_in_ready, l + 1)
                        soft_tail(log_alpha.rearrange(flat), log_tmp)
                        act.drain().then_inc(alpha_soft_ready, 1)
                    elif kind == "gla_q":
                        tf = t + st["t"]
                        act.wait_ge(t_ready, tf.value(1, 1))
                        act.activation(lin_qt[:, :, :], t_bank[tf.slot(2)][:, :].rearrange("p (h n) -> p h n", h=2), ACT.Copy,
                                       scale=DH ** -0.5).then_inc(t_free[tf.slot(2)], 1)
                        act.drain().then_inc(gla_q_ready, 1)
                    elif kind == "decay":
                        tf = t + st["t"]
                        act.wait_ge(t_ready, tf.value(1, 1))
                        act.activation(decay.rearrange(flat), t_bank[tf.slot(2)][:, :], ACT.Exp).then_inc(t_free[tf.slot(2)], 1)
                        tf = t + (st["t"] + 1)
                        act.wait_ge(t_ready, tf.value(1, 1))
                        act.activation(lam[:, :], t_bank[tf.slot(2)][:, 0:8], ACT.Exp).then_inc(t_free[tf.slot(2)], 1)
                        act.drain().then_inc(decay_ready, 1)
                    elif kind == "gla_out":
                        act.wait_ge(var_ready, At(4 + 5, (l, 11)).value(1, 1))
                        act.activation(mean_sq8[:, :, :], mean_sq8[:, :, :], ACT.Sqrt).then_inc(rstd_ready, 1)
                act_xt(t + T_AFTER_MIX2, 3)
                for k in range(6):
                    ahead(u + 29, k)
                act_xt(t + (T_AFTER_MIX2 + 6), 2)
                for k in range(4):
                    ahead(u + 35, k)
                unit_is_used(act, u + 38)
                out_roots(6, mix_fills(f), mix_junk, 1.0)

                feed_forward(second, 2, 8, 1)

        @block.tensor
        def _(pe):
            pe.sem_inc(w_used, 2 * RING)
            pe.sem_inc(credits, 1)
            pe.wait_ge(const_in, 16)
            pe.wait_ge(x_in, 16)
            pe.wait_ge(credits, 3)

            def s_at(h, kn):
                a = 512 * (h % 2) + (h // 2) * kn
                return s_bank[:, a:a + kn]

            def s_wait(s):
                pe.wait_ge(s_free, s.value(1, 1))

            def rot_head(blk, half, a, n):
                return rot_t[64 * half:64 * half + 64, blk, a:a + n]

            rho = pe.alloc_register("rounds_done_pe")
            pe.reg_mov(rho, 0)
            with pe.Fori(0, DEPTH) as l:
                done = pe.snap(rho, min_val=0, max_val=4)
                at = layer1(l, done)
                u, f, t = at["u"], at["g"], at["t"]
                pe_xt(x, t, 2, lambda e, tt: e.wait_ge(x_ready, 2 * l + 1))
                pe.wait_ge(xt_ready, 4 * l + 1)
                for blk in range(5):
                    pe_block(u + 2 * blk, f + 2 * blk, min(512, N_QKV - blk * 512))
                    if blk == 1:
                        pe.wait_ge(qkv_ready, 5 * l + 1)
                        for tt in range(TT):
                            bank = t_wait(t + (4 + tt))
                            pe.transpose(bank[:, 0:P], qkv[:, tt, A_C:A_C + P], ident).then_inc(t_ready, 1)
                pe.wait_ge(lat_t_ready, l + 1)
                pe.wait_ge(small_in, 48 * l + 48)
                for tt in range(TT):
                    bank = g_wait(f + (10 + tt))
                    last = pe.matmul(bank[:, 0:P], lat_t[:, tt, :], w_ukv[:, :], start=True, stop=True)
                last.then_inc(kv_lat_done, 1)

                for st in PLAN1:
                    kind = st["kind"]
                    if kind == "rt":
                        j = st["j"]
                        if j == 0:
                            pe.wait_ge(rot_ready, l + 1)
                        bank = t_wait(t + st["t"])
                        for i in range(4):
                            blk, tt = 2 * j + i // 2, i % 2
                            last = pe.transpose(bank[:, i * P:(i + 1) * P], rot[:, tt, blk * P:(blk + 1) * P], ident)
                        last.then_inc(t_ready, 1)
                    elif kind == "gate":
                        n = st["n"]
                        pe_block(u + (10 + 2 * n), f + (12 + 2 * n))
                    elif kind == "index":
                        tt, kn = st["tt"], P * (1 + st["tt"])
                        pe.wait_ge(rot_t_ready, l + 1)
                        s_wait(at["s"] + st["s"])
                        for h in range(4):
                            half = h % 2
                            last = pe.matmul(s_at(h, kn), rot_head(RB_IQ + h // 2, half, tt * P, P),
                                             rot_head(RB_KAIK if half else RB_IKKA, half, 0, kn), start=True, stop=True)
                        last.then_inc(s_ready, 1)
                    elif kind == "scores":
                        tt, kn, grp = st["tt"], P * (1 + st["tt"]), st["grp"]
                        s_wait(at["s"] + st["s"])
                        for h in range(4):
                            half = h % 2
                            if grp == 0:
                                q, kk = RB_AQ + h // 2, RB_IKKA if half else RB_KAIK
                            elif grp == 1:
                                q, kk = RB_BQ + h // 2, RB_BK + h // 2
                            else:
                                q, kk = RB_CQ + (4 * (grp - 2) + h) // 2, RB_CK if grp - 2 == half else RB_CK2
                            last = pe.matmul(s_at(h, kn), rot_head(q, half, tt * P, P),
                                             rot_head(kk, half, 0, kn), start=True, stop=True)
                        last.then_inc(s_ready, 1)
                    elif kind == "values":
                        tt, kn, grp, i = st["tt"], P * (1 + st["tt"]), st["grp"], st["n"]
                        pr = probs[:, i % 2, 0:4 * kn].rearrange("p (h k) -> p h k", h=4)
                        pe.wait_ge(probs_ready, 8 * l + (i + 1))
                        for kt in range(1 + tt):
                            bank = t_wait(t + (st["t"] + kt))
                            for h in range(4):
                                last = pe.transpose(bank[:, h * P:(h + 1) * P], pr[:, h, kt * P:(kt + 1) * P], ident)
                            last.then_inc(t_ready, 1)
                        bank = t_wait(t + (st["t"] + 1 + tt))
                        pe.wait_ge(probs_t_ready, 8 * l + (i + 1))
                        for j, h in enumerate((0, 2, 1, 3)):
                            for kt in range(1 + tt):
                                v = (kv_lat[:, kt, DH:2 * DH] if grp == 0 else
                                     qkv[:, kt, B_V + h * DH:B_V + (h + 1) * DH] if grp == 1 else
                                     qkv[:, kt, C_V + (grp - 2) * DH:C_V + (grp - 1) * DH])
                                last = pe.matmul(bank[:, j * DH:(j + 1) * DH], probs_t[:, kt, j, :], v,
                                                 start=(kt == 0), stop=(kt == tt))
                        last.then_inc(t_ready, 1)
                pe_xt(attn, t + T_AFTER_MIX1, 2, lambda e, tt: e.wait_ge(attn_ready, 8 * l + 8))
                pe.wait_ge(xt_ready, 4 * l + 2)
                for blk in range(2):
                    for half in range(2):
                        uu = u + (22 + 2 * blk + half)
                        s = uu.slot(RING)
                        for h in range(2):
                            half_is_split(uu, h)
                            br, first, stop = ((h, True, True), (2, h == 0, h == 1))[half]
                            for tt in range(TT):
                                ff = f + (24 + 6 * blk + 2 * br + tt)
                                bank = g_wait(ff) if first else g_bank[ff.slot(4)]
                                for k in (2 * h, 2 * h + 1):
                                    kk = 4 * half + k
                                    last = mm3(bank[:, :], xt_hi[:, kk, tt * P:(tt + 1) * P], xt_lo[:, kk, tt * P:(tt + 1) * P],
                                               w_hi[:, s, k * 512:(k + 1) * 512], w_lo[:, s, k * 512:(k + 1) * 512],
                                               first and k == 2 * h, stop and k == 2 * h + 1)
                            last.then_inc(w_used, 1)
                pe_xt(merged, t + (T_AFTER_MIX1 + 4), 2, lambda e, tt: e.wait_ge(merged_ready, 2 * l + 2))
                pe.wait_ge(xt_ready, 4 * l + 3)
                for blk in range(2):
                    pe_block(u + (26 + 2 * blk), f + (36 + 2 * blk))
                pe_xt(x, t + (T_AFTER_MIX1 + 8), 2, lambda e, tt: e.wait_ge(x_ready, 2 * l + 2))
                pe.wait_ge(xt_ready, 4 * l + 4)
                pe.wait_ge(router_split, 2)
                bank = t_wait(t + (T_AFTER_MIX1 + 12))
                for tt in range(TT):
                    for k in range(8):
                        last = mm3(bank[:, tt * NE:(tt + 1) * NE], xt_hi[:, k, tt * P:(tt + 1) * P],
                                   xt_lo[:, k, tt * P:(tt + 1) * P], wr_hi[:, k, :], wr_lo[:, k, :], k == 0, k == 7)
                last.then_inc(t_ready, 1)
                pe.wait_ge(in_grp_ready, l + 1)
                bank = t_wait(t + (T_AFTER_MIX1 + 13))
                pe.matmul(bank[:, 0:NG], c("before"), in_grp[:, 0, :], start=True, stop=True)
                pe.matmul(bank[:, NG:2 * NG], c("before"), in_grp[:, 1, :], start=True, stop=False)
                pe.matmul(bank[:, NG:2 * NG], c("ones", 0, P), in_grp[:, 0, :], start=False, stop=True)
                pe.matmul(bank[:, 2 * NG:3 * NG], c("ones", 0, P), in_grp[:, 0, :], start=True, stop=False)
                pe.matmul(bank[:, 2 * NG:3 * NG], c("ones", 0, P), in_grp[:, 1, :], start=False, stop=True).then_inc(t_ready, 1)

                R = rounds_loop(pe, 1, l + 1)
                with pe.Fori(0, R) as r:
                    at_r = in_round(l, done + r)
                    rnd = done + r
                    pe.wait_ge(onehot_ready, rnd + 1)
                    for tt in range(TT):
                        bank = t_wait(at_r["t"] + tt)
                        for g in range(NG):
                            last = pe.transpose(bank[:, g * P:(g + 1) * P], onehot[:, tt, g, :], ident)
                        last.then_inc(t_ready, 1)
                    for i in range(2):
                        bank = t_wait(at_r["t"] + (2 + i))
                        for j in range(2):
                            g = 2 * i + j
                            for tt in range(TT):
                                last = pe.matmul(bank[:, 4 * j:4 * j + 4], onehot[:, tt, g, :], comb[:, tt, 4 * g:4 * g + 4],
                                                 start=(tt == 0), stop=(tt == TT - 1))
                        last.then_inc(t_ready, 1)

                    def run(part, g):
                        count = plus(At(0, (rnd, 16)), 0, g, 4)
                        for what, e, half, place in walk(part, at_r, g):
                            if what == "gather":
                                src = g if part == "start" else g + 1
                                for i in range(2):
                                    bank = t_wait(place + i)
                                    for j in range(4):
                                        k = 4 * i + j
                                        for tt in range(TT):
                                            last = pe.matmul(bank[:, j * P:(j + 1) * P], x[:, tt, k * P:(k + 1) * P],
                                                             onehot[:, tt, bass.ds(src, 1), :].rearrange("p a b -> p (a b)"),
                                                             start=(tt == 0), stop=(tt == TT - 1))
                                    last.then_inc(t_ready, 1)
                            elif what == "hid_t":
                                pe.wait_ge(hid_ready, count.value(1, 2 + e + 1))
                                bank = t_wait(place)
                                for j in range(4):
                                    last = pe.transpose(bank[:, j * P:(j + 1) * P], hid[:, e % 2, j * P:(j + 1) * P], ident)
                                last.then_inc(t_ready, 1)
                            elif what == "back":
                                pe.drain().then_inc(s_ready, 1)
                            else:
                                s = place.slot(RING)
                                if what == "down" and half == 0:
                                    pe.wait_ge(hid_t_ready, count.value(1, 1 + e))
                                    if e == 0:
                                        s_wait(plus(at_r["s"], 0, g, 1))
                                if what == "gate" and half == 0 and e % EPG == 0:
                                    pe.wait_ge(xg_ready, plus(At(0, (rnd, 4)), 1 + (e > 0), g, 1).value())
                                for h in range(2):
                                    half_is_split(place, h)
                                    if what == "down":
                                        for nb in range(2):
                                            kk, c0 = 2 * half + h, h * DM + nb * 512
                                            last = mm3(s_bank[:, nb * 512:(nb + 1) * 512], hid_t_hi[:, e % 2, kk, :], hid_t_lo[:, e % 2, kk, :],
                                                       w_hi[:, s, c0:c0 + 512], w_lo[:, s, c0:c0 + 512],
                                                       e == 0 and kk == 0, e == EPG - 1 and kk == 3)
                                    else:
                                        ff = expert_fill(at_r, what, g, e)
                                        bank = g_bank[ff.slot(4)] if half or h else g_wait(ff)
                                        for k in (2 * h, 2 * h + 1):
                                            kk = 4 * half + k
                                            last = mm3(bank[:, :], xg_hi[:, kk, :], xg_lo[:, kk, :], w_hi[:, s, k * 512:(k + 1) * 512],
                                                       w_lo[:, s, k * 512:(k + 1) * 512], kk == 0, kk == 7)
                                    last.then_inc(w_used, 1)

                    all_parts(pe, run)
                    pe.wait_ge(y_ready, 4 * rnd + 4)
                    for i in range(4):
                        tt, nb = i // 2, i % 2
                        bank = g_wait(at_r["g"] + (32 + i))
                        for g in range(NG):
                            pe.matmul(bank[:, :], onehot_t[:, tt, g, :], y_hi[:, g, nb * 512:(nb + 1) * 512], start=(g == 0), stop=False)
                            last = pe.matmul(bank[:, :], onehot_t[:, tt, g, :], y_lo[:, g, nb * 512:(nb + 1) * 512], start=False, stop=(g == NG - 1))
                        last.then_inc(returned, 1)
                pe.reg_add(rho, rho, R)

            if stacks < 2:
                return
            done = pe.snap(rho, min_val=0, max_val=4)
            with pe.Fori(0, DEPTH) as l:
                first, mixer, second = layer2(l, done)

                def feed_forward(at, n, w, n_xt):
                    u, f, t, s0 = at["u"], at["g"], at["t"], at["s"]
                    pe_xt(ffn_y, t, 2, lambda e, tt: e.wait_ge(normed_ready, 6 * l + (2 * n + tt)))
                    pe.wait_ge(xt_ready, 5 * l + (2 * 4 + n_xt))
                    q0 = At(w * FB, (l, 2 * FB))

                    def gate_up(uj, sj):
                        s_wait(sj)
                        for half in range(2):
                            uu = uj + half
                            s = uu.slot(RING)
                            for h in range(2):
                                half_is_split(uu, h)
                                for tt in range(TT):
                                    for k in (2 * h, 2 * h + 1):
                                        kk = 4 * half + k
                                        last = mm3(s_bank[:, tt * 512:(tt + 1) * 512], xt_hi[:, kk, tt * P:(tt + 1) * P],
                                                   xt_lo[:, kk, tt * P:(tt + 1) * P], w_hi[:, s, k * 512:(k + 1) * 512],
                                                   w_lo[:, s, k * 512:(k + 1) * 512], kk == 0, kk == 7)
                                last.then_inc(w_used, 1)
                        pe.sem_inc(s_ready, 1)

                    def down(uu, q, first_, last_):
                        s = uu.slot(RING)
                        pe.wait_ge(ffn_t_ready, q.value(1, 1))
                        for k in range(2):
                            half_is_split(uu, k)
                            for i in range(4):
                                tt, nb = i // 2, i % 2
                                bank = g_wait(f + i) if first_ and k == 0 else g_bank[(f + i).slot(4)]
                                c0 = k * DM + nb * 512
                                last = mm3(bank[:, :], ffn_t_hi[:, k, tt * P:(tt + 1) * P], ffn_t_lo[:, k, tt * P:(tt + 1) * P],
                                           w_hi[:, s, c0:c0 + 512], w_lo[:, s, c0:c0 + 512], first_ and k == 0, last_ and k == 1)
                            last.then_inc(w_used, 1)

                    def hid_t(tj, q):
                        pe.wait_ge(ffn_hid_ready, q.value(1, 2))
                        for tt in range(TT):
                            bank = t_wait(tj + tt)
                            for k in range(2):
                                last = pe.transpose(bank[:, k * P:(k + 1) * P], ffn_hid[:, tt, k * P:(k + 1) * P], ident)
                            last.then_inc(t_ready, 1)

                    gate_up(u, s0)
                    hid_t(t + 4, q0)
                    gate_up(u + 2, s0 + 1)
                    down(u + 4, q0, True, False)
                    hid_t(t + 6, q0 + 1)
                    with pe.Fori(2, FB) as j:
                        uj, tj, qj, sj = (At(a.const + b, *a.terms, (j, k)) for a, b, k in ((u, -1, 3), (t, 4, 2), (q0, 0, 1), (s0, 0, 1)))
                        gate_up(uj, sj)
                        down(uj + 2, qj + -1, False, False)
                        hid_t(tj, qj)
                    down(u + (U_FFN - 1), q0 + (FB - 1), False, True)

                feed_forward(first, 1, 0, 1)

                u, f, t = mixer["u"], mixer["g"], mixer["t"]
                pe_xt(mix_y, t, 2, lambda e, tt: e.wait_ge(normed_ready, 6 * l + (4 + tt)))
                pe.wait_ge(xt_ready, 5 * l + (2 * 4 + 2))

                def head2(blk, half, a, n):
                    return qk_t[64 * half:64 * half + 64, blk, a:a + n]

                for i, blk in enumerate(PROJ2_ORDER):
                    pe_block(u + 2 * i, f + 2 * i)
                    if i == 2:
                        pe.wait_ge(mixer_in, 64 * l + 64)
                        bank = t_wait(t + 4)
                        fence(pe)
                        for k in range(4):
                            last = pe.transpose(bank[:, k * 32:(k + 1) * 32], taps_raw[:, k * P:(k + 1) * P], ident[0:32, 0:32])
                        last.then_inc(t_ready, 1)
                        pe.wait_ge(conv_u_ready, l + 1)
                        for tt in range(TT):
                            bank = t_wait(t + (5 + tt))
                            for k in range(4):
                                last = pe.transpose(bank[:, k * P:(k + 1) * P], proj[:, tt, CONV + k * P:CONV + (k + 1) * P], ident)
                            last.then_inc(t_ready, 1)
                    if i == 5:
                        pe.wait_ge(proj_ready, 9 * l + 4)
                        for j in range(4):
                            bank = t_wait(t + (7 + j))
                            for a in range(4):
                                b2, tt = 2 * j + a // 2, a % 2
                                last = pe.transpose(bank[:, a * P:(a + 1) * P], proj[:, tt, b2 * P:(b2 + 1) * P], ident)
                            last.then_inc(t_ready, 1)
                uu = u + 16
                s = uu.slot(RING)
                for h in range(2):
                    half_is_split(uu, h)
                    for tt in range(TT):
                        bank = g_bank[(f + (16 + tt)).slot(4)] if h else g_wait(f + (16 + tt))
                        for k in range(4 * h, 4 * h + 4):
                            last = mm3(bank[:, 0:16], xt_hi[:, k, tt * P:(tt + 1) * P], xt_lo[:, k, tt * P:(tt + 1) * P],
                                       w_hi[:, s, k * 256:k * 256 + 16], w_lo[:, s, k * 256:k * 256 + 16], k == 0, k == 7)
                    last.then_inc(w_used, 1)

                for st in PLAN2:
                    kind = st["kind"]
                    if kind == "gate":
                        n = st["n"]
                        pe_block(u + (17 + 2 * n), f + GATE2_G[n])
                    elif kind == "scores":
                        tt, kn, grp = st["tt"], P * (1 + st["tt"]), st["grp"]
                        pe.wait_ge(qk_t_ready, l + 1)
                        s_wait(mixer["s"] + st["s"])
                        for h in range(4):
                            b2 = (4 * grp + h) // 2
                            last = pe.matmul(s_at(h, kn), head2(b2, h % 2, tt * P, P), head2(4 + b2, h % 2, 0, kn), start=True, stop=True)
                        last.then_inc(s_ready, 1)
                    elif kind == "values":
                        tt, kn, grp, i = st["tt"], P * (1 + st["tt"]), st["grp"], st["n"]
                        pe.wait_ge(stick_ready, 4 * l + (i + 1))
                        for kt in range(1 + tt):
                            bank = t_wait(t + (st["t"] + kt))
                            for h in range(4):
                                last = pe.transpose(bank[:, h * P:(h + 1) * P], logit[:, h, kt * P:(kt + 1) * P], ident)
                            last.then_inc(t_ready, 1)
                        bank = t_wait(t + (st["t"] + 1 + tt))
                        pe.wait_ge(probs_t2_ready, 4 * l + (i + 1))
                        pe.wait_ge(proj_ready, 9 * l + 9)
                        for j, h in enumerate((0, 2, 1, 3)):
                            for kt in range(1 + tt):
                                c0 = S_V + (4 * grp + h) * DH
                                last = pe.matmul(bank[:, j * DH:(j + 1) * DH], probs_t2[:, kt, j, :], proj[:, kt, c0:c0 + DH],
                                                 start=(kt == 0), stop=(kt == tt))
                        last.then_inc(t_ready, 1)
                    elif kind == "conv_back":
                        pe.wait_ge(conv_y_ready, l + 1)
                        for tt in range(TT):
                            bank = t_wait(t + (st["t"] + tt))
                            for k in range(4):
                                last = pe.transpose(bank[:, k * P:(k + 1) * P], conv_y[:, k, tt * P:(tt + 1) * P], ident)
                            last.then_inc(t_ready, 1)
                    elif kind == "alpha":
                        for tt in range(TT):
                            bank = t_wait(t + (st["t"] + tt))
                            pe.transpose(bank[0:16, 0:P], proj[:, tt, L_LR:L_LR + 16], ident).then_inc(t_ready, 1)
                        pe.wait_ge(lr_t_ready, l + 1)
                        pe.wait_ge(alpha_in, 48 * l + 48)
                        for tt in range(TT):
                            bank = g_wait(f + (26 + tt))
                            last = pe.matmul(bank[:, 0:256], lr_t[:, tt, :], w_alpha, start=True, stop=True)
                        last.then_inc(kv_lat_done, 1)
                    elif kind == "gla_q":
                        bank = t_wait(t + st["t"])
                        for a in range(4):
                            h2, tt = a // 2, a % 2
                            last = pe.transpose(bank[:, a * P:(a + 1) * P], proj[:, tt, L_Q + h2 * P:L_Q + (h2 + 1) * P], ident)
                        last.then_inc(t_ready, 1)
                    elif kind == "decay":
                        pe.wait_ge(log_alpha_ready, l + 1)
                        bank = t_wait(t + st["t"])
                        for tt in range(TT):
                            last = pe.matmul(bank[:, tt * 256:(tt + 1) * 256], c("later_in_chunk"), log_alpha[:, tt, :], start=True, stop=True)
                        last.then_inc(t_ready, 1)
                        bank = t_wait(t + (st["t"] + 1))
                        for h2 in range(2):
                            for tt in range(TT):
                                a = h2 * 4 + tt * 2
                                last = pe.matmul(bank[:, a:a + 2], log_alpha[:, tt, h2 * P:(h2 + 1) * P], c("chunk_of"), start=True, stop=True)
                        last.then_inc(t_ready, 1)
                    elif kind == "states":
                        pe.wait_ge(k_dec_ready, l + 1)
                        for ch in range(4):
                            tt, c2 = ch // 2, ch % 2
                            bank = t_wait(t + (st["t"] + ch))
                            for h2 in range(2):
                                last = pe.matmul(bank[:, h2 * 256:(h2 + 1) * 256], k_dec[:, tt, c2, h2 * P:(h2 + 1) * P],
                                                 proj[:, tt, L_V + h2 * 256:L_V + (h2 + 1) * 256], start=True, stop=True)
                            last.then_inc(t_ready, 1)
                    elif kind == "gla_out":
                        pe.wait_ge(gla_q_ready, l + 1)
                        for tt in range(TT):
                            bank = t_wait(t + (st["t"] + tt))
                            pe.wait_ge(state_ready, 4 * l + (2 * tt + 2))
                            for c2 in range(2):
                                for h2 in range(2):
                                    a = tt * P + c2 * 64
                                    last = pe.matmul(bank[64 * c2:64 * c2 + 64, h2 * 256:(h2 + 1) * 256], lin_qt[:, h2, a:a + 64],
                                                     state[:, 2 * tt + c2, h2, :], start=True, stop=True)
                            last.then_inc(t_ready, 1)

                pe.wait_ge(branch_ready, 6 * l + 6)
                for i in range(TT * 3):
                    tt, br = divmod(i, 3)
                    bank = t_wait(t + (T_AFTER_MIX2 + i))
                    for j in range(4):
                        c0 = ATTN2[br] + j * P
                        last = pe.transpose(bank[:, j * P:(j + 1) * P], proj[:, tt, c0:c0 + P], ident)
                    last.then_inc(t_ready, 1)
                pe.wait_ge(xt_ready, 5 * l + (2 * 4 + 3))
                for blk in range(2):
                    for br in range(3):
                        uu = u + (29 + 3 * blk + br)
                        s = uu.slot(RING)
                        for h in range(2):
                            half_is_split(uu, h)
                            for tt in range(TT):
                                ff = f + (32 + 6 * blk + 2 * br + tt)
                                bank = g_bank[ff.slot(4)] if h else g_wait(ff)
                                for k in (2 * h, 2 * h + 1):
                                    kk = 4 * br + k
                                    last = mm3(bank[:, :], xt_hi[:, kk, tt * P:(tt + 1) * P], xt_lo[:, kk, tt * P:(tt + 1) * P],
                                               w_hi[:, s, k * 512:(k + 1) * 512], w_lo[:, s, k * 512:(k + 1) * 512], k == 0, k == 3)
                            last.then_inc(w_used, 1)
                pe_xt(merged2, t + (T_AFTER_MIX2 + 6), 2, lambda e, tt: e.wait_ge(merged2_ready, 2 * l + 2))
                pe.wait_ge(xt_ready, 5 * l + (2 * 4 + 4))
                for blk in range(2):
                    pe_block(u + (35 + 2 * blk), f + (44 + 2 * blk))

                feed_forward(second, 3, 1, 5)

        @block.vector
        def _(dve):
            dve.sem_inc(lo_ready, 2 * RING)
            for b in g_free + t_free:
                dve.sem_inc(b, 1)
            dve.sem_inc(s_free, 1)
            dve.sem_inc(x_ready, 1)
            dve.sem_inc(hid_ready, 2)
            dve.sem_inc(ffn_hid_ready, 1)
            dve.sem_inc(normed_ready, 1)
            dve.sem_inc(credits, 2)
            dve.wait_ge(const_in, 16)
            dve.wait_ge(x_in, 16)
            dve.wait_ge(router_split, 1)
            dve.tensor_tensor(wr_lo[:, :, :], w_router[:, :, :], wr_hi[:, :, :].bitcast(F32), ALU.subtract).then_inc(router_split, 1)

            ahead = ahead_of(split_lo)
            for h in range(AHEAD):
                split_lo(At(0), h)

            def rope(src, lo, heads):
                dst = rot[:, :, lo:lo + heads * DH].rearrange("p t (h d) -> p t h d", d=DH)
                src = src.rearrange("p t (h d) -> p t h d", d=DH)
                tab = c("rope").rearrange("p (t m) -> p t m", t=TT)
                h = DH // 2
                dve.drain()
                for tt in range(TT):
                    def table(a, n):
                        return tab[:, tt, a:a + n].unsqueeze(1).to_broadcast([P, heads, n])
                    dve.tensor_tensor(dst[:, tt], src[:, tt], table(0, DH), ALU.mult)
                    dve.tensor_tensor(rope_tmp[:, tt, 0:heads, 0:h], src[:, tt, :, h:DH], table(DH, h), ALU.mult)
                    dve.tensor_tensor(rope_tmp[:, tt, 0:heads, h:DH], src[:, tt, :, 0:h], table(DH + h, h), ALU.mult)
                dve.drain()
                for tt in range(TT):
                    last = dve.tensor_tensor(dst[:, tt], dst[:, tt], rope_tmp[:, tt, 0:heads, :], ALU.add)
                return last

            def all_equal_max(src, of, n, out_hot):
                dve.tensor_reduce(best[:, :], src, AX.X, ALU.max)
                dve.drain()
                dve.tensor_tensor(key[:, :, 0:n], src, best[:, :].unsqueeze(2).to_broadcast([P, TT, n]), ALU.is_equal)
                dve.drain()
                dve.tensor_tensor(key[:, :, 0:n], key[:, :, 0:n], of.unsqueeze(1).to_broadcast([P, TT, n]), ALU.mult)
                dve.drain()
                dve.tensor_reduce(best[:, :], key[:, :, 0:n], AX.X, ALU.max)
                dve.drain()
                dve.tensor_tensor(out_hot, key[:, :, 0:n], best[:, :].unsqueeze(2).to_broadcast([P, TT, n]), ALU.is_equal)
                dve.drain()

            rho = dve.alloc_register("rounds_done_dve")
            dve.reg_mov(rho, 0)
            with dve.Fori(0, DEPTH) as l:
                done = dve.snap(rho, min_val=0, max_val=4)
                at = layer1(l, done)
                u, f, t = at["u"], at["g"], at["t"]
                dve_xt(t, At(0, (l, 16)), 2)
                for blk in range(5):
                    ahead(u, 2 * blk)
                    ahead(u, 2 * blk + 1)
                    if blk == 2:
                        dve.wait_ge(qkv_ready, 5 * l + 2)
                        fence(dve)
                        rope(qkv[:, :, A_Q:A_Q + 256], 0, 4)
                        rope(qkv[:, :, A_IQ:A_IQ + 320], 256, 5)
                    if blk == 3:
                        dve.wait_ge(qkv_ready, 5 * l + 3)
                        fence(dve)
                        rope(qkv[:, :, B_Q:B_Q + 512], 640, 8)
                dve.wait_ge(qkv_ready, 5 * l + 5)
                fence(dve)
                rope(qkv[:, :, C_Q:C_Q + 640], 1152, 10)
                dve.wait_ge(kv_lat_ready, l + 1)
                fence(dve)
                rope(kv_lat[:, :, 0:DH], 576, 1)
                dve.drain()
                for tt in range(TT):
                    for a, b in ((1792, 576), (1856, 512), (1920, 1728), (1984, 1664)):
                        dve.tensor_copy(rot[:, tt, a:a + DH], rot[:, tt, b:b + DH])
                dve.drain().then_inc(rot_ready, 1)

                for st in PLAN1:
                    kind = st["kind"]
                    if kind == "gate":
                        k = 10 + 2 * st["n"]
                        ahead(u, k)
                        ahead(u, k + 1)
                    elif kind == "index":
                        tt = st["tt"]
                        kn = P * (1 + tt)
                        mask = c("mask_causal", 256 - kn)
                        work = idx_work[:, 0:kn]
                        dve.drain()
                        dve.wait_ge(relu_ready, 2 * l + (tt + 1))
                        dve.sem_inc(s_free, 1)
                        dve.tensor_scalar(work, relu_dots[:, 0, 0:kn], qkv[:, tt, A_IW:A_IW + 1], 0.0, ALU.mult, ALU.add)
                        order = (0, 2, 1, 3)
                        for h in range(1, 4):
                            dve.drain()
                            dve.scalar_tensor_tensor(out=work, in0=relu_dots[:, h, 0:kn], scalar=qkv[:, tt, A_IW + order[h]:A_IW + order[h] + 1],
                                                     in1=work, op0=ALU.mult, op1=ALU.add)
                        dve.drain().then_inc(chosen_ready, 1)
                        dve.tensor_tensor(work, work, mask, ALU.add)
                        for _ in range(TOPK // 8):
                            dve.drain()
                            dve.max(top8[:, :], work)
                            dve.drain()
                            dve.match_replace(out=work, in_to_replace=top8[:, :], in_values=work, imm_value=TAKEN)
                        dve.drain()
                        dve.tensor_scalar(work, work, TAKEN / 3, 1.0, ALU.is_le, ALU.subtract)
                        dve.drain()
                        dve.scalar_tensor_tensor(out=chosen[:, tt, 0:kn], in0=work, scalar=-NEG, in1=mask, op0=ALU.mult, op1=ALU.add)
                    elif kind == "scores":
                        tt, i, grp = st["tt"], st["n"], st["grp"]
                        kn, b = P * (1 + tt), st["n"] % 2
                        mask = (chosen[:, tt, 0:kn] if grp == 0 else c("mask_causal" if grp == 1 else "mask_window", 256 - kn))
                        sc = masked[:, b, 0:4 * kn].rearrange("p (h k) -> p h k", h=4)
                        dve.drain()
                        dve.wait_ge(s_ready, (at["s"] + st["s"]).value(1, 1))
                        for half in range(2):
                            dve.scalar_tensor_tensor(out=sc[:, 2 * half:2 * half + 2, :], in0=s_half(half, kn), scalar=SCALE,
                                                     in1=mask.unsqueeze(1).to_broadcast([P, 2, kn]), op0=ALU.mult, op1=ALU.add)
                        dve.drain().then_inc(s_free, 1)
                        dve.tensor_reduce(row_max[:, b, :], sc, AX.X, ALU.max)
                        dve.drain()
                        if grp >= 2:
                            sk = sinks[:, 4 * (grp - 2):4 * (grp - 1)].rearrange("p (i half) -> p half i", half=2)
                            mx = row_max[:, b, :].rearrange("p (half i) -> p half i", half=2)
                            dve.tensor_tensor(mx, mx, sk, ALU.max)
                            dve.drain()
                            dve.tensor_tensor(sink_exp[:, b, :].rearrange("p (half i) -> p half i", half=2), sk, mx, ALU.subtract)
                        dve.tensor_scalar(neg_max[:, b, :], row_max[:, b, :], -1.0, None, ALU.mult)
                        dve.drain().then_inc(max_ready, 1)
                    elif kind == "values":
                        tt, i, grp = st["tt"], st["n"], st["grp"]
                        b = i % 2
                        tf = t + (st["t"] + 1 + tt)
                        dve.wait_ge(probs_ready, 8 * l + (i + 1))
                        if grp >= 2:
                            dve.tensor_tensor(row_sum[:, b, :], row_sum[:, b, :], sink_exp[:, b, :], ALU.add)
                            dve.drain()
                        dve.reciprocal(inv_sum[:, b, :], row_sum[:, b, :])
                        dve.drain()
                        dve.wait_ge(t_ready, tf.value(1, 1))
                        for half in range(2):
                            dve.tensor_tensor(attn[:, tt, grp * 256:(grp + 1) * 256].rearrange("p (i half d) -> p half i d", half=2, d=DH)[:, half],
                                              t_bank[tf.slot(2)][:, half * P:(half + 1) * P].rearrange("p (i d) -> p i d", d=DH),
                                              inv_sum[:, b, 2 * half:2 * half + 2].unsqueeze(2).to_broadcast([P, 2, DH]), ALU.mult)
                        dve.drain().then_inc(t_free[tf.slot(2)], 1)
                        dve.sem_inc(attn_ready, 1)
                dve_xt(t + T_AFTER_MIX1, At(4, (l, 16)), 2)
                dve.wait_ge(gate_ready, 6 * l + 6)
                for blk in range(2):
                    for half in range(2):
                        ahead(u + 22, 2 * blk + half)
                        unit_is_used(dve, u + (22 + 2 * blk + half))
                        fence(dve)
                        for br in ((0, 1) if half == 0 else (2,)):
                            for tt in range(TT):
                                b = (f + (24 + 6 * blk + 2 * br + tt)).slot(4)
                                g_ = gate[:, tt, br * DM + blk * 512:br * DM + blk * 512 + 512]
                                m_ = merged[:, tt, blk * 512:(blk + 1) * 512]
                                dve.drain()
                                dve.tensor_tensor(m_ if br == 0 else gated[:, tt, :], g_bank[b][:, :], g_, ALU.mult).then_inc(g_free[b], 1)
                                if br:
                                    dve.drain()
                                    dve.tensor_tensor(m_, m_, gated[:, tt, :], ALU.add)
                    dve.drain().then_inc(merged_ready, 1)
                dve_xt(t + (T_AFTER_MIX1 + 4), At(8, (l, 16)), 2)
                for blk in range(2):
                    ahead(u + 26, 2 * blk)
                    ahead(u + 26, 2 * blk + 1)
                    unit_is_used(dve, u + (26 + 2 * blk + 1))
                    for tt in range(TT):
                        b = (f + (36 + 2 * blk + tt)).slot(4)
                        xs = x[:, tt, blk * 512:(blk + 1) * 512]
                        dve.scalar_tensor_tensor(out=xs, in0=xs, scalar=ALPHA, in1=g_bank[b][:, :], op0=ALU.mult,
                                                 op1=ALU.add).then_inc(g_free[b], 1)
                layer_norm(x, x, At(0, (l, 2)), gains[:, 0, :], gains[:, 1, :], 64 * l + 32)
                dve_xt(t + (T_AFTER_MIX1 + 8), At(12, (l, 16)), 2)

                dve.wait_ge(aff_ready, l + 1)
                dve.tensor_tensor(sel[:, :, :], aff[:, :, :], b_router[:, :].unsqueeze(1).to_broadcast([P, TT, NE]), ALU.add)
                dve.drain()
                s4 = sel[:, :, :].rearrange("p t (g e) -> p (t g) e", e=EPG)
                dve.tensor_tensor(pair[:, :, 0:3], s4[:, :, 0:3], s4[:, :, 1:4], ALU.add)
                dve.tensor_tensor(pair[:, :, 3:5], s4[:, :, 0:2], s4[:, :, 2:4], ALU.add)
                dve.tensor_tensor(pair[:, :, 5:6], s4[:, :, 0:1], s4[:, :, 3:4], ALU.add)
                dve.drain()
                dve.tensor_reduce(grp_score[:, :, :].rearrange("p t g -> p (t g)"), pair[:, :, :], AX.X, ALU.max)
                dve.drain()
                all_equal_max(grp_score[:, :, :], c("first_of4"), NG, in_grp[:, :, :])
                dve.drain().then_inc(in_grp_ready, 1)
                dve.tensor_scalar(grp_score[:, :, :], in_grp[:, :, :], 1.0, -NEG, ALU.subtract, ALU.mult)
                dve.drain()
                dve.tensor_tensor(s4, s4, grp_score[:, :, :].rearrange("p t g -> p (t g)").unsqueeze(2).to_broadcast([P, TT * NG, EPG]), ALU.add)
                dve.drain()
                all_equal_max(sel[:, :, :], c("first_of16"), NE, hot1[:, :, :])
                dve.scalar_tensor_tensor(out=sel[:, :, :], in0=hot1[:, :, :], scalar=2 * NEG, in1=sel[:, :, :], op0=ALU.mult, op1=ALU.add)
                dve.drain()
                all_equal_max(sel[:, :, :], c("first_of16"), NE, hot2[:, :, :])
                dve.tensor_tensor(hot1[:, :, :], hot1[:, :, :], hot2[:, :, :], ALU.add)
                dve.drain()
                dve.tensor_tensor(comb[:, :, :], hot1[:, :, :], aff[:, :, :], ALU.mult)
                dve.drain()
                dve.tensor_reduce(best[:, :], comb[:, :, :], AX.X, ALU.add)
                dve.drain()
                dve.reciprocal(best[:, :], best[:, :])
                dve.drain()
                dve.tensor_tensor(comb[:, :, :], comb[:, :, :], best[:, :].unsqueeze(2).to_broadcast([P, TT, NE]), ALU.mult)
                tf = t + (T_AFTER_MIX1 + 13)
                dve.wait_ge(t_ready, tf.value(1, 1))
                dve.scalar_tensor_tensor(out=place[:, :, :], in0=t_bank[tf.slot(2)][:, 0:2 * NG].rearrange("p (t g) -> p t g", t=TT), scalar=1024.0, in1=in_grp[:, :, :],
                                         op0=ALU.add, op1=ALU.mult)
                dve.tensor_copy(n_grp[:, :], t_bank[tf.slot(2)][:, 2 * NG:3 * NG]).then_inc(t_free[tf.slot(2)], 1)
                dve.drain()
                dve.tensor_scalar(place[:, :, :], place[:, :, :], -1024.0, None, ALU.add)
                dve.tensor_reduce(rounds_f[:, :], n_grp[:, :], AX.X, ALU.max)
                dve.drain()
                dve.tensor_scalar(rounds_f[:, :], rounds_f[:, :], float(P), 1.0, ALU.is_gt, ALU.add)
                dve.drain()
                dve.tensor_copy(rounds_i[:, :], rounds_f[:, :])
                dve.drain().then_inc(rounds_ready, 1)
                for tt in range(TT):
                    dve.tensor_scalar(acc[:, tt, :], x[:, tt, :], ALPHA, None, ALU.mult)
                R = rounds_loop(dve, 1, l + 1)
                with dve.Fori(0, R) as r:
                    at_r = in_round(l, done + r)
                    rnd = done + r
                    dve.drain()
                    for tt in range(TT):
                        for g in range(NG):
                            dve.tensor_scalar(onehot[:, tt, g, :], c("iota"), place[:, tt, g:g + 1], None, ALU.is_equal)
                    dve.drain().then_inc(onehot_ready, 1)
                    dve.tensor_scalar(place[:, :, :], place[:, :, :], float(-P), None, ALU.add)
                    dve.wait_ge(comb_slot_ready, rnd + 1)
                    fence(dve)

                    def run(part, g):
                        count = plus(At(0, (rnd, 16)), 0, g, 4)
                        for what, e, half, place in walk(part, at_r, g):
                            if half is not None:
                                ahead(place)
                                if what == "up" and half == 1:
                                    b = expert_fill(at_r, what, g, e).slot(4)
                                    unit_is_used(dve, place)
                                    dve.wait_ge(silu_ready, count.value(1, e + 1))
                                    dve.scalar_tensor_tensor(out=hid[:, e % 2, :], in0=g_bank[b][:, :],
                                                             scalar=comb_slot[:, bass.ds(g * EPG + e, 1)], in1=silu_g[:, e % 2, :],
                                                             op0=ALU.mult, op1=ALU.mult).then_inc(g_free[b], 1)
                                    dve.drain().then_inc(hid_ready, 1)
                            elif what == "gather":
                                first_count = plus(At(0, (rnd, 8)), 1 if part == "start" else 3, g, 2)
                                for i in range(2):
                                    tf = place + i
                                    dve.wait_ge(xg_hi_ready, (first_count + i).value())
                                    dve.tensor_tensor(xg_lo[:, 4 * i:4 * i + 4, :], t_bank[tf.slot(2)][:, :].rearrange("p (a b) -> p a b", a=4),
                                                      xg_hi[:, 4 * i:4 * i + 4, :].bitcast(F32), ALU.subtract).then_inc(t_free[tf.slot(2)], 1)
                                dve.drain().then_inc(xg_ready, 1)
                            elif what == "hid_t":
                                dve.wait_ge(hid_hi_ready, count.value(1, e + 1))
                                dve.tensor_tensor(hid_t_lo[:, e % 2, :, :], t_bank[place.slot(2)][:, :].rearrange("p (a b) -> p a b", a=4),
                                                  hid_t_hi[:, e % 2, :, :].bitcast(F32), ALU.subtract).then_inc(t_free[place.slot(2)], 1)
                                dve.drain().then_inc(hid_t_ready, 1)
                            else:
                                dve.wait_ge(y_hi_ready, plus(At(0, (rnd, 4)), 1, g, 1).value())
                                dve.tensor_tensor(y_lo[:, bass.ds(g, 1), :], s_bank[:, :].unsqueeze(1), y_hi[:, bass.ds(g, 1), :].bitcast(F32),
                                                  ALU.subtract).then_inc(s_free, 1)
                                dve.drain().then_inc(y_ready, 1)

                    all_parts(dve, run)
                    for i in range(4):
                        tt, nb = i // 2, i % 2
                        b = (at_r["g"] + (32 + i)).slot(4)
                        dve.wait_ge(returned, 4 * rnd + (i + 1))
                        a_ = acc[:, tt, nb * 512:(nb + 1) * 512]
                        dve.tensor_tensor(a_, a_, g_bank[b][:, :], ALU.add).then_inc(g_free[b], 1)
                    dve.drain()
                dve.reg_add(rho, rho, R)
                layer_norm(acc, x, At(1, (l, 2)), gains[:, 0, :], gains[:, 1, :], 64 * l + 64)

            if stacks < 2:
                return
            done = dve.snap(rho, min_val=0, max_val=4)
            with dve.Fori(0, DEPTH) as l:
                first, mixer, second = layer2(l, done)

                def norm_in(dst, i):
                    dve.wait_ge(pre_in, 48 * l + (16 * i + 16))
                    for tt in range(TT):
                        dve.tensor_tensor(dst[:, tt, :], x[:, tt, :], gains[:, 0, :], ALU.mult)
                        dve.drain().then_inc(normed_ready, 1)

                def in_root(n, sq):
                    dve.wait_ge(square_ready, 15 * l + (sq + 1))
                    dve.tensor_scalar(rstd_in[:, :], mean_sq[:, :, 0:1].rearrange("p a b -> p (a b)"), RMS_EPS, None, ALU.add)
                    dve.drain()
                    dve.reciprocal(rstd_in[:, :], rstd_in[:, :]).then_inc(var_ready, 1)
                    dve.wait_ge(rstd_ready, At(4 + n, (l, 11)).value(1, 1))
                    fence(dve)

                def norm_out(dst, n, sq, i, fills, factor):
                    dve.wait_ge(post_in, 48 * l + (16 * i + 16))
                    fence(dve)
                    for tt in range(TT):
                        for nb in range(2):
                            cols = slice(nb * 512, (nb + 1) * 512)
                            b = fills[tt][nb].slot(4)
                            dve.wait_ge(square_ready, 15 * l + (sq + 2 * tt + nb + 1))
                            dve.tensor_tensor(dst[:, tt, cols], g_bank[b][:, :], gains[:, 1, cols], ALU.mult).then_inc(g_free[b], 1)
                        dve.scalar_tensor_tensor(out=rstd[:, tt:tt + 1], in0=mean_sq[:, tt, 0:1], scalar=RMS_EPS / factor ** 2,
                                                 in1=mean_sq[:, tt, 1:2], op0=ALU.add, op1=ALU.add)
                        dve.drain()
                        dve.reciprocal(rstd[:, tt:tt + 1], rstd[:, tt:tt + 1]).then_inc(var_ready, 1)
                    for tt in range(TT):
                        dve.wait_ge(rstd_ready, At(4 + n + tt, (l, 11)).value(1, 1))
                        dve.scalar_tensor_tensor(out=x[:, tt, :], in0=dst[:, tt, :], scalar=rstd[:, tt:tt + 1], in1=x[:, tt, :],
                                                 op0=ALU.mult, op1=ALU.add)
                    dve.drain().then_inc(x_ready, 1)

                def feed_forward(at, n, sq, i, w, n_xt):
                    u, f, t = at["u"], at["g"], at["t"]
                    norm_in(ffn_y, i)
                    dve_xt(t, At(16 * DEPTH + n_xt, (l, XT_LAYER2)), 2)
                    in_root(n, sq)
                    q0 = At(w * FB, (l, 2 * FB))

                    def hidden(q):
                        dve.wait_ge(up_silu_ready, q.value(1, 1))
                        for tt in range(TT):
                            dve.scalar_tensor_tensor(out=ffn_hid[:, tt, :], in0=s_bank[:, tt * 512 + 256:(tt + 1) * 512],
                                                     scalar=rstd_in[:, tt:tt + 1], in1=ffn_silu[:, tt, :], op0=ALU.mult, op1=ALU.mult)
                        dve.drain().then_inc(ffn_hid_ready, 1)
                        dve.sem_inc(s_free, 1)

                    def hid_t(tj, q):
                        for tt in range(TT):
                            tf = tj + tt
                            dve.wait_ge(ffn_hi_ready, q.value(2, tt + 1))
                            part = slice(tt * P, (tt + 1) * P)
                            dve.tensor_tensor(ffn_t_lo[:, :, part], t_bank[tf.slot(2)][:, 0:256].rearrange("p (a b) -> p a b", a=2),
                                              ffn_t_hi[:, :, part].bitcast(F32), ALU.subtract).then_inc(t_free[tf.slot(2)], 1)
                        dve.drain().then_inc(ffn_t_ready, 1)

                    ahead(u)
                    ahead(u, 1)
                    hidden(q0)
                    hid_t(t + 4, q0)
                    ahead(u, 2)
                    ahead(u, 3)
                    hidden(q0 + 1)
                    ahead(u, 4)
                    hid_t(t + 6, q0 + 1)

                    with dve.Fori(2, FB) as j:
                        uj, tj, qj = (At(a.const + b, *a.terms, (j, k)) for a, b, k in ((u, -1, 3), (t, 4, 2), (q0, 0, 1)))
                        ahead(uj)
                        ahead(uj, 1)
                        hidden(qj)
                        ahead(uj, 2)
                        hid_t(tj, qj)
                    ahead(u, U_FFN - 1)
                    unit_is_used(dve, u + (U_FFN - 1))
                    fence(dve)
                    norm_out(ffn_y, n + 1, sq + 1, i, ffn_fills(f), 0.5)

                feed_forward(first, 0, 0, 0, 0, 0)

                u, f, t = mixer["u"], mixer["g"], mixer["t"]
                norm_in(mix_y, 1)
                dve_xt(t, At(16 * DEPTH + 4, (l, XT_LAYER2)), 2)
                in_root(3, 5)

                def convolve(a, b):
                    for k in range(a, b):
                        dve.drain()
                        for ch in range(4):
                            src = conv_in[:, ch, k:k + TT * P]
                            if k == 0:
                                dve.tensor_scalar(conv_y[:, ch, :], src, taps[:, ch, 0:1], taps[:, ch, TAPS:TAPS + 1], ALU.mult, ALU.add)
                            else:
                                dve.scalar_tensor_tensor(out=conv_y[:, ch, :], in0=src, scalar=taps[:, ch, k:k + 1], in1=conv_y[:, ch, :],
                                                         op0=ALU.mult, op1=ALU.add)
                    if b == TAPS:
                        dve.drain().then_inc(conv_y_ready, 1)

                for i, blk in enumerate(PROJ2_ORDER):
                    ahead(u, 2 * i)
                    ahead(u, 2 * i + 1)
                    if i == 2:
                        dve.wait_ge(proj_ready, 9 * l + 2)
                        for tt in range(TT):
                            dve.tensor_tensor(proj[:, tt, CONV:CONV + 512], proj[:, tt, CONV:CONV + 512], proj[:, tt, CONV + 512:CONV + 1024], ALU.mult)
                        dve.drain().then_inc(conv_u_ready, 1)
                    if i == 3:
                        dve.wait_ge(conv_in_ready, l + 1)
                        fence(dve)
                    if i >= 3:
                        convolve(4 * (i - 3), 4 * (i - 2))
                ahead(u, 16)

                for st in PLAN2:
                    kind = st["kind"]
                    if kind == "gate":
                        k = 17 + 2 * st["n"]
                        ahead(u, k)
                        ahead(u, k + 1)
                        if st["taps"][1]:
                            convolve(*st["taps"])
                    elif kind == "scores":
                        tt, i = st["tt"], st["n"]
                        kn = P * (1 + tt)
                        mask = c("mask_earlier", 256 - kn)
                        dve.drain()
                        dve.wait_ge(s_ready, (mixer["s"] + st["s"]).value(1, 1))
                        for half in range(2):
                            dve.scalar_tensor_tensor(out=logit[:, 2 * half:2 * half + 2, 0:kn], in0=s_half(half, kn), scalar=SCALE,
                                                     in1=mask.unsqueeze(1).to_broadcast([P, 2, kn]), op0=ALU.mult, op1=ALU.add)
                        dve.drain().then_inc(s_free, 1)
                        dve.sem_inc(logit_ready, 1)
                        dve.wait_ge(soft_ready, 4 * l + (i + 1))
                        sp_ = soft[:, :, 0:kn]
                        dve.scalar_tensor_tensor(out=sp_, in0=logit[:, :, 0:kn], scalar=0.0, in1=sp_, op0=ALU.max, op1=ALU.add)
                        dve.drain()
                        for h in range(4):
                            row = soft[:, h, kn - 1::-1] if kn == 256 else soft[:, h, 0:kn][:, ::-1]
                            dve.tensor_tensor_scan(row, c("ones", 0, 1).to_broadcast([P, kn]), row, 0.0, ALU.mult, ALU.add)
                        dve.drain()
                        dve.tensor_tensor(logit[:, :, 0:kn], logit[:, :, 0:kn], sp_, ALU.subtract)
                        dve.drain().then_inc(log_w_ready, 1)
                    elif kind == "values":
                        tt, grp = st["tt"], st["grp"]
                        tf = t + (st["t"] + 1 + tt)
                        dve.wait_ge(t_ready, tf.value(1, 1))
                        for half in range(2):
                            dve.tensor_copy(proj[:, tt, grp * 256:(grp + 1) * 256].rearrange("p (i half d) -> p half i d", half=2, d=DH)[:, half],
                                            t_bank[tf.slot(2)][:, half * P:(half + 1) * P].rearrange("p (i d) -> p i d", d=DH))
                        dve.drain().then_inc(t_free[tf.slot(2)], 1)
                        dve.sem_inc(branch_ready, 1)
                    elif kind == "conv_back":
                        dve.drain()
                        for tt in range(TT):
                            tf = t + (st["t"] + tt)
                            dve.wait_ge(t_ready, tf.value(1, 1))
                            dve.bn_stats(stats[:, tt, 0:6], t_bank[tf.slot(2)][:, :])
                        dve.drain()
                        for tt in range(TT):
                            dve.bn_aggr(mean_var[:, tt, :], stats[:, tt, 0:6])
                        dve.drain()
                        dve.tensor_scalar(mean_var[:, :, 1:2], mean_var[:, :, 1:2], RMS_EPS, None, ALU.add)
                        dve.drain()
                        dve.reciprocal(rstd[:, :], mean_var[:, :, 1:2].rearrange("p a b -> p (a b)")).then_inc(var_ready, 1)
                        dve.wait_ge(rstd_ready, At(4 + 4, (l, 11)).value(1, 1))
                        out_ = [proj[:, tt, ATTN2[1]:ATTN2[1] + 512] for tt in range(TT)]
                        for tt in range(TT):
                            tf = t + (st["t"] + tt)
                            dve.tensor_scalar(out_[tt], t_bank[tf.slot(2)][:, :], mean_var[:, tt, 0:1], rstd[:, tt:tt + 1],
                                              ALU.subtract, ALU.mult).then_inc(t_free[tf.slot(2)], 1)
                        dve.drain()
                        for tt in range(TT):
                            dve.tensor_tensor(out_[tt], out_[tt], conv_row[:, 0:512], ALU.mult)
                        dve.drain()
                        for tt in range(TT):
                            dve.tensor_tensor(out_[tt], out_[tt], conv_row[:, 512:1024], ALU.add)
                        dve.drain().then_inc(conv_mid_ready, 1)
                    elif kind == "alpha":
                        dve.wait_ge(kv_lat_done, l + (DEPTH + 1))
                        dve.wait_ge(alpha_in, 48 * l + 48)
                        for tt in range(TT):
                            b = (f + (26 + tt)).slot(4)
                            dve.tensor_tensor(log_alpha[:, tt, :], g_bank[b][:, 0:256], b_alpha, ALU.add).then_inc(g_free[b], 1)
                        dve.drain().then_inc(alpha_in_ready, 1)
                        dve.wait_ge(alpha_soft_ready, l + 1)
                        la = log_alpha.rearrange(flat)
                        dve.scalar_tensor_tensor(out=la, in0=la, scalar=0.0, in1=log_tmp, op0=ALU.min, op1=ALU.subtract)
                        dve.drain()
                        dve.tensor_scalar(la, la, 1.0 / 16.0, None, ALU.mult)
                        dve.drain().then_inc(log_alpha_ready, 1)
                    elif kind == "states":
                        dve.wait_ge(decay_ready, l + 1)
                        dve.tensor_tensor(decay, decay, proj[:, :, L_K:L_K + 256], ALU.mult)
                        dve.drain()
                        for tt in range(TT):
                            for c2 in range(2):
                                dve.tensor_scalar(k_dec[:, tt, c2, :], decay[:, tt, :], c("chunk_of", c2, c2 + 1), None, ALU.mult)
                        dve.drain().then_inc(k_dec_ready, 1)
                        block_mask = c("chunk_of").unsqueeze(1).unsqueeze(3).to_broadcast([P, 2, 2, P])
                        for ch in range(4):
                            tf = t + (st["t"] + ch)
                            dst = state[:, 0, :, :].rearrange("p h (v n) -> p h v n", v=2) if ch == 0 else kv_new.rearrange("p (h v n) -> p h v n", h=2, v=2)
                            dve.wait_ge(t_ready, tf.value(1, 1))
                            dve.tensor_tensor(dst, t_bank[tf.slot(2)][:, :].rearrange("p (h v n) -> p h v n", h=2, v=2), block_mask, ALU.mult)\
                               .then_inc(t_free[tf.slot(2)], 1)
                            dve.drain()
                            for h2 in range(2) if ch else ():
                                dve.scalar_tensor_tensor(out=state[:, ch, h2, :], in0=state[:, ch - 1, h2, :], scalar=lam[:, h2 * 4 + ch:h2 * 4 + ch + 1],
                                                         in1=kv_new[:, h2 * 256:(h2 + 1) * 256], op0=ALU.mult, op1=ALU.add)
                            dve.drain().then_inc(state_ready, 1)
                    elif kind == "gla_out":
                        for tt in range(TT):
                            tf = t + (st["t"] + tt)
                            dve.wait_ge(t_ready, tf.value(1, 1))
                            dve.tensor_copy(gla_o[:, tt, :], t_bank[tf.slot(2)][:, :]).then_inc(t_free[tf.slot(2)], 1)
                            dve.drain()
                            dve.tensor_tensor(kv_new, gla_o[:, tt, :], gla_o[:, tt, :], ALU.mult)
                            dve.drain()
                            dve.tensor_reduce(mean_sq8[:, tt, :], kv_new.rearrange("p (h n) -> p h n", h=4), AX.X, ALU.add)
                        dve.drain()
                        dve.tensor_scalar(mean_sq8[:, :, :], mean_sq8[:, :, :], 1.0 / 128.0, RMS_EPS, ALU.mult, ALU.add)
                        dve.drain()
                        dve.reciprocal(mean_sq8[:, :, :], mean_sq8[:, :, :]).then_inc(var_ready, 1)
                        dve.wait_ge(rstd_ready, At(4 + 5, (l, 11)).value(1, 1))
                        for tt in range(TT):
                            dve.tensor_tensor(gla_o[:, tt, :].rearrange("p (h n) -> p h n", h=4), gla_o[:, tt, :].rearrange("p (h n) -> p h n", h=4),
                                              mean_sq8[:, tt, :].unsqueeze(2).to_broadcast([P, 4, P]), ALU.mult)
                        dve.drain()
                        for tt in range(TT):
                            dve.tensor_tensor(gla_o[:, tt, :], gla_o[:, tt, :], gla_gain, ALU.mult)
                        dve.drain()
                        for tt in range(TT):
                            dve.tensor_tensor(proj[:, tt, ATTN2[2]:ATTN2[2] + 512], gla_o[:, tt, :], proj[:, tt, L_R:L_R + 512], ALU.mult)
                        dve.drain().then_inc(branch_ready, 1)
                dve_xt(t + T_AFTER_MIX2, At(16 * DEPTH + 8, (l, XT_LAYER2)), 3)
                dve.wait_ge(gate2_ready, 6 * l + 6)
                for blk in range(2):
                    for br in range(3):
                        k = 3 * blk + br
                        ahead(u + 29, k)
                        unit_is_used(dve, u + (29 + k))
                        fence(dve)
                        for tt in range(TT):
                            b = (f + (32 + 6 * blk + 2 * br + tt)).slot(4)
                            g_ = gate2[:, tt, br * DM + blk * 512:br * DM + blk * 512 + 512]
                            m_ = merged2[:, tt, blk * 512:(blk + 1) * 512]
                            tmp = gla_o[:, tt, :]
                            dve.drain()
                            dve.tensor_tensor(m_ if br == 0 else tmp, g_bank[b][:, :], g_, ALU.mult).then_inc(g_free[b], 1)
                            if br:
                                dve.drain()
                                dve.tensor_tensor(m_, m_, tmp, ALU.add)
                    dve.drain().then_inc(merged2_ready, 1)
                dve_xt(t + (T_AFTER_MIX2 + 6), At(16 * DEPTH + 14, (l, XT_LAYER2)), 2)
                for k in range(4):
                    ahead(u + 35, k)
                unit_is_used(dve, u + 38)
                fence(dve)
                norm_out(mix_y, 6, 6, 1, mix_fills(f), 1.0)

                feed_forward(second, 8, 10, 2, 1, 18)


def kernel(**inputs):
    import numpy as _np
    import concourse.bacc as _bacc
    from concourse import mybir as _mybir
    from concourse.bass_utils import run_bass_kernel_spmd as _run

    nc = _bacc.Bacc("TRN2", target_bir_lowering=False, num_devices=1)
    table, const_at = shape_constants()
    arrays, d = {}, {}
    for name, a in dict(inputs, shape_constants=table).items():
        a = _np.ascontiguousarray(a)
        arrays[f"in_{name}_dram"] = a
        d[name] = nc.dram_tensor(f"in_{name}_dram", a.shape, _mybir.dt.from_np(a.dtype), kind="ExternalInput").ap()
    d["out_0_dram"] = nc.dram_tensor("out_0_dram", (1, TT * P, DM), F32, kind="ExternalOutput").ap()
    build(nc, d, const_at)
    r = _run(nc, [arrays], core_ids=[0])
    return r.results[0]["out_0_dram"]
```

```python
from contextlib import ExitStack

import concourse.bass as bass
from concourse import mybir

F32 = mybir.dt.float32
F32R = mybir.dt.float32r
I32 = mybir.dt.int32
ALU = mybir.AluOpType
ACT = mybir.ActivationFunctionType
AX = mybir.AxisListType

P = 128
DM = 1024
TT = 2
DEPTH = 2
DH = 64
NEG = -1e30
TAKEN = -3e38
TOPK = 64
LN_EPS, RMS_EPS = 1e-5, 1e-6
ALPHA = (2 * DEPTH) ** 0.25
SCALE = DH ** -0.5
NE, NG, EPG, DE = 16, 4, 4, 512

RING = 3
UNIT = 2048
HALF = UNIT // 2
AHEAD = 5

A_Q, A_C, A_IQ, A_IK, A_IW, B_Q, B_K, B_V, C_Q, C_K, C_V, N_QKV = (
    0, 256, 384, 640, 704, 708, 964, 1220, 1476, 1988, 2116, 2244)
N_GATE = 3 * DM
RB_AQ, RB_IQ, RB_IKKA, RB_BQ, RB_BK, RB_CQ, RB_CK, RB_KAIK, RB_CK2, N_RB = 0, 2, 4, 5, 7, 9, 13, 14, 15, 16

U_LAYER, U_ROUND = 22 + 4 + 4, NE * 6
G_LAYER, G_ROUND = 40, 2 * NE + 4
T_LAYER, T_ROUND = 48, 4 + 6 * NG
S_LAYER, S_ROUND = 11, NG

DFF = 2816
N_IN2 = 7184
S_Q, S_K, S_V, CONV, L_Q, L_K, L_V, L_R, L_LR, GATE2 = 0, 512, 1024, 1536, 2560, 2816, 3072, 3584, 4096, 4112
TAPS = 31
N_PROJ2 = L_LR
PROJ2_ORDER = (3, 4, 0, 1, 5, 2, 6, 7)
FB = DFF // 256
U_FFN, U_MIX2 = 3 * FB, 2 * 8 + 1 + 12 + 6 + 4
U_LAYER2 = 2 * U_FFN + U_MIX2
G_MIX2, G_LAYER2 = 48, 56
T_FFN, T_MIX2 = 4 + 2 * FB, 42
T_LAYER2 = 2 * T_FFN + T_MIX2
S_FFN, S_MIX2 = FB, 4
S_LAYER2 = 2 * S_FFN + S_MIX2
XT_LAYER2 = 22


class At:

    def __init__(self, const, *terms):
        self.const, self.terms = const, terms

    def __add__(self, k):
        return At(self.const + k, *self.terms)

    def value(self, scale=1, more=0):
        v = self.const * scale + more
        for reg, step in self.terms:
            v = reg * (step * scale) + v
        return v

    def turn(self, n):
        assert all(step % n == 0 for _, step in self.terms), (self.terms, n)
        return At(self.const // n, *[(reg, step // n) for reg, step in self.terms])

    def slot(self, n):
        return self.const % n


def plan_mixer1():
    t, s, steps = 4 + 2, 0, []

    def step(kind, n_t=0, n_s=0, **more):
        nonlocal t, s
        steps.append(dict(kind=kind, t=t, s=s, **more))
        t, s = t + n_t, s + n_s

    def gate(n, half):
        step("gate", n=n, half=half)

    groups = [(1, 0), (1, 1), (2, 0), (2, 1), (3, 0), (3, 1), (0, 0), (0, 1)]

    def scores(i):
        step("scores", n_s=1, grp=groups[i][0], tt=groups[i][1], n=i)

    def exp(i):
        step("exp", grp=groups[i][0], tt=groups[i][1], n=i)

    rounds = [tt for tt in range(TT) for _ in range(TOPK // 8)]
    gate(0, 0)
    gate(0, 1)
    for j in range(8):
        step("rt", n_t=1, j=j)
    step("index", n_s=1, tt=0)
    gate(1, 0)
    step("index", n_s=1, tt=1)
    scores(0)
    exp(0)
    gate(1, 1)
    for i, (grp, tt) in enumerate(groups):
        here = dict(grp=grp, tt=tt, n=i)
        last = i == len(groups) - 1
        if not last:
            scores(i + 1)
        if i < 5:
            step("topk", tiles=rounds[3 * i:3 * i + 3 if i < 4 else None], last=(i == 4))
        step("probs_t", n_t=1 + tt, **here)
        if not last:
            exp(i + 1)
            gate(2 + i // 2, i % 2)
        step("values", n_t=1, **here)
        if last:
            gate(2 + i // 2, i % 2)
    assert t == 4 + 2 + 8 + 12 + 8 and s == S_LAYER - 1
    return steps, t


PLAN1, T_AFTER_MIX1 = plan_mixer1()


def plan_mixer2():
    t, g, s, steps = 4 + 1 + 2 + 4, 16 + 2, 0, []
    halves = iter([(n, half) for n in range(6) for half in range(2)])
    groups = [(0, 0), (0, 1), (1, 0), (1, 1)]

    def step(kind, n_t=0, n_g=0, n_s=0, **more):
        nonlocal t, g, s
        steps.append(dict(kind=kind, t=t, g=g, s=s, **more))
        t, g, s = t + n_t, g + n_g, s + n_s

    def gate(taps=(0, 0)):
        n, half = next(halves)
        if half == 0:
            step("gate", n_g=2, n=n, half=0, taps=taps)
        else:
            first = [st["g"] for st in steps if st["kind"] == "gate" and st["n"] == n][0]
            steps.append(dict(kind="gate", t=t, g=first, s=s, n=n, half=1, taps=taps))

    for i, (grp, tt) in enumerate(groups):
        here = dict(grp=grp, tt=tt, n=i)
        before = dict(grp=groups[i - 1][0], tt=groups[i - 1][1], n=i - 1)
        step("scores", n_s=1, **here)
        if i:
            step("probs_t", n_t=1 + before["tt"], **before)
        step("soft", **here)
        step("scan", **here)
        gate()
        if i:
            step("values", n_t=1, **before)
        step("stick", **here)
        gate((20 + 3 * i, min(23 + 3 * i, TAPS)))
    step("probs_t", n_t=1 + tt, **here)
    step("alpha", n_g=2)
    step("values", n_t=1, **here)
    step("conv_back", n_t=2)
    step("alpha_end")
    gate()
    step("conv_norm")
    step("gla_q", n_t=1)
    step("decay", n_t=2)
    gate()
    step("states", n_t=4)
    gate()
    step("gla_out", n_t=2)
    gate()
    step("branches_t", n_t=4)
    assert t == 36 and g == 32 and s == S_MIX2
    return steps, t


PLAN2, T_AFTER_MIX2 = plan_mixer2()


def shape_constants():
    import numpy as np

    i = np.arange(P)
    q, k = i[:, None], i[None, :]
    causal = np.where(k <= q, 0.0, NEG)
    band = np.where(k > q, 0.0, NEG)
    earlier = np.where(k < q, 0.0, NEG)
    zero = np.zeros((P, P))
    inv = (np.float32(1.0) / (np.float32(10000.0) ** (np.arange(0, DH, 2, dtype=np.float32) / np.float32(DH)))).astype(np.float32)
    ang = np.arange(TT * P, dtype=np.float32)[:, None] * inv[None, :]
    cos, sin = np.cos(ang).astype(np.float32), np.sin(ang).astype(np.float32)
    rope = np.concatenate([cos, cos, -sin, sin], axis=1).reshape(TT, P, 4 * DH // 2)
    parts = {
        "ident": np.eye(P),
        "mask_causal": np.concatenate([zero, causal], axis=1),
        "mask_window": np.concatenate([band, causal], axis=1),
        "mask_earlier": np.concatenate([zero, earlier], axis=1),
        "rope": np.concatenate([rope[0], rope[1]], axis=1),
        "before": (q < k) * 1.0,
        "ones": np.ones((P, P)),
        "iota": np.broadcast_to(k, (P, P)),
        "first_of16": np.broadcast_to(16 - np.arange(16), (P, 16)),
        "first_of4": np.broadcast_to(4 - np.arange(4), (P, 4)),
        "later_in_chunk": ((q > k) & (q // 64 == k // 64)) * 1.0,
        "chunk_of": (q // 64 == np.arange(2)[None, :]) * 1.0,
    }
    at, n = {}, 0
    for name, a in parts.items():
        at[name] = (n, n + a.shape[1])
        n += a.shape[1]
    return np.concatenate([np.asarray(a, np.float32) for a in parts.values()], axis=1), at


def build(nc, d, const_at):
    d_const, out = d["shape_constants"], d["out_0_dram"]
    n_const = d_const.shape[1]
    with ExitStack() as ctx:
        def sb(name, shape, dt=F32, scope=ctx):
            return scope.enter_context(nc.sbuf_tensor(name, shape, dt))

        def sem(name):
            return ctx.enter_context(nc.semaphore(name))

        g_bank = [ctx.enter_context(nc.psum_tensor(f"g_bank{i}", [P, 512], F32)) for i in range(4)]
        t_bank = [ctx.enter_context(nc.psum_tensor(f"t_bank{i}", [P, 512], F32)) for i in range(2)]
        s_bank = ctx.enter_context(nc.psum_tensor("s_bank", [P, 1024], F32))

        const = sb("const", [P, n_const])
        w_raw = sb("w_raw", [P, RING, UNIT])
        w_hi = sb("w_hi", [P, RING, UNIT], F32R)
        w_lo = sb("w_lo", [P, RING, UNIT], F32R)
        x = sb("x_res", [P, TT, DM])
        xt_hi = sb("xt_hi", [P, 12, TT * P], F32R)
        xt_lo = sb("xt_lo", [P, 12, TT * P], F32R)
        gains = sb("gains", [P, 2, DM])
        stats = sb("stats", [P, TT, 12])
        mean_var = sb("mean_var", [P, TT, 2])
        rstd = sb("rstd", [P, TT])
        rstd_in = sb("rstd_in", [P, TT])
        rstd_half = sb("rstd_half", [P, TT])
        mean_sq = sb("mean_sq", [P, TT, 2])
        w_ukv = sb("w_ukv", [P, 2 * DH])
        sinks = sb("sinks", [P, 8])
        w_router = sb("w_router", [P, 8, NE])
        wr_hi = sb("wr_hi", [P, 8, NE], F32R)
        wr_lo = sb("wr_lo", [P, 8, NE], F32R)
        b_router = sb("b_router", [P, NE])

        def c(name, a=0, b=None):
            lo, hi = const_at[name]
            return const[:, lo + a:(hi if b is None else lo + b)]

        ident = c("ident")

        mix1 = ctx.enter_context(ExitStack())
        qkv = sb("qkv", [P, TT, N_QKV], scope=mix1)
        gate = sb("gate", [P, TT, N_GATE], scope=mix1)
        rot = sb("rot", [P, TT, 2048], scope=mix1)
        rot_t = sb("rot_t", [P, N_RB, TT * P], scope=mix1)
        kv_lat = sb("kv_lat", [P, TT, 2 * DH], scope=mix1)
        top8 = sb("top8", [P, 8], scope=mix1)
        chosen = sb("chosen", [P, TT, 256], scope=mix1)
        masked = sb("masked", [P, 2, 1024], scope=mix1)
        probs = masked
        relu_dots = masked[:, 0, :].rearrange("p (h k) -> p h k", h=4)
        rope_tmp = masked[:, :, 0:10 * DH].rearrange("p t (h d) -> p t h d", d=DH)
        gated = masked[:, :, 0:512]
        probs_t = rot[:, :, DM:DM + 512].rearrange("p k (h q) -> p k h q", h=4)
        lat_t = chosen[:, :, 0:P]
        row_max = sb("row_max", [P, 2, 4], scope=mix1)
        neg_max = sb("neg_max", [P, 2, 4], scope=mix1)
        row_sum = sb("row_sum", [P, 2, 4], scope=mix1)
        sink_exp = sb("sink_exp", [P, 2, 4], scope=mix1)
        inv_sum = sb("inv_sum", [P, 2, 4], scope=mix1)
        attn = rot[:, :, 0:DM]
        merged = rot[:, :, DM:2 * DM]
        mix1.close()

        moe = ctx.enter_context(ExitStack())
        router_t = sb("router_t", [NE, TT * P], scope=moe)
        aff = sb("aff", [P, TT, NE], scope=moe)
        sel = sb("sel", [P, TT, NE], scope=moe)
        pair = sb("pair", [P, TT * NG, 6], scope=moe)
        grp_score = sb("grp_score", [P, TT, NG], scope=moe)
        in_grp = sb("in_grp", [P, TT, NG], scope=moe)
        key = sb("key", [P, TT, NE], scope=moe)
        best = sb("best", [P, TT], scope=moe)
        hot1 = sb("hot1", [P, TT, NE], scope=moe)
        hot2 = sb("hot2", [P, TT, NE], scope=moe)
        comb = sb("comb", [P, TT, NE], scope=moe)
        place = sb("place", [P, TT, NG], scope=moe)
        n_grp = sb("n_grp", [P, NG], scope=moe)
        rounds_f = sb("rounds_f", [P, 1], scope=moe)
        rounds_i = sb("rounds_i", [P, 1], I32, scope=moe)
        onehot = sb("onehot", [P, TT, NG, P], scope=moe)
        onehot_t = sb("onehot_t", [P, TT, NG, P], F32R, scope=moe)
        comb_slot = sb("comb_slot", [P, NE], scope=moe)
        xg_hi = sb("xg_hi", [P, 8, P], F32R, scope=moe)
        xg_lo = sb("xg_lo", [P, 8, P], F32R, scope=moe)
        silu_g = sb("silu_g", [P, 2, DE], scope=moe)
        hid = sb("hid", [P, 2, DE], scope=moe)
        hid_t_hi = sb("hid_t_hi", [P, 2, 4, P], F32R, scope=moe)
        hid_t_lo = sb("hid_t_lo", [P, 2, 4, P], F32R, scope=moe)
        y_hi = sb("y_hi", [P, NG, DM], F32R, scope=moe)
        y_lo = sb("y_lo", [P, NG, DM], F32R, scope=moe)
        acc = sb("acc", [P, TT, DM], scope=moe)
        moe.close()

        ffn = ctx.enter_context(ExitStack())
        ffn_y = sb("ffn_y", [P, TT, DM], scope=ffn)
        ffn_junk = sb("ffn_junk", [P, DM], scope=ffn)
        ffn_silu = sb("ffn_silu", [P, TT, 256], scope=ffn)
        ffn_hid = sb("ffn_hid", [P, TT, 256], scope=ffn)
        ffn_t_hi = sb("ffn_t_hi", [P, 2, TT * P], F32R, scope=ffn)
        ffn_t_lo = sb("ffn_t_lo", [P, 2, TT * P], F32R, scope=ffn)
        ffn.close()

        mix2 = ctx.enter_context(ExitStack())
        proj = sb("proj", [P, TT, N_PROJ2], scope=mix2)
        gate2 = sb("gate2", [P, TT, N_GATE], scope=mix2)
        qk_t = sb("qk_t", [P, 8, TT * P], scope=mix2)
        logit = sb("logit", [P, 4, 256], scope=mix2)
        soft = sb("soft", [P, 4, 256], scope=mix2)
        probs_t2 = sb("probs_t2", [P, 2, 4, P], scope=mix2)
        conv_in = sb("conv_in", [P, 4, TAPS - 1 + TT * P], scope=mix2)
        conv_y = sb("conv_y", [P, 4, TT * P], scope=mix2)
        taps = sb("taps", [P, 4, 32], scope=mix2)
        lam = sb("lam", [P, 8], scope=mix2)
        mean_sq8 = sb("mean_sq8", [P, TT, 4], scope=mix2)
        mix_y = gate2[:, :, 0:DM]
        mix_junk = proj[:, 0, 0:DM]
        gla_gain = proj[:, 0, CONV + 512:CONV + 1024]
        b_alpha = proj[:, 1, CONV + 512:CONV + 768]
        w_alpha = proj[0:16, 1, CONV + 768:CONV + 1024]
        conv_row = gains[:, 1, :]
        flat = "p a b -> p (a b)"
        taps_raw = probs_t2[0:32, 0, :, :].rearrange(flat)
        state = qk_t[:, :, :].rearrange("p (c h) n -> p c h n", c=4)
        k_dec = logit[:, :, :].rearrange("p (t c) n -> p t c n", t=TT)
        logits = (logit[:, :, :].rearrange("p (t a) n -> p t a n", t=2),
                  proj[:, :, CONV:CONV + 512].rearrange("p t (a n) -> p t a n", a=2))
        soft_heads = soft[:, :, :].rearrange("p (t a) n -> p t a n", t=2)
        log_alpha = soft[:, 0:2, :]
        decay = soft[:, 2:4, :]
        log_tmp = logit[:, 0:2, :].rearrange(flat)
        kv_new = probs_t2[:, 1, :, :].rearrange(flat)
        lin_qt = conv_in[:, :, :].rearrange(flat)[:, 0:512].rearrange("p (h n) -> p h n", h=2)
        lr_t = sb("lr_t", [16, TT * P], scope=mix2)
        gla_o = conv_y[:, :, :].rearrange("p (t a) n -> p t (a n)", t=TT)
        merged2 = proj[:, :, 512:512 + DM]
        conv_tmp = (w_ukv[:, :], w_router[:, :, :].rearrange("p a b -> p (a b)"))
        ATTN2 = (0, 1536, 2048)
        mix2.close()

        const_in, x_in, small_in, gains_in, router_in, x_out = (
            sem(n) for n in ("const_in", "x_in", "small_in", "gains_in", "router_in", "x_out"))
        landed = [sem(f"landed{i}") for i in range(2 * RING)]
        fences = {e: sem(f"fence_{i}") for i, e in enumerate(
            (nc.sync.engine, nc.scalar.engine, nc.vector.engine, nc.tensor.engine, nc.gpsimd.engine))}
        credits = sem("credits")
        hi_ready, lo_ready, w_used = sem("hi_ready"), sem("lo_ready"), sem("w_used")
        g_free = [sem(f"g_free{i}") for i in range(4)]
        t_ready, s_ready, s_free = sem("t_ready"), sem("s_ready"), sem("s_free")
        t_free = [sem(f"t_free{i}") for i in range(2)]
        xt_hi_ready, xt_ready, x_ready = sem("xt_hi_ready"), sem("xt_ready"), sem("x_ready")
        qkv_ready, lat_t_ready, kv_lat_ready, rot_ready, rot_t_ready = (
            sem(n) for n in ("qkv_ready", "lat_t_ready", "kv_lat_ready", "rot_ready", "rot_t_ready"))
        kv_lat_done, returned = sem("kv_lat_done"), sem("returned")
        relu_ready, chosen_ready, max_ready, probs_ready, probs_t_ready, attn_ready = (
            sem(n) for n in ("relu_ready", "chosen_ready", "max_ready", "probs_ready", "probs_t_ready", "attn_ready"))
        gate_ready, merged_ready, var_ready, rstd_ready = (
            sem(n) for n in ("gate_ready", "merged_ready", "var_ready", "rstd_ready"))
        router_split, aff_ready, in_grp_ready, rounds_ready, onehot_ready, onehot_t_ready, comb_slot_ready = (
            sem(n) for n in ("router_split", "aff_ready", "in_grp_ready", "rounds_ready", "onehot_ready",
                             "onehot_t_ready", "comb_slot_ready"))
        xg_hi_ready, xg_ready, silu_ready, hid_ready, hid_hi_ready, hid_t_ready, y_hi_ready, y_ready = (
            sem(n) for n in ("xg_hi_ready", "xg_ready", "silu_ready", "hid_ready", "hid_hi_ready", "hid_t_ready",
                             "y_hi_ready", "y_ready"))

        (square_ready, normed_ready, up_silu_ready, ffn_hid_ready, ffn_hi_ready, ffn_t_ready, proj_ready, conv_u_ready,
         conv_in_ready, taps_ready, qk_t_ready, logit_ready, soft_ready, log_w_ready, stick_ready, probs_t2_ready,
         branch_ready, conv_y_ready, conv_mid_ready, lr_t_ready, alpha_in_ready, alpha_soft_ready, log_alpha_ready,
         gla_q_ready, decay_ready, k_dec_ready, state_ready, merged2_ready, gate2_ready, pad_ready, mixer_in, alpha_in) = (
            sem(n) for n in (
                "square_ready", "normed_ready", "up_silu_ready", "ffn_hid_ready", "ffn_hi_ready", "ffn_t_ready",
                "proj_ready", "conv_u_ready", "conv_in_ready", "taps_ready", "qk_t_ready", "logit_ready", "soft_ready",
                "log_w_ready", "stick_ready", "probs_t2_ready", "branch_ready", "conv_y_ready", "conv_mid_ready",
                "lr_t_ready", "alpha_in_ready", "alpha_soft_ready", "log_alpha_ready", "gla_q_ready", "decay_ready",
                "k_dec_ready", "state_ready", "merged2_ready", "gate2_ready", "pad_ready", "mixer_in", "alpha_in"))
        pre_in, post_in, gla_ready, row_ready = sem("pre_in"), sem("post_in"), sem("gla_ready"), sem("row_ready")
        router_t_ready, comb_ready = sem("router_t_ready"), sem("comb_ready")

        def half_slot(u, h):
            return (2 * u.const + h) % (2 * RING)

        def half_of(ring, u, h):
            hs = half_slot(u, h)
            return ring[:, hs // 2, (hs % 2) * HALF:(hs % 2 + 1) * HALF]

        def unit_is_used(eng, u):
            eng.wait_ge(w_used, u.value(2, 2 * RING + 2))

        def half_is_split(u, h):
            nc.tensor.wait_ge(lo_ready, u.value(2, 2 * RING + 1 + h))

        def split_hi(u, h):
            place = u + h // 2
            nc.scalar.wait_ge(w_used, u.value(2, 1 + h))
            nc.scalar.wait_ge(landed[half_slot(u, h)], place.turn(RING).value(32, 32))
            nc.scalar.activation(half_of(w_hi, u, h), half_of(w_raw, u, h), ACT.Copy).then_inc(hi_ready, 1)

        def split_lo(u, h):
            nc.vector.wait_ge(hi_ready, u.value(2, 1 + h))
            nc.vector.tensor_tensor(half_of(w_lo, u, h), half_of(w_raw, u, h), half_of(w_hi, u, h).bitcast(F32),
                                    ALU.subtract).then_inc(lo_ready, 1)

        def ahead_of(split):
            def ahead(u, k=0):
                split(u, 2 * k + AHEAD)
                split(u, 2 * k + AHEAD + 1)
            return ahead

        def mm3(dst, a_hi, a_lo, b_hi, b_lo, first, last):
            nc.tensor.matmul(dst, a_hi, b_hi, start=first, stop=False)
            nc.tensor.matmul(dst, a_hi, b_lo, start=False, stop=False)
            return nc.tensor.matmul(dst, a_lo, b_hi, start=False, stop=last)

        def g_wait(f):
            nc.tensor.wait_ge(g_free[f.slot(4)], f.turn(4).value(1, 1))
            return g_bank[f.slot(4)]

        def t_wait(t):
            nc.tensor.wait_ge(t_free[t.slot(2)], t.turn(2).value(1, 1))
            return t_bank[t.slot(2)]

        def pe_block(u, f, n=512, halves=(0, 1)):
            for half in halves:
                uu = u + half
                s = uu.slot(RING)
                for h in range(2):
                    half_is_split(uu, h)
                    for tt in range(TT):
                        bank = g_bank[(f + tt).slot(4)] if half or h else g_wait(f + tt)
                        for k in (2 * h, 2 * h + 1):
                            kk = half * 4 + k
                            last = mm3(bank[:, 0:n], xt_hi[:, kk, tt * P:(tt + 1) * P], xt_lo[:, kk, tt * P:(tt + 1) * P],
                                       w_hi[:, s, k * 512:k * 512 + n], w_lo[:, s, k * 512:k * 512 + n],
                                       kk == 0, kk == 7)
                    last.then_inc(w_used, 1)

        def xt_batches(tts, quads):
            return [(tt, kq) for tt in tts for kq in quads]

        def pe_xt(src, t, quads, ready):
            for i in range(TT * quads):
                tt, kq = divmod(i, quads)
                if kq == 0:
                    ready(nc.tensor, tt)
                bank = t_wait(t + i)
                for j in range(4):
                    last = nc.tensor.transpose(bank[:, j * P:(j + 1) * P], src[:, tt, (4 * kq + j) * P:(4 * kq + j + 1) * P], ident)
                last.then_inc(t_ready, 1)

        def act_xt(t, quads, batches=None):
            for i, (tt, kq) in enumerate(batches or xt_batches(range(TT), range(quads))):
                nc.scalar.wait_ge(t_ready, (t + i).value(1, 1))
                nc.scalar.activation(xt_hi[:, 4 * kq:4 * kq + 4, tt * P:(tt + 1) * P],
                                     t_bank[(t + i).slot(2)][:, :].rearrange("p (a b) -> p a b", a=4),
                                     ACT.Copy).then_inc(xt_hi_ready, 1)

        def dve_xt(t, n, quads, batches=None):
            for i, (tt, kq) in enumerate(batches or xt_batches(range(TT), range(quads))):
                nc.vector.wait_ge(xt_hi_ready, (n + i).value(1, 1))
                nc.vector.tensor_tensor(xt_lo[:, 4 * kq:4 * kq + 4, tt * P:(tt + 1) * P],
                                        t_bank[(t + i).slot(2)][:, :].rearrange("p (a b) -> p a b", a=4),
                                        xt_hi[:, 4 * kq:4 * kq + 4, tt * P:(tt + 1) * P].bitcast(F32),
                                        ALU.subtract).then_inc(t_free[(t + i).slot(2)], 1)
            nc.vector.drain().then_inc(xt_ready, 1)

        EARLY_BRANCHES = [(tt, br) for br in (0, 1) for tt in range(TT)]
        LAST_BRANCH = [(tt, 2) for tt in range(TT)]

        def row_stats(src, tt, half):
            nc.vector.drain()
            nc.vector.bn_stats(stats[:, tt, half * 6:half * 6 + 6], src[:, tt, half * 512:half * 512 + 512])

        def layer_norm(src, dst, norm, gain, bias, gains_at, times=1):
            dve = nc.vector
            dve.drain()
            for tt in range(TT):
                dve.bn_aggr(mean_var[:, tt, :], stats[:, tt, :])
            dve.drain()
            dve.tensor_scalar(mean_var[:, :, 1:2], mean_var[:, :, 1:2], LN_EPS * times ** 2, None, ALU.add)
            dve.drain()
            dve.reciprocal(rstd[:, :], mean_var[:, :, 1:2].rearrange("p a b -> p (a b)")).then_inc(var_ready, 1)
            dve.wait_ge(rstd_ready, norm.value(1, 1))
            dve.wait_ge(gains_in, gains_at)
            for tt in range(TT):
                dve.tensor_scalar(dst[:, tt, :], src[:, tt, :], mean_var[:, tt, 0:1], rstd[:, tt:tt + 1],
                                  ALU.subtract, ALU.mult)
            dve.drain()
            for tt in range(TT):
                dve.tensor_tensor(dst[:, tt, :], dst[:, tt, :], gain, ALU.mult)
                dve.drain()
                dve.tensor_tensor(dst[:, tt, :], dst[:, tt, :], bias, ALU.add).then_inc(row_ready, 1)
            dve.drain().then_inc(x_ready, 1)

        def act_root(norm):
            nc.scalar.wait_ge(var_ready, norm.value(1, 1))
            nc.scalar.activation(rstd[:, :], rstd[:, :], ACT.Sqrt).then_inc(rstd_ready, 1)

        def layer1(l, rho):
            return dict(u=At(0, (l, U_LAYER), (rho, U_ROUND)), g=At(0, (l, G_LAYER), (rho, G_ROUND)),
                        t=At(0, (l, T_LAYER), (rho, T_ROUND)), s=At(0, (l, S_LAYER), (rho, S_ROUND)))

        def s_half(half, kn):
            return s_bank[:, 512 * half:512 * half + 2 * kn].rearrange("p (i k) -> p i k", i=2)

        def layer2(l, rho):
            def at(consts, per):
                return At(DEPTH * consts[0], (rho, consts[1]), (l, per))

            first = dict(u=at((U_LAYER, U_ROUND), U_LAYER2), g=at((G_LAYER, G_ROUND), G_LAYER2),
                         t=at((T_LAYER, T_ROUND), T_LAYER2), s=at((S_LAYER, S_ROUND), S_LAYER2))
            mixer = dict(u=first["u"] + U_FFN, g=first["g"] + 4, t=first["t"] + T_FFN, s=first["s"] + S_FFN)
            second = dict(u=mixer["u"] + U_MIX2, g=mixer["g"] + G_MIX2, t=mixer["t"] + T_MIX2, s=mixer["s"] + S_MIX2)
            return first, mixer, second

        def ffn_fills(f):
            return [[f + (2 * tt + nb) for nb in range(2)] for tt in range(TT)]

        def mix_fills(f):
            return [[f + (44 + 2 * nb + tt) for nb in range(2)] for tt in range(TT)]

        def fence(eng):
            eng.sem_inc(fences[eng.engine], 1)

        def in_round(l, rho):
            at = layer1(l, rho)
            return dict(u=at["u"] + U_LAYER, g=at["g"] + G_LAYER, t=at["t"] + T_LAYER, s=at["s"] + S_LAYER)

        def group_steps(part):
            if part == "start":
                return [("gather", 0), ("slots", 0), ("gate", 0), ("up", 0)]
            steps = []
            for e in range(1, EPG + 1 if part == "group" else EPG):
                steps += [("gate", e), ("hid_t", e - 1), ("up", e)]
                if e == EPG - 1 and part == "group":
                    steps.append(("gather", 0))
                steps.append(("down", e - 1))
            if part == "last":
                steps[-1:] = [("down", EPG - 2, 0), ("hid_t", EPG - 1), ("down", EPG - 2, 1), ("down", EPG - 1)]
            return steps + [("back", 0)]

        def plus(a, c, g, step):
            return a + (c + g * step) if isinstance(g, int) else At(a.const + c, *a.terms, (g, step))

        def walk(part, at_r, g):
            later = part != "start"
            u, t = plus(at_r["u"], 4 * later, g, 24), plus(at_r["t"], 6 * later, g, 6)
            for kind, e, *halves in group_steps(part):
                if kind in ("gate", "up", "down"):
                    for half in halves or range(2):
                        yield kind, e, half, u
                        u = u + 1
                else:
                    yield kind, e, None, t
                    t = t + {"gather": 2, "slots": 4, "hid_t": 1, "back": 0}[kind]

        def all_parts(eng, run):
            run("start", 0)
            with eng.Fori(0, NG - 1) as g:
                run("group", g)
            run("last", NG - 1)

        def expert_fill(at_r, kind, g, e):
            return plus(at_r["g"], 2 * e + (kind == "up"), g, 8)

        def rounds_of(eng, value):
            eng.wait_ge(rounds_ready, value)
            fence(eng)
            return eng.value_load(rounds_i[0:1, 0:1], min_val=1, max_val=2)

        block = ctx.enter_context(nc.Block())

        @block.sync
        def _(sp):
            sp.dma_start(const[:, :], d_const).then_inc(const_in, 16)
            sp.dma_start(x[:, :, :], d["x"].rearrange("a (t p) n -> p (a t) n", p=P)).then_inc(x_in, 16)

            def load(u, src, n=512, k=4):
                s = u.slot(RING)
                dst = w_raw[:, s, :].rearrange("p (k n) -> p k n", k=k)[:, :, 0:n]
                for h in range(2):
                    sp.wait_ge(lo_ready, u.value(2, 1 + h))
                    fence(sp)
                    a = h * (k // 2)
                    hs = half_slot(u, h)
                    sp.dma_start(dst[:, a:a + k // 2, :], src[:, a:a + k // 2, :]).then_inc(landed[hs], 16)
                    sp.sem_inc(landed[hs], 16)

            def rows(w, l, k0, n0, n=512, k=4):
                return w[bass.ds(l, 1), k0 * P:(k0 + k) * P, n0:n0 + n].rearrange("a (k p) n -> p (a k) n", p=P)

            rho = sp.alloc_register("rounds_done_sp")
            sp.reg_mov(rho, 0)
            with sp.Fori(0, DEPTH) as l:
                done = sp.snap(rho, min_val=0, max_val=4)
                at = layer1(l, done)
                u = at["u"]
                for blk in range(5):
                    n = min(512, N_QKV - blk * 512)
                    for half in range(2):
                        load(u + (2 * blk + half), rows(d["w_in"], l, 4 * half, blk * 512, n), n)
                for blk in range(6):
                    for half in range(2):
                        load(u + (10 + 2 * blk + half), rows(d["w_in"], l, 4 * half, N_QKV + blk * 512))
                for i, w in ((22, "w_branch"), (26, "w_o")):
                    for blk in range(2):
                        for half in range(2):
                            load(u + (i + 2 * blk + half), rows(d[w], l, 4 * half, blk * 512))
                def round_of_experts(rnd):
                    at_r = in_round(l, rnd)

                    def expert(u, what, ex):
                        src = d[f"moe_w_{what}"].rearrange("l e k n -> (l e) k n")
                        rows_, n, k = (256, DM, 2) if what == "down" else (512, DE, 4)
                        for half in range(2):
                            load(u + half, src[bass.ds(ex, 1), half * rows_:(half + 1) * rows_, :]
                                 .rearrange("a (k p) n -> p (a k) n", p=P), n, k)

                    u = at_r["u"]
                    expert(u, "gate", l * NE)
                    expert(u + 2, "up", l * NE)
                    with sp.Fori(1, NE) as e:
                        ue = At(u.const - 2, *u.terms, (e, 6))
                        expert(ue, "gate", l * NE + e)
                        expert(ue + 2, "up", l * NE + e)
                        expert(ue + 4, "down", l * NE + e - 1)
                    expert(u + (U_ROUND - 2), "down", l * NE + (NE - 1))

                round_of_experts(done)
                R = rounds_of(sp, l + 1)
                with sp.If(R > 1):
                    round_of_experts(done + 1)
                sp.reg_add(rho, rho, R)
            done = sp.snap(rho, min_val=0, max_val=4)
            with sp.Fori(0, DEPTH) as l:
                first, mixer, second = layer2(l, done)

                def gate_up(u, w, j):
                    for h in range(4):
                        sp.wait_ge(lo_ready, u.value(2, 1 + h))
                        fence(sp)
                        for i, name in enumerate(("gate", "up")):
                            src = d[f"{w}_w_{name}_2"][bass.ds(l, 1), h * 256:(h + 1) * 256, bass.ds(j * 256, 256)]
                            sp.dma_start(half_of(w_raw, u, h).rearrange("p (k n) -> p k n", k=2)[:, :, i * 256:(i + 1) * 256],
                                         src.rearrange("a (k p) n -> p (a k) n", p=P)).then_inc(landed[half_slot(u, h)], 16)

                def down(u, w, j):
                    src = d[f"{w}_w_down_2"][bass.ds(l, 1), bass.ds(j * 256, 256), :]
                    load(u, src.rearrange("a (k p) n -> p (a k) n", p=P), DM, 2)

                def feed_forward(u, w):
                    gate_up(u, w, 0)
                    gate_up(u + 2, w, 1)
                    down(u + 4, w, 0)
                    with sp.Fori(2, FB) as j:
                        uj = At(u.const - 1, *u.terms, (j, 3))
                        gate_up(uj, w, j)
                        down(uj + 2, w, j - 1)
                    down(u + (U_FFN - 1), w, FB - 1)

                feed_forward(first["u"], "ffn1")
                u = mixer["u"]
                for i, blk in enumerate(PROJ2_ORDER):
                    for half in range(2):
                        load(u + (2 * i + half), rows(d["w_in_2"], l, 4 * half, blk * 512))
                load(u + 16, rows(d["w_in_2"], l, 0, L_LR, 16, 8), 16, 8)
                for blk in range(6):
                    for half in range(2):
                        load(u + (17 + 2 * blk + half), rows(d["w_in_2"], l, 4 * half, GATE2 + blk * 512))
                for blk in range(2):
                    for br in range(3):
                        src = d["w_branch_2"][bass.ds(l, 1), br, :, blk * 512:(blk + 1) * 512]
                        load(u + (29 + 3 * blk + br), src.rearrange("a (k p) n -> p (a k) n", p=P))
                for blk in range(2):
                    for half in range(2):
                        load(u + (35 + 2 * blk + half), rows(d["w_out_2"], l, 4 * half, blk * 512))
                feed_forward(second["u"], "ffn2")
            end = layer2(DEPTH, done)[0]["u"]
            for h in range(AHEAD):
                sp.wait_ge(lo_ready, end.value(2, 1 + h))
                sp.sem_inc(landed[half_slot(end, h)], 32)
            sp.wait_ge(x_ready, 2 * DEPTH + 1 + 3 * DEPTH)
            sp.dma_start(out.rearrange("a (t p) n -> p (a t) n", p=P), x[:, :, :]).then_inc(x_out, 16)
            sp.wait_ge(x_out, 16)

        @block.gpsimd
        def _(pool):
            pool.dma_start(w_router[:, :, :], d["router_w"].rearrange("(k p) n -> p k n", p=P)).then_inc(router_in, 16)
            pool.dma_start(b_router[:, :], d["router_b"].rearrange("(a n) -> a n", a=1).to_broadcast([P, NE])).then_inc(router_in, 16)
            pool.wait_ge(credits, 3)
            with pool.Fori(0, DEPTH) as l:
                pool.wait_ge(x_ready, 2 * l + 1)
                fence(pool)
                for i, w in enumerate(("ln1_g", "ln1_b")):
                    pool.dma_start(gains[:, i, :], d[w][bass.ds(l, 1), :].to_broadcast([P, DM])).then_inc(gains_in, 16)
                pool.dma_start(sinks[:, :], d["c_sinks"][bass.ds(l, 1), :].to_broadcast([P, 8])).then_inc(small_in, 16)
                for i, w in enumerate(("a_w_uk", "a_w_uv")):
                    pool.dma_start(w_ukv[:, i * DH:(i + 1) * DH], d[w][bass.ds(l, 1), :, :].rearrange("a p n -> p (a n)")).then_inc(small_in, 16)
                pool.wait_ge(x_ready, 2 * l + 2)
                fence(pool)
                for i, w in enumerate(("ln2_g", "ln2_b")):
                    pool.dma_start(gains[:, i, :], d[w][bass.ds(l, 1), :].to_broadcast([P, DM])).then_inc(gains_in, 16)

            with pool.Fori(0, DEPTH) as l:
                for i in range(3):
                    pool.wait_ge(normed_ready, 6 * l + (2 * i + 1))
                    if i == 0:
                        pool.wait_ge(x_ready, 2 * DEPTH + 1)
                    fence(pool)
                    pool.dma_start(gains[:, 0, :], d["norm_pre_2"][bass.ds(l, 1), i, :].to_broadcast([P, DM])).then_inc(pre_in, 16)
                    pool.wait_ge(x_ready, 3 * l + (2 * DEPTH + 1 + i))
                    fence(pool)
                    if i == 1:
                        pool.wait_ge(normed_ready, 6 * l + 5)
                        fence(pool)
                        pool.memset(conv_in[:, :, 0:TAPS - 1], 0.0).then_inc(pad_ready, 1)
                        for j, w in enumerate(("conv_ln_g_2", "conv_ln_b_2")):
                            pool.dma_start(conv_row[:, j * 512:(j + 1) * 512],
                                           d[w][bass.ds(l, 1), :].to_broadcast([P, 512])).then_inc(mixer_in, 16)
                        pool.dma_start(taps_raw[0:TAPS, :], d["conv_w_2"][bass.ds(l, 1), :, :].rearrange("a t n -> (a t) n")).then_inc(mixer_in, 16)
                        pool.dma_start(taps_raw[TAPS:TAPS + 1, :], d["conv_b_2"][bass.ds(l, 1), :]).then_inc(mixer_in, 16)
                        pool.wait_ge(conv_u_ready, l + 1)
                        fence(pool)
                        pool.dma_start(gla_gain, d["gla_norm_g_2"][bass.ds(l, 1), :].to_broadcast([P, 512])).then_inc(alpha_in, 16)
                        pool.dma_start(b_alpha, d["gla_b_alpha_2"][bass.ds(l, 1), :].to_broadcast([P, 256])).then_inc(alpha_in, 16)
                        pool.dma_start(w_alpha, d["gla_w_alpha_2"][bass.ds(l, 1), :, :].rearrange("a t n -> (a t) n")).then_inc(alpha_in, 16)
                        pool.wait_ge(conv_in_ready, l + 1)
                        fence(pool)
                        y_ = conv_y[:, 3, :]
                        for k in range(TAPS):
                            src = conv_in[:, 3, k:k + TT * P]
                            if k == 0:
                                pool.tensor_scalar(y_, src, taps[:, 3, 0:1], taps[:, 3, TAPS:TAPS + 1], ALU.mult, ALU.add)
                            else:
                                pool.drain()
                                for tt in range(TT):
                                    pool.tensor_scalar(conv_tmp[tt], src[:, tt * P:(tt + 1) * P], taps[:, 3, k:k + 1], None, ALU.mult)
                                pool.drain()
                                for tt in range(TT):
                                    part = y_[:, tt * P:(tt + 1) * P]
                                    pool.tensor_tensor(part, part, conv_tmp[tt], ALU.add)
                        pool.drain()
                        pool.sem_inc(conv_y_ready, 1)
                        pool.wait_ge(conv_mid_ready, l + 1)
                        fence(pool)
                    pool.dma_start(gains[:, 1, :], d["norm_post_2"][bass.ds(l, 1), i, :].to_broadcast([P, DM])).then_inc(post_in, 16)

        @block.scalar
        def _(act):
            act.wait_ge(const_in, 16)
            act.wait_ge(router_in, 32)
            act.wait_ge(credits, 3)
            act.activation(wr_hi[:, :, :], w_router[:, :, :], ACT.Copy).then_inc(router_split, 1)

            ahead = ahead_of(split_hi)
            for h in range(AHEAD):
                split_hi(At(0), h)

            def experts(at_r, rnd):
                def run(part, g):
                    count = plus(At(0, (rnd, 16)), 0, g, 4)
                    for what, e, half, place in walk(part, at_r, g):
                        if half is not None:
                            ahead(place)
                            if what == "gate" and half == 1:
                                b = expert_fill(at_r, what, g, e).slot(4)
                                unit_is_used(act, place)
                                act.wait_ge(hid_ready, count.value(1, 1 + e))
                                act.activation(silu_g[:, e % 2, :], g_bank[b][:, :], ACT.Silu).then_inc(g_free[b], 1)
                                act.drain().then_inc(silu_ready, 1)
                        elif what == "gather":
                            for i in range(2):
                                act.wait_ge(t_ready, (place + i).value(1, 1))
                                act.activation(xg_hi[:, 4 * i:4 * i + 4, :], t_bank[(place + i).slot(2)][:, :].rearrange("p (a b) -> p a b", a=4),
                                               ACT.Copy).then_inc(xg_hi_ready, 1)
                        elif what == "slots":
                            for tt in range(TT):
                                tf = place + tt
                                act.wait_ge(t_ready, tf.value(1, 1))
                                act.activation(onehot_t[:, tt, :, :], t_bank[tf.slot(2)][:, :].rearrange("p (a b) -> p a b", a=NG),
                                               ACT.Copy).then_inc(t_free[tf.slot(2)], 1)
                            for i in range(2):
                                tf = place + (2 + i)
                                act.wait_ge(t_ready, tf.value(1, 1))
                                act.activation(comb_slot[:, 8 * i:8 * i + 8], t_bank[tf.slot(2)][:, 0:8], ACT.Copy).then_inc(t_free[tf.slot(2)], 1)
                            act.drain().then_inc(comb_slot_ready, 1)
                        elif what == "hid_t":
                            act.wait_ge(t_ready, place.value(1, 1))
                            act.activation(hid_t_hi[:, e % 2, :, :], t_bank[place.slot(2)][:, :].rearrange("p (a b) -> p a b", a=4),
                                           ACT.Copy).then_inc(hid_hi_ready, 1)
                        else:
                            act.wait_ge(s_ready, plus(at_r["s"], 0, g, 1).value(1, 1))
                            act.activation(y_hi[:, bass.ds(g, 1), :], s_bank[:, :].unsqueeze(1), ACT.Copy).then_inc(y_hi_ready, 1)

                all_parts(act, run)

            rho = act.alloc_register("rounds_done_act")
            act.reg_mov(rho, 0)
            with act.Fori(0, DEPTH) as l:
                done = act.snap(rho, min_val=0, max_val=4)
                at = layer1(l, done)
                u, f, t = at["u"], at["g"], at["t"]
                act_xt(t, 2)
                for blk in range(5):
                    n = min(512, N_QKV - blk * 512)
                    ahead(u, 2 * blk)
                    ahead(u, 2 * blk + 1)
                    unit_is_used(act, u + (2 * blk + 1))
                    for tt in range(TT):
                        b = (f + (2 * blk + tt)).slot(4)
                        act.activation(qkv[:, tt, blk * 512:blk * 512 + n], g_bank[b][:, 0:n], ACT.Copy).then_inc(g_free[b], 1)
                    act.drain().then_inc(qkv_ready, 1)
                    if blk == 0:
                        for tt in range(TT):
                            act.wait_ge(t_ready, (t + (4 + tt)).value(1, 1))
                            act.activation(lat_t[:, tt, :], t_bank[tt][:, 0:P], ACT.Copy).then_inc(t_free[tt], 1)
                        act.drain().then_inc(lat_t_ready, 1)
                    if blk == 4:
                        act.wait_ge(kv_lat_done, l + 1)
                        for tt in range(TT):
                            b = (f + (10 + tt)).slot(4)
                            act.activation(kv_lat[:, tt, :], g_bank[b][:, 0:P], ACT.Copy).then_inc(g_free[b], 1)
                        act.drain().then_inc(kv_lat_ready, 1)
                for st in PLAN1:
                    kind = st["kind"]
                    if kind == "rt":
                        tf = t + st["t"]
                        act.wait_ge(t_ready, tf.value(1, 1))
                        act.activation(rot_t[:, 2 * st["j"]:2 * st["j"] + 2, :],
                                       t_bank[tf.slot(2)][:, :].rearrange("p (a b) -> p a b", a=2), ACT.Copy).then_inc(t_free[tf.slot(2)], 1)
                        if st["j"] == 7:
                            act.drain().then_inc(rot_t_ready, 1)
                    elif kind == "gate":
                        n, half = st["n"], st["half"]
                        k = 10 + 2 * n + half
                        ahead(u, k)
                        if half:
                            unit_is_used(act, u + k)
                            for tt in range(TT):
                                b = (f + (12 + 2 * n + tt)).slot(4)
                                act.activation(gate[:, tt, n * 512:(n + 1) * 512], g_bank[b][:, :], ACT.Tanh, scale=0.5).then_inc(g_free[b], 1)
                            act.drain().then_inc(gate_ready, 1)
                    elif kind == "index":
                        kn = P * (1 + st["tt"])
                        act.wait_ge(s_ready, (at["s"] + st["s"]).value(1, 1))
                        if st["tt"]:
                            act.wait_ge(chosen_ready, 2 * l + 1)
                        for half in range(2):
                            last = act.activation(relu_dots[:, 2 * half:2 * half + 2, 0:kn], s_half(half, kn), ACT.Relu)
                        act.drain().then_inc(relu_ready, 1)
                    elif kind == "exp":
                        kn, i = P * (1 + st["tt"]), st["n"]
                        act.wait_ge(max_ready, 8 * l + (i + 1))
                        pr = probs[:, i % 2, 0:4 * kn].rearrange("p (h k) -> p h k", h=4)
                        sc = masked[:, i % 2, 0:4 * kn].rearrange("p (h k) -> p h k", h=4)
                        for h in range(4):
                            act.activation(pr[:, h, :], sc[:, h, :], ACT.Exp, bias=neg_max[:, i % 2, h:h + 1],
                                           accum_out=row_sum[:, i % 2, h:h + 1])
                        if st["grp"] >= 2:
                            act.activation(sink_exp[:, i % 2, :], sink_exp[:, i % 2, :], ACT.Exp)
                        act.drain().then_inc(probs_ready, 1)
                    elif kind == "probs_t":
                        for kt in range(1 + st["tt"]):
                            tf = t + (st["t"] + kt)
                            act.wait_ge(t_ready, tf.value(1, 1))
                            act.activation(probs_t[:, kt, :, :], t_bank[tf.slot(2)][:, :].rearrange("p (h q) -> p h q", h=4),
                                           ACT.Copy).then_inc(t_free[tf.slot(2)], 1)
                        act.drain().then_inc(probs_t_ready, 1)
                act_xt(t + T_AFTER_MIX1, 2)
                for k in range(4):
                    ahead(u + 22, k)
                act_xt(t + (T_AFTER_MIX1 + 4), 2)
                for k in range(4):
                    ahead(u + 26, k)
                act_root(At(0, (l, 2)))
                act_xt(t + (T_AFTER_MIX1 + 8), 2)
                act.wait_ge(s_ready, (at["s"] + (S_LAYER - 1)).value(1, 1))
                act.activation(router_t[:, :], s_bank[0:NE, 0:TT * P], ACT.Copy).then_inc(s_free, 1)
                act.drain().then_inc(router_t_ready, 1)
                tf = t + (T_AFTER_MIX1 + 12)
                act.wait_ge(t_ready, tf.value(1, 1))
                act.activation(aff[:, :, :], t_bank[tf.slot(2)][:, 0:TT * NE].rearrange("p (a b) -> p a b", a=TT),
                               ACT.Sigmoid).then_inc(t_free[tf.slot(2)], 1)
                act.drain().then_inc(aff_ready, 1)
                R = rounds_of(act, l + 1)
                with act.Fori(0, R) as r:
                    at_r = in_round(l, done + r)
                    rnd = done + r
                    experts(at_r, rnd)
                act.reg_add(rho, rho, R)
                act_root(At(1, (l, 2)))

            done = act.snap(rho, min_val=0, max_val=4)
            with act.Fori(0, DEPTH) as l:
                first, mixer, second = layer2(l, done)

                def in_root(i, n, junk):
                    act.wait_ge(x_ready, 3 * l + (2 * DEPTH + 1 + i))
                    fence(act)
                    for tt in range(TT):
                        act.activation(junk, x[:, tt, :], ACT.Square, scale=DM ** -0.5, accum_out=mean_sq[:, tt, 0:1])
                        act.drain()
                    act.sem_inc(square_ready, 1)
                    act.wait_ge(var_ready, At(4 + n, (l, 11)).value(1, 1))
                    act.activation(rstd_in[:, :], rstd_in[:, :], ACT.Sqrt)
                    act.drain().then_inc(rstd_ready, 1)
                    act.activation(rstd_half[:, :], rstd_in[:, :], ACT.Copy, scale=0.5)
                    act.drain()

                def out_roots(n, fills, junk, factor):
                    for tt in range(TT):
                        for nb in range(2):
                            act.activation(junk[:, nb * 512:(nb + 1) * 512], g_bank[fills[tt][nb].slot(4)][:, :], ACT.Square,
                                           scale=DM ** -0.5 / factor, accum_out=mean_sq[:, tt, nb:nb + 1])
                            act.drain().then_inc(square_ready, 1)
                    for tt in range(TT):
                        act.wait_ge(var_ready, At(4 + n + tt, (l, 11)).value(1, 1))
                        act.activation(rstd[:, tt:tt + 1], rstd[:, tt:tt + 1], ACT.Sqrt).then_inc(rstd_ready, 1)

                def feed_forward(at, i, n, w):
                    u, f, t = at["u"], at["g"], at["t"]
                    act_xt(t, 2)
                    in_root(i, n, ffn_junk[:, :])

                    def silu(u_up, q):
                        unit_is_used(act, u_up)
                        act.wait_ge(ffn_hid_ready, q.value(1, 1))
                        for tt in range(TT):
                            act.activation(ffn_silu[:, tt, :], s_bank[:, tt * 512:tt * 512 + 256], ACT.Silu, scale=rstd_in[:, tt:tt + 1])
                        act.drain().then_inc(up_silu_ready, 1)

                    def hid_t(tj):
                        for tt in range(TT):
                            tf = tj + tt
                            act.wait_ge(t_ready, tf.value(1, 1))
                            act.activation(ffn_t_hi[:, :, tt * P:(tt + 1) * P], t_bank[tf.slot(2)][:, 0:256].rearrange("p (a b) -> p a b", a=2),
                                           ACT.Copy).then_inc(ffn_hi_ready, 1)

                    q0 = At(w * FB, (l, 2 * FB))
                    ahead(u)
                    ahead(u, 1)
                    silu(u + 1, q0)
                    hid_t(t + 4)
                    ahead(u, 2)
                    ahead(u, 3)
                    silu(u + 3, q0 + 1)
                    ahead(u, 4)
                    hid_t(t + 6)

                    with act.Fori(2, FB) as j:
                        uj, tj, qj = (At(a.const + b, *a.terms, (j, k)) for a, b, k in ((u, -1, 3), (t, 4, 2), (q0, 0, 1)))
                        ahead(uj)
                        ahead(uj, 1)
                        silu(uj + 1, qj)
                        ahead(uj, 2)
                        hid_t(tj)
                    ahead(u, U_FFN - 1)
                    unit_is_used(act, u + (U_FFN - 1))
                    out_roots(n + 1, ffn_fills(f), ffn_junk[:, :], 0.5)

                feed_forward(first, 0, 0, 0)

                u, f, t = mixer["u"], mixer["g"], mixer["t"]
                act_xt(t, 2)
                in_root(1, 3, mix_junk)
                for i, blk in enumerate(PROJ2_ORDER):
                    ahead(u, 2 * i)
                    ahead(u, 2 * i + 1)
                    unit_is_used(act, u + (2 * i + 1))
                    for tt in range(TT):
                        b = (f + (2 * i + tt)).slot(4)
                        act.activation(proj[:, tt, blk * 512:(blk + 1) * 512], g_bank[b][:, :],
                                       {4: ACT.Sigmoid, 7: ACT.Silu}.get(blk, ACT.Copy),
                                       scale=rstd_in[:, tt:tt + 1]).then_inc(g_free[b], 1)
                    act.drain().then_inc(proj_ready, 1)
                    if i == 2:
                        act.wait_ge(t_ready, (t + 4).value(1, 1))
                        act.activation(taps[:, :, :], t_bank[0][:, 0:P].rearrange("p (c t) -> p c t", c=4), ACT.Copy).then_inc(t_free[0], 1)
                        act.drain().then_inc(taps_ready, 1)
                        act.wait_ge(pad_ready, l + 1)
                        for tt in range(TT):
                            tf = t + (5 + tt)
                            act.wait_ge(t_ready, tf.value(1, 1))
                            act.activation(conv_in[:, :, TAPS - 1 + tt * P:TAPS - 1 + (tt + 1) * P],
                                           t_bank[tf.slot(2)][:, :].rearrange("p (c n) -> p c n", c=4), ACT.Copy).then_inc(t_free[tf.slot(2)], 1)
                        act.drain().then_inc(conv_in_ready, 1)
                    if i == 5:
                        for j in range(4):
                            tf = t + (7 + j)
                            act.wait_ge(t_ready, tf.value(1, 1))
                            act.activation(qk_t[:, 2 * j:2 * j + 2, :], t_bank[tf.slot(2)][:, :].rearrange("p (a b) -> p a b", a=2),
                                           ACT.Copy).then_inc(t_free[tf.slot(2)], 1)
                        act.drain().then_inc(qk_t_ready, 1)
                ahead(u, 16)
                unit_is_used(act, u + 16)
                b = (f + 16).slot(4)
                act.activation(lr_t[:, :], g_bank[b][0:16, 0:TT * P], ACT.Copy).then_inc(g_free[b], 1)
                act.drain().then_inc(lr_t_ready, 1)
                act.sem_inc(g_free[(f + 17).slot(4)], 1)
                act.sem_inc(proj_ready, 1)

                def soft_tail(z, tmp):
                    act.activation(tmp, z, ACT.Abs)
                    act.drain()
                    act.activation(tmp, tmp, ACT.Exp, scale=-1.0)
                    act.drain()
                    act.activation(tmp, tmp, ACT.Ln, bias=1.0)

                for st in PLAN2:
                    kind = st["kind"]
                    if kind == "gate":
                        n, half = st["n"], st["half"]
                        k = 17 + 2 * n + half
                        ahead(u, k)
                        if half:
                            unit_is_used(act, u + k)
                            for tt in range(TT):
                                b = (f + (st["g"] + tt)).slot(4)
                                act.activation(gate2[:, tt, n * 512:(n + 1) * 512], g_bank[b][:, :], ACT.Tanh,
                                               scale=rstd_half[:, tt:tt + 1]).then_inc(g_free[b], 1)
                            act.drain().then_inc(gate2_ready, 1)
                    elif kind == "soft":
                        kn, i = P * (1 + st["tt"]), st["n"]
                        act.wait_ge(logit_ready, 4 * l + (i + 1))
                        soft_tail(logits[i % 2][:, :, :, 0:kn], soft_heads[:, :, :, 0:kn])
                        act.drain().then_inc(soft_ready, 1)
                    elif kind == "stick":
                        kn, i = P * (1 + st["tt"]), st["n"]
                        act.wait_ge(log_w_ready, 4 * l + (i + 1))
                        act.activation(logits[i % 2][:, :, :, 0:kn], logits[i % 2][:, :, :, 0:kn], ACT.Exp)
                        act.drain().then_inc(stick_ready, 1)
                    elif kind == "probs_t":
                        for kt in range(1 + st["tt"]):
                            tf = t + (st["t"] + kt)
                            act.wait_ge(t_ready, tf.value(1, 1))
                            act.activation(probs_t2[:, kt, :, :], t_bank[tf.slot(2)][:, :].rearrange("p (h q) -> p h q", h=4),
                                           ACT.Copy).then_inc(t_free[tf.slot(2)], 1)
                        act.drain().then_inc(probs_t2_ready, 1)
                    elif kind == "branches_t":
                        act_xt(t + st["t"], 2, EARLY_BRANCHES)
                    elif kind == "conv_norm":
                        act_root(At(4 + 4, (l, 11)))
                        act.wait_ge(conv_mid_ready, l + 1)
                        act.activation(proj[:, :, ATTN2[1]:ATTN2[1] + 512], proj[:, :, ATTN2[1]:ATTN2[1] + 512], ACT.Silu)
                        act.drain().then_inc(branch_ready, 1)
                    elif kind == "alpha":
                        act.wait_ge(alpha_in_ready, l + 1)
                        soft_tail(log_alpha.rearrange(flat), log_tmp)
                        act.drain().then_inc(alpha_soft_ready, 1)
                    elif kind == "gla_q":
                        tf = t + st["t"]
                        act.wait_ge(t_ready, tf.value(1, 1))
                        act.activation(lin_qt[:, :, :], t_bank[tf.slot(2)][:, :].rearrange("p (h n) -> p h n", h=2), ACT.Copy,
                                       scale=DH ** -0.5).then_inc(t_free[tf.slot(2)], 1)
                        act.drain().then_inc(gla_q_ready, 1)
                    elif kind == "decay":
                        tf = t + st["t"]
                        act.wait_ge(t_ready, tf.value(1, 1))
                        act.activation(decay.rearrange(flat), t_bank[tf.slot(2)][:, :], ACT.Exp).then_inc(t_free[tf.slot(2)], 1)
                        tf = t + (st["t"] + 1)
                        act.wait_ge(t_ready, tf.value(1, 1))
                        act.activation(lam[:, :], t_bank[tf.slot(2)][:, 0:8], ACT.Exp).then_inc(t_free[tf.slot(2)], 1)
                        act.drain().then_inc(decay_ready, 1)
                    elif kind == "gla_out":
                        act.wait_ge(var_ready, At(4 + 5, (l, 11)).value(1, 1))
                        act.activation(mean_sq8[:, :, :], mean_sq8[:, :, :], ACT.Sqrt).then_inc(rstd_ready, 1)
                act_xt(t + T_AFTER_MIX2, 1, LAST_BRANCH)
                for k in range(6):
                    ahead(u + 29, k)
                act_xt(t + (T_AFTER_MIX2 + 2), 2)
                for k in range(4):
                    ahead(u + 35, k)
                unit_is_used(act, u + 38)
                out_roots(6, mix_fills(f), mix_junk, 1.0)

                feed_forward(second, 2, 8, 1)

        @block.tensor
        def _(pe):
            pe.sem_inc(w_used, 2 * RING)
            pe.sem_inc(credits, 1)
            pe.wait_ge(const_in, 16)
            pe.wait_ge(x_in, 16)
            pe.wait_ge(credits, 3)

            def s_at(h, kn):
                a = 512 * (h % 2) + (h // 2) * kn
                return s_bank[:, a:a + kn]

            def s_wait(s):
                pe.wait_ge(s_free, s.value(1, 1))

            def rot_head(blk, half, a, n):
                return rot_t[64 * half:64 * half + 64, blk, a:a + n]

            rho = pe.alloc_register("rounds_done_pe")
            pe.reg_mov(rho, 0)
            with pe.Fori(0, DEPTH) as l:
                done = pe.snap(rho, min_val=0, max_val=4)
                at = layer1(l, done)
                u, f, t = at["u"], at["g"], at["t"]
                pe_xt(x, t, 2, lambda e, tt: e.wait_ge(row_ready, 4 * l + (tt + 1)))
                pe.wait_ge(xt_ready, 4 * l + 1)
                for blk in range(5):
                    pe_block(u + 2 * blk, f + 2 * blk, min(512, N_QKV - blk * 512))
                    if blk == 1:
                        pe.wait_ge(qkv_ready, 5 * l + 1)
                        for tt in range(TT):
                            bank = t_wait(t + (4 + tt))
                            pe.transpose(bank[:, 0:P], qkv[:, tt, A_C:A_C + P], ident).then_inc(t_ready, 1)
                pe.wait_ge(lat_t_ready, l + 1)
                pe.wait_ge(small_in, 48 * l + 48)
                for tt in range(TT):
                    bank = g_wait(f + (10 + tt))
                    last = pe.matmul(bank[:, 0:P], lat_t[:, tt, :], w_ukv[:, :], start=True, stop=True)
                last.then_inc(kv_lat_done, 1)

                for st in PLAN1:
                    kind = st["kind"]
                    if kind == "rt":
                        j = st["j"]
                        if j == 0:
                            pe.wait_ge(rot_ready, l + 1)
                        bank = t_wait(t + st["t"])
                        for i in range(4):
                            blk, tt = 2 * j + i // 2, i % 2
                            last = pe.transpose(bank[:, i * P:(i + 1) * P], rot[:, tt, blk * P:(blk + 1) * P], ident)
                        last.then_inc(t_ready, 1)
                    elif kind == "gate":
                        n = st["n"]
                        pe_block(u + (10 + 2 * n), f + (12 + 2 * n), halves=(st["half"],))
                    elif kind == "index":
                        tt, kn = st["tt"], P * (1 + st["tt"])
                        pe.wait_ge(rot_t_ready, l + 1)
                        s_wait(at["s"] + st["s"])
                        for h in range(4):
                            half = h % 2
                            last = pe.matmul(s_at(h, kn), rot_head(RB_IQ + h // 2, half, tt * P, P),
                                             rot_head(RB_KAIK if half else RB_IKKA, half, 0, kn), start=True, stop=True)
                        last.then_inc(s_ready, 1)
                    elif kind == "scores":
                        tt, kn, grp = st["tt"], P * (1 + st["tt"]), st["grp"]
                        s_wait(at["s"] + st["s"])
                        for h in range(4):
                            half = h % 2
                            if grp == 0:
                                q, kk = RB_AQ + h // 2, RB_IKKA if half else RB_KAIK
                            elif grp == 1:
                                q, kk = RB_BQ + h // 2, RB_BK + h // 2
                            else:
                                q, kk = RB_CQ + (4 * (grp - 2) + h) // 2, RB_CK if grp - 2 == half else RB_CK2
                            last = pe.matmul(s_at(h, kn), rot_head(q, half, tt * P, P),
                                             rot_head(kk, half, 0, kn), start=True, stop=True)
                        last.then_inc(s_ready, 1)
                    elif kind == "probs_t":
                        tt, kn, i = st["tt"], P * (1 + st["tt"]), st["n"]
                        pr = probs[:, i % 2, 0:4 * kn].rearrange("p (h k) -> p h k", h=4)
                        pe.wait_ge(probs_ready, 8 * l + (i + 1))
                        for kt in range(1 + tt):
                            bank = t_wait(t + (st["t"] + kt))
                            for h in range(4):
                                last = pe.transpose(bank[:, h * P:(h + 1) * P], pr[:, h, kt * P:(kt + 1) * P], ident)
                            last.then_inc(t_ready, 1)
                    elif kind == "values":
                        tt, grp, i = st["tt"], st["grp"], st["n"]
                        bank = t_wait(t + st["t"])
                        pe.wait_ge(probs_t_ready, 8 * l + (i + 1))
                        for j, h in enumerate((0, 2, 1, 3)):
                            for kt in range(1 + tt):
                                v = (kv_lat[:, kt, DH:2 * DH] if grp == 0 else
                                     qkv[:, kt, B_V + h * DH:B_V + (h + 1) * DH] if grp == 1 else
                                     qkv[:, kt, C_V + (grp - 2) * DH:C_V + (grp - 1) * DH])
                                last = pe.matmul(bank[:, j * DH:(j + 1) * DH], probs_t[:, kt, j, :], v,
                                                 start=(kt == 0), stop=(kt == tt))
                        last.then_inc(t_ready, 1)
                pe_xt(attn, t + T_AFTER_MIX1, 2, lambda e, tt: e.wait_ge(attn_ready, 8 * l + 8))
                pe.wait_ge(xt_ready, 4 * l + 2)
                for blk in range(2):
                    for half in range(2):
                        uu = u + (22 + 2 * blk + half)
                        s = uu.slot(RING)
                        for h in range(2):
                            half_is_split(uu, h)
                            br, first, stop = ((h, True, True), (2, h == 0, h == 1))[half]
                            for tt in range(TT):
                                ff = f + (24 + 6 * blk + 2 * br + tt)
                                bank = g_wait(ff) if first else g_bank[ff.slot(4)]
                                for k in (2 * h, 2 * h + 1):
                                    kk = 4 * half + k
                                    last = mm3(bank[:, :], xt_hi[:, kk, tt * P:(tt + 1) * P], xt_lo[:, kk, tt * P:(tt + 1) * P],
                                               w_hi[:, s, k * 512:(k + 1) * 512], w_lo[:, s, k * 512:(k + 1) * 512],
                                               first and k == 2 * h, stop and k == 2 * h + 1)
                            last.then_inc(w_used, 1)
                pe_xt(merged, t + (T_AFTER_MIX1 + 4), 2, lambda e, tt: e.wait_ge(merged_ready, 2 * l + 2))
                pe.wait_ge(xt_ready, 4 * l + 3)
                for blk in range(2):
                    pe_block(u + (26 + 2 * blk), f + (36 + 2 * blk))
                pe_xt(x, t + (T_AFTER_MIX1 + 8), 2, lambda e, tt: e.wait_ge(row_ready, 4 * l + (2 + tt + 1)))
                pe.wait_ge(xt_ready, 4 * l + 4)
                pe.wait_ge(router_split, 2)
                s_wait(at["s"] + (S_LAYER - 1))
                for k in range(8):
                    last = mm3(s_bank[0:NE, 0:TT * P], wr_hi[:, k, :], wr_lo[:, k, :], xt_hi[:, k, :], xt_lo[:, k, :], k == 0, k == 7)
                last.then_inc(s_ready, 1)
                pe.wait_ge(router_t_ready, l + 1)
                bank = t_wait(t + (T_AFTER_MIX1 + 12))
                fence(pe)
                for tt in range(TT):
                    last = pe.transpose(bank[:, tt * NE:(tt + 1) * NE], router_t[:, tt * P:(tt + 1) * P], ident[0:NE, 0:NE])
                last.then_inc(t_ready, 1)
                pe.wait_ge(in_grp_ready, l + 1)
                bank = t_wait(t + (T_AFTER_MIX1 + 13))
                pe.matmul(bank[:, 0:NG], c("before"), in_grp[:, 0, :], start=True, stop=True)
                pe.matmul(bank[:, NG:2 * NG], c("before"), in_grp[:, 1, :], start=True, stop=False)
                pe.matmul(bank[:, NG:2 * NG], c("ones", 0, P), in_grp[:, 0, :], start=False, stop=True)
                pe.matmul(bank[:, 2 * NG:3 * NG], c("ones", 0, P), in_grp[:, 0, :], start=True, stop=False)
                pe.matmul(bank[:, 2 * NG:3 * NG], c("ones", 0, P), in_grp[:, 1, :], start=False, stop=True).then_inc(t_ready, 1)

                R = rounds_of(pe, l + 1)
                with pe.Fori(0, R) as r:
                    at_r = in_round(l, done + r)
                    rnd = done + r

                    def run(part, g):
                        count = plus(At(0, (rnd, 16)), 0, g, 4)
                        for what, e, half, place in walk(part, at_r, g):
                            if what == "gather":
                                src = g if part == "start" else g + 1
                                if part == "start":
                                    pe.wait_ge(onehot_ready, done + l + (r + 1))
                                for i in range(2):
                                    bank = t_wait(place + i)
                                    for j in range(4):
                                        k = 4 * i + j
                                        for tt in range(TT):
                                            last = pe.matmul(bank[:, j * P:(j + 1) * P], x[:, tt, k * P:(k + 1) * P],
                                                             onehot[:, tt, bass.ds(src, 1), :].rearrange("p a b -> p (a b)"),
                                                             start=(tt == 0), stop=(tt == TT - 1))
                                    last.then_inc(t_ready, 1)
                            elif what == "slots":
                                for tt in range(TT):
                                    bank = t_wait(place + tt)
                                    for gg in range(NG):
                                        last = pe.transpose(bank[:, gg * P:(gg + 1) * P], onehot[:, tt, gg, :], ident)
                                    last.then_inc(t_ready, 1)
                                pe.wait_ge(comb_ready, l + 1)
                                for i in range(2):
                                    bank = t_wait(place + (2 + i))
                                    for j in range(2):
                                        gg = 2 * i + j
                                        for tt in range(TT):
                                            last = pe.matmul(bank[:, 4 * j:4 * j + 4], onehot[:, tt, gg, :], comb[:, tt, 4 * gg:4 * gg + 4],
                                                             start=(tt == 0), stop=(tt == TT - 1))
                                    last.then_inc(t_ready, 1)
                            elif what == "hid_t":
                                pe.wait_ge(hid_ready, count.value(1, 2 + e + 1))
                                bank = t_wait(place)
                                for j in range(4):
                                    last = pe.transpose(bank[:, j * P:(j + 1) * P], hid[:, e % 2, j * P:(j + 1) * P], ident)
                                last.then_inc(t_ready, 1)
                            elif what == "back":
                                pe.drain().then_inc(s_ready, 1)
                            else:
                                s = place.slot(RING)
                                if what == "down" and half == 0:
                                    pe.wait_ge(hid_t_ready, count.value(1, 1 + e))
                                    if e == 0:
                                        s_wait(plus(at_r["s"], 0, g, 1))
                                if what == "gate" and half == 0 and e % EPG == 0:
                                    pe.wait_ge(xg_ready, plus(At(0, (rnd, 4)), 1 + (e > 0), g, 1).value())
                                for h in range(2):
                                    half_is_split(place, h)
                                    if what == "down":
                                        for nb in range(2):
                                            kk, c0 = 2 * half + h, h * DM + nb * 512
                                            last = mm3(s_bank[:, nb * 512:(nb + 1) * 512], hid_t_hi[:, e % 2, kk, :], hid_t_lo[:, e % 2, kk, :],
                                                       w_hi[:, s, c0:c0 + 512], w_lo[:, s, c0:c0 + 512],
                                                       e == 0 and kk == 0, e == EPG - 1 and kk == 3)
                                    else:
                                        ff = expert_fill(at_r, what, g, e)
                                        bank = g_bank[ff.slot(4)] if half or h else g_wait(ff)
                                        for k in (2 * h, 2 * h + 1):
                                            kk = 4 * half + k
                                            last = mm3(bank[:, :], xg_hi[:, kk, :], xg_lo[:, kk, :], w_hi[:, s, k * 512:(k + 1) * 512],
                                                       w_lo[:, s, k * 512:(k + 1) * 512], kk == 0, kk == 7)
                                    last.then_inc(w_used, 1)

                    all_parts(pe, run)
                    pe.wait_ge(y_ready, 4 * rnd + 4)
                    for i in range(4):
                        tt, nb = i // 2, i % 2
                        bank = g_wait(at_r["g"] + (32 + i))
                        for g in range(NG):
                            pe.matmul(bank[:, :], onehot_t[:, tt, g, :], y_hi[:, g, nb * 512:(nb + 1) * 512], start=(g == 0), stop=False)
                            last = pe.matmul(bank[:, :], onehot_t[:, tt, g, :], y_lo[:, g, nb * 512:(nb + 1) * 512], start=False, stop=(g == NG - 1))
                        last.then_inc(returned, 1)
                pe.reg_add(rho, rho, R)

            done = pe.snap(rho, min_val=0, max_val=4)
            with pe.Fori(0, DEPTH) as l:
                first, mixer, second = layer2(l, done)

                def feed_forward(at, n, w, n_xt):
                    u, f, t, s0 = at["u"], at["g"], at["t"], at["s"]
                    pe_xt(ffn_y, t, 2, lambda e, tt: e.wait_ge(normed_ready, 6 * l + (2 * n + tt)))
                    pe.wait_ge(xt_ready, 6 * l + (2 * 4 + n_xt))
                    q0 = At(w * FB, (l, 2 * FB))

                    def gate_up(uj, sj):
                        s_wait(sj)
                        for half in range(2):
                            uu = uj + half
                            s = uu.slot(RING)
                            for h in range(2):
                                half_is_split(uu, h)
                                for tt in range(TT):
                                    for k in (2 * h, 2 * h + 1):
                                        kk = 4 * half + k
                                        last = mm3(s_bank[:, tt * 512:(tt + 1) * 512], xt_hi[:, kk, tt * P:(tt + 1) * P],
                                                   xt_lo[:, kk, tt * P:(tt + 1) * P], w_hi[:, s, k * 512:(k + 1) * 512],
                                                   w_lo[:, s, k * 512:(k + 1) * 512], kk == 0, kk == 7)
                                last.then_inc(w_used, 1)
                        pe.sem_inc(s_ready, 1)

                    def down(uu, q, first_, last_):
                        s = uu.slot(RING)
                        pe.wait_ge(ffn_t_ready, q.value(1, 1))
                        for k in range(2):
                            half_is_split(uu, k)
                            for i in range(4):
                                tt, nb = i // 2, i % 2
                                bank = g_wait(f + i) if first_ and k == 0 else g_bank[(f + i).slot(4)]
                                c0 = k * DM + nb * 512
                                last = mm3(bank[:, :], ffn_t_hi[:, k, tt * P:(tt + 1) * P], ffn_t_lo[:, k, tt * P:(tt + 1) * P],
                                           w_hi[:, s, c0:c0 + 512], w_lo[:, s, c0:c0 + 512], first_ and k == 0, last_ and k == 1)
                            last.then_inc(w_used, 1)

                    def hid_t(tj, q):
                        pe.wait_ge(ffn_hid_ready, q.value(1, 2))
                        for tt in range(TT):
                            bank = t_wait(tj + tt)
                            for k in range(2):
                                last = pe.transpose(bank[:, k * P:(k + 1) * P], ffn_hid[:, tt, k * P:(k + 1) * P], ident)
                            last.then_inc(t_ready, 1)

                    gate_up(u, s0)
                    hid_t(t + 4, q0)
                    gate_up(u + 2, s0 + 1)
                    down(u + 4, q0, True, False)
                    hid_t(t + 6, q0 + 1)
                    with pe.Fori(2, FB) as j:
                        uj, tj, qj, sj = (At(a.const + b, *a.terms, (j, k)) for a, b, k in ((u, -1, 3), (t, 4, 2), (q0, 0, 1), (s0, 0, 1)))
                        gate_up(uj, sj)
                        down(uj + 2, qj + -1, False, False)
                        hid_t(tj, qj)
                    down(u + (U_FFN - 1), q0 + (FB - 1), False, True)

                feed_forward(first, 1, 0, 1)

                u, f, t = mixer["u"], mixer["g"], mixer["t"]
                pe_xt(mix_y, t, 2, lambda e, tt: e.wait_ge(normed_ready, 6 * l + (4 + tt)))
                pe.wait_ge(xt_ready, 6 * l + (2 * 4 + 2))

                def head2(blk, half, a, n):
                    return qk_t[64 * half:64 * half + 64, blk, a:a + n]

                for i, blk in enumerate(PROJ2_ORDER):
                    pe_block(u + 2 * i, f + 2 * i)
                    if i == 2:
                        pe.wait_ge(mixer_in, 64 * l + 64)
                        bank = t_wait(t + 4)
                        fence(pe)
                        for k in range(4):
                            last = pe.transpose(bank[:, k * 32:(k + 1) * 32], taps_raw[:, k * P:(k + 1) * P], ident[0:32, 0:32])
                        last.then_inc(t_ready, 1)
                        pe.wait_ge(conv_u_ready, l + 1)
                        for tt in range(TT):
                            bank = t_wait(t + (5 + tt))
                            for k in range(4):
                                last = pe.transpose(bank[:, k * P:(k + 1) * P], proj[:, tt, CONV + k * P:CONV + (k + 1) * P], ident)
                            last.then_inc(t_ready, 1)
                    if i == 5:
                        pe.wait_ge(proj_ready, 9 * l + 4)
                        for j in range(4):
                            bank = t_wait(t + (7 + j))
                            for a in range(4):
                                b2, tt = 2 * j + a // 2, a % 2
                                last = pe.transpose(bank[:, a * P:(a + 1) * P], proj[:, tt, b2 * P:(b2 + 1) * P], ident)
                            last.then_inc(t_ready, 1)
                uu = u + 16
                s = uu.slot(RING)
                for h in range(2):
                    half_is_split(uu, h)
                    bank = g_bank[(f + 16).slot(4)] if h else g_wait(f + 16)
                    for k in range(4 * h, 4 * h + 4):
                        last = mm3(bank[0:16, 0:TT * P], w_hi[:, s, k * 256:k * 256 + 16], w_lo[:, s, k * 256:k * 256 + 16],
                                   xt_hi[:, k, :], xt_lo[:, k, :], k == 0, k == 7)
                    last.then_inc(w_used, 1)

                for st in PLAN2:
                    kind = st["kind"]
                    if kind == "gate":
                        n = st["n"]
                        pe_block(u + (17 + 2 * n), f + st["g"], halves=(st["half"],))
                    elif kind == "scores":
                        tt, kn, grp = st["tt"], P * (1 + st["tt"]), st["grp"]
                        pe.wait_ge(qk_t_ready, l + 1)
                        s_wait(mixer["s"] + st["s"])
                        for h in range(4):
                            b2 = (4 * grp + h) // 2
                            last = pe.matmul(s_at(h, kn), head2(b2, h % 2, tt * P, P), head2(4 + b2, h % 2, 0, kn), start=True, stop=True)
                        last.then_inc(s_ready, 1)
                    elif kind == "probs_t":
                        tt, i = st["tt"], st["n"]
                        pe.wait_ge(stick_ready, 4 * l + (i + 1))
                        for kt in range(1 + tt):
                            bank = t_wait(t + (st["t"] + kt))
                            for h in range(4):
                                last = pe.transpose(bank[:, h * P:(h + 1) * P], logits[i % 2][:, h // 2, h % 2, kt * P:(kt + 1) * P], ident)
                            last.then_inc(t_ready, 1)
                    elif kind == "branches_t":
                        pe.wait_ge(branch_ready, 5 * l + 5)
                        for i, (tt, br) in enumerate(EARLY_BRANCHES):
                            bank = t_wait(t + (st["t"] + i))
                            for j in range(4):
                                last = pe.transpose(bank[:, j * P:(j + 1) * P], proj[:, tt, ATTN2[br] + j * P:ATTN2[br] + (j + 1) * P], ident)
                            last.then_inc(t_ready, 1)
                    elif kind == "values":
                        tt, grp, i = st["tt"], st["grp"], st["n"]
                        bank = t_wait(t + st["t"])
                        pe.wait_ge(probs_t2_ready, 4 * l + (i + 1))
                        pe.wait_ge(proj_ready, 9 * l + 9)
                        for j, h in enumerate((0, 2, 1, 3)):
                            for kt in range(1 + tt):
                                c0 = S_V + (4 * grp + h) * DH
                                last = pe.matmul(bank[:, j * DH:(j + 1) * DH], probs_t2[:, kt, j, :], proj[:, kt, c0:c0 + DH],
                                                 start=(kt == 0), stop=(kt == tt))
                        last.then_inc(t_ready, 1)
                    elif kind == "conv_back":
                        pe.wait_ge(conv_y_ready, 2 * l + 2)
                        for tt in range(TT):
                            bank = t_wait(t + (st["t"] + tt))
                            for k in range(4):
                                last = pe.transpose(bank[:, k * P:(k + 1) * P], conv_y[:, k, tt * P:(tt + 1) * P], ident)
                            last.then_inc(t_ready, 1)
                    elif kind == "alpha":
                        pe.wait_ge(lr_t_ready, l + 1)
                        pe.wait_ge(alpha_in, 48 * l + 48)
                        for tt in range(TT):
                            bank = g_wait(f + (st["g"] + tt))
                            last = pe.matmul(bank[:, 0:256], lr_t[:, tt * P:(tt + 1) * P], w_alpha, start=True, stop=True)
                        last.then_inc(kv_lat_done, 1)
                    elif kind == "gla_q":
                        bank = t_wait(t + st["t"])
                        for a in range(4):
                            h2, tt = a // 2, a % 2
                            last = pe.transpose(bank[:, a * P:(a + 1) * P], proj[:, tt, L_Q + h2 * P:L_Q + (h2 + 1) * P], ident)
                        last.then_inc(t_ready, 1)
                    elif kind == "decay":
                        pe.wait_ge(log_alpha_ready, l + 1)
                        bank = t_wait(t + st["t"])
                        for tt in range(TT):
                            last = pe.matmul(bank[:, tt * 256:(tt + 1) * 256], c("later_in_chunk"), log_alpha[:, tt, :], start=True, stop=True)
                        last.then_inc(t_ready, 1)
                        bank = t_wait(t + (st["t"] + 1))
                        for h2 in range(2):
                            for tt in range(TT):
                                a = h2 * 4 + tt * 2
                                last = pe.matmul(bank[:, a:a + 2], log_alpha[:, tt, h2 * P:(h2 + 1) * P], c("chunk_of"), start=True, stop=True)
                        last.then_inc(t_ready, 1)
                    elif kind == "states":
                        pe.wait_ge(k_dec_ready, l + 1)
                        for ch in range(4):
                            tt, c2 = ch // 2, ch % 2
                            bank = t_wait(t + (st["t"] + ch))
                            for h2 in range(2):
                                last = pe.matmul(bank[:, h2 * 256:(h2 + 1) * 256], k_dec[:, tt, c2, h2 * P:(h2 + 1) * P],
                                                 proj[:, tt, L_V + h2 * 256:L_V + (h2 + 1) * 256], start=True, stop=True)
                            last.then_inc(t_ready, 1)
                    elif kind == "gla_out":
                        pe.wait_ge(gla_q_ready, l + 1)
                        for tt in range(TT):
                            bank = t_wait(t + (st["t"] + tt))
                            pe.wait_ge(state_ready, 4 * l + (2 * tt + 2))
                            for c2 in range(2):
                                for h2 in range(2):
                                    a = tt * P + c2 * 64
                                    last = pe.matmul(bank[64 * c2:64 * c2 + 64, h2 * 256:(h2 + 1) * 256], lin_qt[:, h2, a:a + 64],
                                                     state[:, 2 * tt + c2, h2, :], start=True, stop=True)
                            last.then_inc(t_ready, 1)

                pe.wait_ge(gla_ready, l + 1)
                for i, (tt, br) in enumerate(LAST_BRANCH):
                    bank = t_wait(t + (T_AFTER_MIX2 + i))
                    for j in range(4):
                        last = pe.transpose(bank[:, j * P:(j + 1) * P], proj[:, tt, ATTN2[br] + j * P:ATTN2[br] + (j + 1) * P], ident)
                    last.then_inc(t_ready, 1)
                pe.wait_ge(xt_ready, 6 * l + (2 * 4 + 4))
                for blk in range(2):
                    for br in range(3):
                        uu = u + (29 + 3 * blk + br)
                        s = uu.slot(RING)
                        for h in range(2):
                            half_is_split(uu, h)
                            for tt in range(TT):
                                ff = f + (32 + 6 * blk + 2 * br + tt)
                                bank = g_bank[ff.slot(4)] if h else g_wait(ff)
                                for k in (2 * h, 2 * h + 1):
                                    kk = 4 * br + k
                                    last = mm3(bank[:, :], xt_hi[:, kk, tt * P:(tt + 1) * P], xt_lo[:, kk, tt * P:(tt + 1) * P],
                                               w_hi[:, s, k * 512:(k + 1) * 512], w_lo[:, s, k * 512:(k + 1) * 512], k == 0, k == 3)
                            last.then_inc(w_used, 1)
                pe_xt(merged2, t + (T_AFTER_MIX2 + 2), 2, lambda e, tt: e.wait_ge(merged2_ready, 2 * l + 2))
                pe.wait_ge(xt_ready, 6 * l + (2 * 4 + 5))
                for blk in range(2):
                    pe_block(u + (35 + 2 * blk), f + (44 + 2 * blk))

                feed_forward(second, 3, 1, 6)

        @block.vector
        def _(dve):
            dve.sem_inc(lo_ready, 2 * RING)
            for b in g_free + t_free:
                dve.sem_inc(b, 1)
            dve.sem_inc(s_free, 1)
            dve.sem_inc(x_ready, 1)
            dve.sem_inc(row_ready, TT)
            dve.sem_inc(hid_ready, 2)
            dve.sem_inc(ffn_hid_ready, 1)
            dve.sem_inc(normed_ready, 1)
            dve.sem_inc(credits, 2)
            dve.wait_ge(const_in, 16)
            dve.wait_ge(x_in, 16)
            dve.wait_ge(router_split, 1)
            dve.tensor_tensor(wr_lo[:, :, :], w_router[:, :, :], wr_hi[:, :, :].bitcast(F32), ALU.subtract).then_inc(router_split, 1)

            ahead = ahead_of(split_lo)
            for h in range(AHEAD):
                split_lo(At(0), h)

            def rope(src, lo, heads):
                dst = rot[:, :, lo:lo + heads * DH].rearrange("p t (h d) -> p t h d", d=DH)
                src = src.rearrange("p t (h d) -> p t h d", d=DH)
                tab = c("rope").rearrange("p (t m) -> p t m", t=TT)
                h = DH // 2
                dve.drain()
                for tt in range(TT):
                    def table(a, n):
                        return tab[:, tt, a:a + n].unsqueeze(1).to_broadcast([P, heads, n])
                    dve.tensor_tensor(dst[:, tt], src[:, tt], table(0, DH), ALU.mult)
                    dve.tensor_tensor(rope_tmp[:, tt, 0:heads, 0:h], src[:, tt, :, h:DH], table(DH, h), ALU.mult)
                    dve.tensor_tensor(rope_tmp[:, tt, 0:heads, h:DH], src[:, tt, :, 0:h], table(DH + h, h), ALU.mult)
                dve.drain()
                for tt in range(TT):
                    last = dve.tensor_tensor(dst[:, tt], dst[:, tt], rope_tmp[:, tt, 0:heads, :], ALU.add)
                return last

            def all_equal_max(src, of, n, out_hot):
                dve.tensor_reduce(best[:, :], src, AX.X, ALU.max)
                dve.drain()
                dve.tensor_tensor(key[:, :, 0:n], src, best[:, :].unsqueeze(2).to_broadcast([P, TT, n]), ALU.is_equal)
                dve.drain()
                dve.tensor_tensor(key[:, :, 0:n], key[:, :, 0:n], of.unsqueeze(1).to_broadcast([P, TT, n]), ALU.mult)
                dve.drain()
                dve.tensor_reduce(best[:, :], key[:, :, 0:n], AX.X, ALU.max)
                dve.drain()
                dve.tensor_tensor(out_hot, key[:, :, 0:n], best[:, :].unsqueeze(2).to_broadcast([P, TT, n]), ALU.is_equal)
                dve.drain()

            rho = dve.alloc_register("rounds_done_dve")
            dve.reg_mov(rho, 0)
            with dve.Fori(0, DEPTH) as l:
                done = dve.snap(rho, min_val=0, max_val=4)
                at = layer1(l, done)
                u, f, t = at["u"], at["g"], at["t"]
                dve_xt(t, At(0, (l, 16)), 2)
                for blk in range(5):
                    ahead(u, 2 * blk)
                    ahead(u, 2 * blk + 1)
                    if blk == 2:
                        dve.wait_ge(qkv_ready, 5 * l + 2)
                        fence(dve)
                        rope(qkv[:, :, A_Q:A_Q + 256], 0, 4)
                        rope(qkv[:, :, A_IQ:A_IQ + 320], 256, 5)
                    if blk == 3:
                        dve.wait_ge(qkv_ready, 5 * l + 3)
                        fence(dve)
                        rope(qkv[:, :, B_Q:B_Q + 512], 640, 8)
                dve.wait_ge(qkv_ready, 5 * l + 5)
                fence(dve)
                rope(qkv[:, :, C_Q:C_Q + 640], 1152, 10)
                dve.wait_ge(kv_lat_ready, l + 1)
                fence(dve)
                rope(kv_lat[:, :, 0:DH], 576, 1)
                dve.drain()
                for tt in range(TT):
                    for a, b in ((1792, 576), (1856, 512), (1920, 1728), (1984, 1664)):
                        dve.tensor_copy(rot[:, tt, a:a + DH], rot[:, tt, b:b + DH])
                dve.drain().then_inc(rot_ready, 1)

                for st in PLAN1:
                    kind = st["kind"]
                    if kind == "gate":
                        ahead(u, 10 + 2 * st["n"] + st["half"])
                    elif kind == "index":
                        tt = st["tt"]
                        kn = P * (1 + tt)
                        work = chosen[:, tt, 0:kn]
                        dve.drain()
                        dve.wait_ge(relu_ready, 2 * l + (tt + 1))
                        dve.sem_inc(s_free, 1)
                        dve.tensor_scalar(work, relu_dots[:, 0, 0:kn], qkv[:, tt, A_IW:A_IW + 1], 0.0, ALU.mult, ALU.add)
                        order = (0, 2, 1, 3)
                        for h in range(1, 4):
                            dve.drain()
                            dve.scalar_tensor_tensor(out=work, in0=relu_dots[:, h, 0:kn], scalar=qkv[:, tt, A_IW + order[h]:A_IW + order[h] + 1],
                                                     in1=work, op0=ALU.mult, op1=ALU.add)
                        dve.drain().then_inc(chosen_ready, 1)
                        dve.tensor_tensor(work, work, c("mask_causal", 256 - kn), ALU.add)
                        dve.drain()
                    elif kind == "topk":
                        for tt in st["tiles"]:
                            work = chosen[:, tt, 0:P * (1 + tt)]
                            dve.drain()
                            dve.max(top8[:, :], work)
                            dve.drain()
                            dve.match_replace(out=work, in_to_replace=top8[:, :], in_values=work, imm_value=TAKEN)
                        if not st["last"]:
                            continue
                        dve.drain()
                        for tt in range(TT):
                            work = chosen[:, tt, 0:P * (1 + tt)]
                            dve.tensor_scalar(work, work, TAKEN / 3, 1.0, ALU.is_le, ALU.subtract)
                        dve.drain()
                        for tt in range(TT):
                            kn = P * (1 + tt)
                            work = chosen[:, tt, 0:kn]
                            dve.scalar_tensor_tensor(out=work, in0=work, scalar=-NEG, in1=c("mask_causal", 256 - kn), op0=ALU.mult, op1=ALU.add)
                    elif kind == "scores":
                        tt, i, grp = st["tt"], st["n"], st["grp"]
                        kn, b = P * (1 + tt), st["n"] % 2
                        mask = (chosen[:, tt, 0:kn] if grp == 0 else c("mask_causal" if grp == 1 else "mask_window", 256 - kn))
                        sc = masked[:, b, 0:4 * kn].rearrange("p (h k) -> p h k", h=4)
                        dve.drain()
                        dve.wait_ge(s_ready, (at["s"] + st["s"]).value(1, 1))
                        for half in range(2):
                            dve.scalar_tensor_tensor(out=sc[:, 2 * half:2 * half + 2, :], in0=s_half(half, kn), scalar=SCALE,
                                                     in1=mask.unsqueeze(1).to_broadcast([P, 2, kn]), op0=ALU.mult, op1=ALU.add)
                        dve.drain().then_inc(s_free, 1)
                        dve.tensor_reduce(row_max[:, b, :], sc, AX.X, ALU.max)
                        dve.drain()
                        if grp >= 2:
                            sk = sinks[:, 4 * (grp - 2):4 * (grp - 1)].rearrange("p (i half) -> p half i", half=2)
                            mx = row_max[:, b, :].rearrange("p (half i) -> p half i", half=2)
                            dve.tensor_tensor(mx, mx, sk, ALU.max)
                            dve.drain()
                            dve.tensor_tensor(sink_exp[:, b, :].rearrange("p (half i) -> p half i", half=2), sk, mx, ALU.subtract)
                        dve.tensor_scalar(neg_max[:, b, :], row_max[:, b, :], -1.0, None, ALU.mult)
                        dve.drain().then_inc(max_ready, 1)
                    elif kind == "values":
                        tt, i, grp = st["tt"], st["n"], st["grp"]
                        b = i % 2
                        tf = t + st["t"]
                        dve.wait_ge(probs_ready, 8 * l + (i + 1))
                        if grp >= 2:
                            dve.tensor_tensor(row_sum[:, b, :], row_sum[:, b, :], sink_exp[:, b, :], ALU.add)
                            dve.drain()
                        dve.reciprocal(inv_sum[:, b, :], row_sum[:, b, :])
                        dve.drain()
                        dve.wait_ge(t_ready, tf.value(1, 1))
                        for half in range(2):
                            dve.tensor_tensor(attn[:, tt, grp * 256:(grp + 1) * 256].rearrange("p (i half d) -> p half i d", half=2, d=DH)[:, half],
                                              t_bank[tf.slot(2)][:, half * P:(half + 1) * P].rearrange("p (i d) -> p i d", d=DH),
                                              inv_sum[:, b, 2 * half:2 * half + 2].unsqueeze(2).to_broadcast([P, 2, DH]), ALU.mult)
                        dve.drain().then_inc(t_free[tf.slot(2)], 1)
                        dve.sem_inc(attn_ready, 1)
                dve_xt(t + T_AFTER_MIX1, At(4, (l, 16)), 2)
                dve.wait_ge(gate_ready, 6 * l + 6)
                for blk in range(2):
                    for half in range(2):
                        ahead(u + 22, 2 * blk + half)
                        unit_is_used(dve, u + (22 + 2 * blk + half))
                        fence(dve)
                        for br in ((0, 1) if half == 0 else (2,)):
                            for tt in range(TT):
                                b = (f + (24 + 6 * blk + 2 * br + tt)).slot(4)
                                g_ = gate[:, tt, br * DM + blk * 512:br * DM + blk * 512 + 512]
                                m_ = merged[:, tt, blk * 512:(blk + 1) * 512]
                                dve.drain()
                                dve.scalar_tensor_tensor(out=m_ if br == 0 else gated[:, tt, :], in0=g_, scalar=1.0, in1=g_bank[b][:, :],
                                                         op0=ALU.add, op1=ALU.mult).then_inc(g_free[b], 1)
                                if br:
                                    dve.drain()
                                    dve.tensor_tensor(m_, m_, gated[:, tt, :], ALU.add)
                    dve.drain().then_inc(merged_ready, 1)
                dve_xt(t + (T_AFTER_MIX1 + 4), At(8, (l, 16)), 2)
                for blk in range(2):
                    ahead(u + 26, 2 * blk)
                    ahead(u + 26, 2 * blk + 1)
                    unit_is_used(dve, u + (26 + 2 * blk + 1))
                    for tt in range(TT):
                        b = (f + (36 + 2 * blk + tt)).slot(4)
                        xs = x[:, tt, blk * 512:(blk + 1) * 512]
                        dve.scalar_tensor_tensor(out=xs, in0=xs, scalar=2 * ALPHA, in1=g_bank[b][:, :], op0=ALU.mult,
                                                 op1=ALU.add).then_inc(g_free[b], 1)
                    for tt in range(TT):
                        row_stats(x, tt, blk)
                layer_norm(x, x, At(0, (l, 2)), gains[:, 0, :], gains[:, 1, :], 64 * l + 32, times=2)
                dve_xt(t + (T_AFTER_MIX1 + 8), At(12, (l, 16)), 2)

                dve.wait_ge(aff_ready, l + 1)
                dve.tensor_tensor(sel[:, :, :], aff[:, :, :], b_router[:, :].unsqueeze(1).to_broadcast([P, TT, NE]), ALU.add)
                dve.drain()
                s4 = sel[:, :, :].rearrange("p t (g e) -> p (t g) e", e=EPG)
                dve.tensor_tensor(pair[:, :, 0:3], s4[:, :, 0:3], s4[:, :, 1:4], ALU.add)
                dve.tensor_tensor(pair[:, :, 3:5], s4[:, :, 0:2], s4[:, :, 2:4], ALU.add)
                dve.tensor_tensor(pair[:, :, 5:6], s4[:, :, 0:1], s4[:, :, 3:4], ALU.add)
                dve.drain()
                dve.tensor_reduce(grp_score[:, :, :].rearrange("p t g -> p (t g)"), pair[:, :, :], AX.X, ALU.max)
                dve.drain()
                all_equal_max(grp_score[:, :, :], c("first_of4"), NG, in_grp[:, :, :])
                dve.drain().then_inc(in_grp_ready, 1)
                tf = t + (T_AFTER_MIX1 + 13)
                dve.wait_ge(t_ready, tf.value(1, 1))
                dve.scalar_tensor_tensor(out=place[:, :, :], in0=t_bank[tf.slot(2)][:, 0:2 * NG].rearrange("p (t g) -> p t g", t=TT), scalar=1024.0, in1=in_grp[:, :, :],
                                         op0=ALU.add, op1=ALU.mult)
                dve.tensor_copy(n_grp[:, :], t_bank[tf.slot(2)][:, 2 * NG:3 * NG]).then_inc(t_free[tf.slot(2)], 1)
                dve.drain()
                dve.tensor_scalar(place[:, :, :], place[:, :, :], -1024.0, None, ALU.add)
                dve.tensor_reduce(rounds_f[:, :], n_grp[:, :], AX.X, ALU.max)
                dve.drain()
                dve.tensor_scalar(rounds_f[:, :], rounds_f[:, :], float(P), 1.0, ALU.is_gt, ALU.add)
                dve.drain()
                dve.tensor_copy(rounds_i[:, :], rounds_f[:, :])
                dve.drain().then_inc(rounds_ready, 1)

                def make_onehot():
                    dve.drain()
                    for tt in range(TT):
                        for g in range(NG):
                            dve.tensor_scalar(onehot[:, tt, g, :], c("iota"), place[:, tt, g:g + 1], None, ALU.is_equal)
                    dve.drain().then_inc(onehot_ready, 1)
                    dve.tensor_scalar(place[:, :, :], place[:, :, :], float(-P), None, ALU.add)

                make_onehot()
                dve.tensor_scalar(grp_score[:, :, :], in_grp[:, :, :], 1.0, -NEG, ALU.subtract, ALU.mult)
                dve.drain()
                dve.tensor_tensor(s4, s4, grp_score[:, :, :].rearrange("p t g -> p (t g)").unsqueeze(2).to_broadcast([P, TT * NG, EPG]), ALU.add)
                dve.drain()
                all_equal_max(sel[:, :, :], c("first_of16"), NE, hot1[:, :, :])
                dve.scalar_tensor_tensor(out=sel[:, :, :], in0=hot1[:, :, :], scalar=2 * NEG, in1=sel[:, :, :], op0=ALU.mult, op1=ALU.add)
                dve.drain()
                all_equal_max(sel[:, :, :], c("first_of16"), NE, hot2[:, :, :])
                dve.tensor_tensor(hot1[:, :, :], hot1[:, :, :], hot2[:, :, :], ALU.add)
                dve.drain()
                dve.tensor_tensor(comb[:, :, :], hot1[:, :, :], aff[:, :, :], ALU.mult)
                dve.drain()
                dve.tensor_reduce(best[:, :], comb[:, :, :], AX.X, ALU.add)
                dve.drain()
                dve.reciprocal(best[:, :], best[:, :])
                dve.drain()
                dve.tensor_tensor(comb[:, :, :], comb[:, :, :], best[:, :].unsqueeze(2).to_broadcast([P, TT, NE]), ALU.mult)
                dve.drain().then_inc(comb_ready, 1)
                for tt in range(TT):
                    dve.tensor_scalar(acc[:, tt, :], x[:, tt, :], ALPHA, None, ALU.mult)
                R = rounds_of(dve, l + 1)
                with dve.Fori(0, R) as r:
                    at_r = in_round(l, done + r)
                    rnd = done + r

                    def run(part, g):
                        count = plus(At(0, (rnd, 16)), 0, g, 4)
                        for what, e, half, place in walk(part, at_r, g):
                            if half is not None:
                                ahead(place)
                                if what == "up" and half == 1:
                                    b = expert_fill(at_r, what, g, e).slot(4)
                                    unit_is_used(dve, place)
                                    dve.wait_ge(silu_ready, count.value(1, e + 1))
                                    dve.scalar_tensor_tensor(out=hid[:, e % 2, :], in0=g_bank[b][:, :],
                                                             scalar=comb_slot[:, bass.ds(g * EPG + e, 1)], in1=silu_g[:, e % 2, :],
                                                             op0=ALU.mult, op1=ALU.mult).then_inc(g_free[b], 1)
                                    dve.drain().then_inc(hid_ready, 1)
                            elif what == "gather":
                                first_count = plus(At(0, (rnd, 8)), 1 if part == "start" else 3, g, 2)
                                for i in range(2):
                                    tf = place + i
                                    dve.wait_ge(xg_hi_ready, (first_count + i).value())
                                    dve.tensor_tensor(xg_lo[:, 4 * i:4 * i + 4, :], t_bank[tf.slot(2)][:, :].rearrange("p (a b) -> p a b", a=4),
                                                      xg_hi[:, 4 * i:4 * i + 4, :].bitcast(F32), ALU.subtract).then_inc(t_free[tf.slot(2)], 1)
                                dve.drain().then_inc(xg_ready, 1)
                            elif what == "slots":
                                dve.wait_ge(comb_slot_ready, rnd + 1)
                                fence(dve)
                            elif what == "hid_t":
                                dve.wait_ge(hid_hi_ready, count.value(1, e + 1))
                                dve.tensor_tensor(hid_t_lo[:, e % 2, :, :], t_bank[place.slot(2)][:, :].rearrange("p (a b) -> p a b", a=4),
                                                  hid_t_hi[:, e % 2, :, :].bitcast(F32), ALU.subtract).then_inc(t_free[place.slot(2)], 1)
                                dve.drain().then_inc(hid_t_ready, 1)
                            else:
                                dve.wait_ge(y_hi_ready, plus(At(0, (rnd, 4)), 1, g, 1).value())
                                dve.tensor_tensor(y_lo[:, bass.ds(g, 1), :], s_bank[:, :].unsqueeze(1), y_hi[:, bass.ds(g, 1), :].bitcast(F32),
                                                  ALU.subtract).then_inc(s_free, 1)
                                dve.drain().then_inc(y_ready, 1)

                    all_parts(dve, run)
                    make_onehot()
                    for i in range(4):
                        tt, nb = i // 2, i % 2
                        b = (at_r["g"] + (32 + i)).slot(4)
                        dve.wait_ge(returned, 4 * rnd + (i + 1))
                        a_ = acc[:, tt, nb * 512:(nb + 1) * 512]
                        dve.tensor_tensor(a_, a_, g_bank[b][:, :], ALU.add).then_inc(g_free[b], 1)
                        row_stats(acc, tt, nb)
                    dve.drain()
                dve.reg_add(rho, rho, R)
                layer_norm(acc, x, At(1, (l, 2)), gains[:, 0, :], gains[:, 1, :], 64 * l + 64)

            done = dve.snap(rho, min_val=0, max_val=4)
            with dve.Fori(0, DEPTH) as l:
                first, mixer, second = layer2(l, done)

                def norm_in(dst, i):
                    dve.wait_ge(pre_in, 48 * l + (16 * i + 16))
                    for tt in range(TT):
                        dve.tensor_tensor(dst[:, tt, :], x[:, tt, :], gains[:, 0, :], ALU.mult)
                        dve.drain().then_inc(normed_ready, 1)

                def in_root(n, sq):
                    dve.wait_ge(square_ready, 15 * l + (sq + 1))
                    dve.tensor_scalar(rstd_in[:, :], mean_sq[:, :, 0:1].rearrange("p a b -> p (a b)"), RMS_EPS, None, ALU.add)
                    dve.drain()
                    dve.reciprocal(rstd_in[:, :], rstd_in[:, :]).then_inc(var_ready, 1)
                    dve.wait_ge(rstd_ready, At(4 + n, (l, 11)).value(1, 1))
                    fence(dve)

                def norm_out(dst, n, sq, i, fills, factor, times=1):
                    dve.wait_ge(post_in, 48 * l + (16 * i + 16))
                    fence(dve)
                    for tt in range(TT):
                        for nb in range(2):
                            cols = slice(nb * 512, (nb + 1) * 512)
                            b = fills[tt][nb].slot(4)
                            dve.wait_ge(square_ready, 15 * l + (sq + 2 * tt + nb + 1))
                            dve.tensor_tensor(dst[:, tt, cols], g_bank[b][:, :], gains[:, 1, cols], ALU.mult).then_inc(g_free[b], 1)
                        dve.scalar_tensor_tensor(out=rstd[:, tt:tt + 1], in0=mean_sq[:, tt, 0:1], scalar=RMS_EPS * (times / factor) ** 2,
                                                 in1=mean_sq[:, tt, 1:2], op0=ALU.add, op1=ALU.add)
                        dve.drain()
                        dve.reciprocal(rstd[:, tt:tt + 1], rstd[:, tt:tt + 1]).then_inc(var_ready, 1)
                    for tt in range(TT):
                        dve.wait_ge(rstd_ready, At(4 + n + tt, (l, 11)).value(1, 1))
                        dve.scalar_tensor_tensor(out=x[:, tt, :], in0=dst[:, tt, :], scalar=rstd[:, tt:tt + 1], in1=x[:, tt, :],
                                                 op0=ALU.mult, op1=ALU.add)
                    dve.drain().then_inc(x_ready, 1)

                def feed_forward(at, n, sq, i, w, n_xt):
                    u, f, t = at["u"], at["g"], at["t"]
                    norm_in(ffn_y, i)
                    dve_xt(t, At(16 * DEPTH + n_xt, (l, XT_LAYER2)), 2)
                    in_root(n, sq)
                    q0 = At(w * FB, (l, 2 * FB))

                    def hidden(q):
                        dve.wait_ge(up_silu_ready, q.value(1, 1))
                        for tt in range(TT):
                            dve.scalar_tensor_tensor(out=ffn_hid[:, tt, :], in0=s_bank[:, tt * 512 + 256:(tt + 1) * 512],
                                                     scalar=rstd_in[:, tt:tt + 1], in1=ffn_silu[:, tt, :], op0=ALU.mult, op1=ALU.mult)
                        dve.drain().then_inc(ffn_hid_ready, 1)
                        dve.sem_inc(s_free, 1)

                    def hid_t(tj, q):
                        for tt in range(TT):
                            tf = tj + tt
                            dve.wait_ge(ffn_hi_ready, q.value(2, tt + 1))
                            part = slice(tt * P, (tt + 1) * P)
                            dve.tensor_tensor(ffn_t_lo[:, :, part], t_bank[tf.slot(2)][:, 0:256].rearrange("p (a b) -> p a b", a=2),
                                              ffn_t_hi[:, :, part].bitcast(F32), ALU.subtract).then_inc(t_free[tf.slot(2)], 1)
                        dve.drain().then_inc(ffn_t_ready, 1)

                    ahead(u)
                    ahead(u, 1)
                    hidden(q0)
                    hid_t(t + 4, q0)
                    ahead(u, 2)
                    ahead(u, 3)
                    hidden(q0 + 1)
                    ahead(u, 4)
                    hid_t(t + 6, q0 + 1)

                    with dve.Fori(2, FB) as j:
                        uj, tj, qj = (At(a.const + b, *a.terms, (j, k)) for a, b, k in ((u, -1, 3), (t, 4, 2), (q0, 0, 1)))
                        ahead(uj)
                        ahead(uj, 1)
                        hidden(qj)
                        ahead(uj, 2)
                        hid_t(tj, qj)
                    ahead(u, U_FFN - 1)
                    unit_is_used(dve, u + (U_FFN - 1))
                    fence(dve)
                    norm_out(ffn_y, n + 1, sq + 1, i, ffn_fills(f), 0.5)

                feed_forward(first, 0, 0, 0, 0, 0)

                u, f, t = mixer["u"], mixer["g"], mixer["t"]
                norm_in(mix_y, 1)
                dve_xt(t, At(16 * DEPTH + 4, (l, XT_LAYER2)), 2)
                in_root(3, 5)

                def convolve(a, b):
                    for k in range(a, b):
                        dve.drain()
                        for ch in range(3):
                            src = conv_in[:, ch, k:k + TT * P]
                            if k == 0:
                                dve.tensor_scalar(conv_y[:, ch, :], src, taps[:, ch, 0:1], taps[:, ch, TAPS:TAPS + 1], ALU.mult, ALU.add)
                            else:
                                dve.scalar_tensor_tensor(out=conv_y[:, ch, :], in0=src, scalar=taps[:, ch, k:k + 1], in1=conv_y[:, ch, :],
                                                         op0=ALU.mult, op1=ALU.add)
                    if b == TAPS:
                        dve.drain().then_inc(conv_y_ready, 1)

                for i, blk in enumerate(PROJ2_ORDER):
                    ahead(u, 2 * i)
                    ahead(u, 2 * i + 1)
                    if i == 2:
                        dve.wait_ge(proj_ready, 9 * l + 2)
                        for tt in range(TT):
                            dve.tensor_tensor(proj[:, tt, CONV:CONV + 512], proj[:, tt, CONV:CONV + 512], proj[:, tt, CONV + 512:CONV + 1024], ALU.mult)
                        dve.drain().then_inc(conv_u_ready, 1)
                    if i == 3:
                        dve.wait_ge(conv_in_ready, l + 1)
                        fence(dve)
                    if i >= 3:
                        convolve(4 * (i - 3), 4 * (i - 2))
                ahead(u, 16)

                for st in PLAN2:
                    kind = st["kind"]
                    if kind == "gate":
                        ahead(u, 17 + 2 * st["n"] + st["half"])
                        if st["taps"][1]:
                            convolve(*st["taps"])
                    elif kind == "scores":
                        tt, i = st["tt"], st["n"]
                        kn = P * (1 + tt)
                        mask = c("mask_earlier", 256 - kn)
                        dve.drain()
                        dve.wait_ge(s_ready, (mixer["s"] + st["s"]).value(1, 1))
                        for half in range(2):
                            dve.scalar_tensor_tensor(out=logits[i % 2][:, half, :, 0:kn], in0=s_half(half, kn), scalar=SCALE,
                                                     in1=mask.unsqueeze(1).to_broadcast([P, 2, kn]), op0=ALU.mult, op1=ALU.add)
                        dve.drain().then_inc(s_free, 1)
                        dve.sem_inc(logit_ready, 1)
                    elif kind == "scan":
                        i = st["n"]
                        kn = P * (1 + st["tt"])
                        dve.wait_ge(soft_ready, 4 * l + (i + 1))
                        fence(dve)
                        z, sp_ = logits[i % 2], soft_heads
                        for half in range(2):
                            dve.scalar_tensor_tensor(out=sp_[:, half, :, 0:kn], in0=z[:, half, :, 0:kn], scalar=0.0,
                                                     in1=sp_[:, half, :, 0:kn], op0=ALU.max, op1=ALU.add)
                        dve.drain()
                        for h in range(4):
                            row = soft[:, h, kn - 1::-1] if kn == 256 else soft[:, h, 0:kn][:, ::-1]
                            dve.tensor_tensor_scan(row, c("ones", 0, 1).to_broadcast([P, kn]), row, 0.0, ALU.mult, ALU.add)
                        dve.drain()
                        for half in range(2):
                            dve.tensor_tensor(z[:, half, :, 0:kn], z[:, half, :, 0:kn], sp_[:, half, :, 0:kn], ALU.subtract)
                        dve.drain().then_inc(log_w_ready, 1)
                    elif kind == "branches_t":
                        dve_xt(t + st["t"], At(16 * DEPTH + 8, (l, XT_LAYER2)), 2, EARLY_BRANCHES)
                    elif kind == "values":
                        tt, grp = st["tt"], st["grp"]
                        tf = t + st["t"]
                        dve.wait_ge(t_ready, tf.value(1, 1))
                        for half in range(2):
                            dve.tensor_copy(proj[:, tt, grp * 256:(grp + 1) * 256].rearrange("p (i half d) -> p half i d", half=2, d=DH)[:, half],
                                            t_bank[tf.slot(2)][:, half * P:(half + 1) * P].rearrange("p (i d) -> p i d", d=DH))
                        dve.drain().then_inc(t_free[tf.slot(2)], 1)
                        dve.sem_inc(branch_ready, 1)
                    elif kind == "conv_back":
                        dve.drain()
                        for tt in range(TT):
                            tf = t + (st["t"] + tt)
                            dve.wait_ge(t_ready, tf.value(1, 1))
                            dve.bn_stats(stats[:, tt, 0:6], t_bank[tf.slot(2)][:, :])
                        dve.drain()
                        for tt in range(TT):
                            dve.bn_aggr(mean_var[:, tt, :], stats[:, tt, 0:6])
                        dve.drain()
                        dve.tensor_scalar(mean_var[:, :, 1:2], mean_var[:, :, 1:2], RMS_EPS, None, ALU.add)
                        dve.drain()
                        dve.reciprocal(rstd[:, :], mean_var[:, :, 1:2].rearrange("p a b -> p (a b)")).then_inc(var_ready, 1)
                        conv_back_t = st["t"]
                    elif kind == "conv_norm":
                        dve.wait_ge(rstd_ready, At(4 + 4, (l, 11)).value(1, 1))
                        out_ = [proj[:, tt, ATTN2[1]:ATTN2[1] + 512] for tt in range(TT)]
                        for tt in range(TT):
                            tf = t + (conv_back_t + tt)
                            dve.tensor_scalar(out_[tt], t_bank[tf.slot(2)][:, :], mean_var[:, tt, 0:1], rstd[:, tt:tt + 1],
                                              ALU.subtract, ALU.mult).then_inc(t_free[tf.slot(2)], 1)
                        dve.drain()
                        for tt in range(TT):
                            dve.tensor_tensor(out_[tt], out_[tt], conv_row[:, 0:512], ALU.mult)
                        dve.drain()
                        for tt in range(TT):
                            dve.tensor_tensor(out_[tt], out_[tt], conv_row[:, 512:1024], ALU.add)
                        dve.drain().then_inc(conv_mid_ready, 1)
                    elif kind == "alpha":
                        dve.wait_ge(kv_lat_done, l + (DEPTH + 1))
                        dve.wait_ge(alpha_in, 48 * l + 48)
                        for tt in range(TT):
                            b = (f + (st["g"] + tt)).slot(4)
                            dve.scalar_tensor_tensor(out=log_alpha[:, tt, :], in0=g_bank[b][:, 0:256], scalar=rstd_in[:, tt:tt + 1], in1=b_alpha,
                                                     op0=ALU.mult, op1=ALU.add).then_inc(g_free[b], 1)
                        dve.drain().then_inc(alpha_in_ready, 1)
                    elif kind == "alpha_end":
                        dve.wait_ge(alpha_soft_ready, l + 1)
                        la = log_alpha.rearrange(flat)
                        dve.scalar_tensor_tensor(out=la, in0=la, scalar=0.0, in1=log_tmp, op0=ALU.min, op1=ALU.subtract)
                        dve.drain()
                        dve.tensor_scalar(la, la, 1.0 / 16.0, None, ALU.mult)
                        dve.drain().then_inc(log_alpha_ready, 1)
                    elif kind == "states":
                        dve.wait_ge(decay_ready, l + 1)
                        dve.tensor_tensor(decay, decay, proj[:, :, L_K:L_K + 256], ALU.mult)
                        dve.drain()
                        for tt in range(TT):
                            for c2 in range(2):
                                dve.tensor_scalar(k_dec[:, tt, c2, :], decay[:, tt, :], c("chunk_of", c2, c2 + 1), None, ALU.mult)
                        dve.drain().then_inc(k_dec_ready, 1)
                        block_mask = c("chunk_of").unsqueeze(1).unsqueeze(3).to_broadcast([P, 2, 2, P])
                        for ch in range(4):
                            tf = t + (st["t"] + ch)
                            dst = state[:, 0, :, :].rearrange("p h (v n) -> p h v n", v=2) if ch == 0 else kv_new.rearrange("p (h v n) -> p h v n", h=2, v=2)
                            dve.wait_ge(t_ready, tf.value(1, 1))
                            dve.tensor_tensor(dst, t_bank[tf.slot(2)][:, :].rearrange("p (h v n) -> p h v n", h=2, v=2), block_mask, ALU.mult)\
                               .then_inc(t_free[tf.slot(2)], 1)
                            dve.drain()
                            for h2 in range(2) if ch else ():
                                dve.scalar_tensor_tensor(out=state[:, ch, h2, :], in0=state[:, ch - 1, h2, :], scalar=lam[:, h2 * 4 + ch:h2 * 4 + ch + 1],
                                                         in1=kv_new[:, h2 * 256:(h2 + 1) * 256], op0=ALU.mult, op1=ALU.add)
                            dve.drain().then_inc(state_ready, 1)
                    elif kind == "gla_out":
                        for tt in range(TT):
                            tf = t + (st["t"] + tt)
                            dve.wait_ge(t_ready, tf.value(1, 1))
                            dve.tensor_copy(gla_o[:, tt, :], t_bank[tf.slot(2)][:, :]).then_inc(t_free[tf.slot(2)], 1)
                            dve.drain()
                            dve.tensor_tensor(kv_new, gla_o[:, tt, :], gla_o[:, tt, :], ALU.mult)
                            dve.drain()
                            dve.tensor_reduce(mean_sq8[:, tt, :], kv_new.rearrange("p (h n) -> p h n", h=4), AX.X, ALU.add)
                        dve.drain()
                        dve.tensor_scalar(mean_sq8[:, :, :], mean_sq8[:, :, :], 1.0 / 128.0, RMS_EPS, ALU.mult, ALU.add)
                        dve.drain()
                        dve.reciprocal(mean_sq8[:, :, :], mean_sq8[:, :, :]).then_inc(var_ready, 1)
                        dve.wait_ge(rstd_ready, At(4 + 5, (l, 11)).value(1, 1))
                        for tt in range(TT):
                            dve.tensor_tensor(gla_o[:, tt, :].rearrange("p (h n) -> p h n", h=4), gla_o[:, tt, :].rearrange("p (h n) -> p h n", h=4),
                                              mean_sq8[:, tt, :].unsqueeze(2).to_broadcast([P, 4, P]), ALU.mult)
                        dve.drain()
                        for tt in range(TT):
                            dve.tensor_tensor(gla_o[:, tt, :], gla_o[:, tt, :], gla_gain, ALU.mult)
                        dve.drain()
                        for tt in range(TT):
                            dve.tensor_tensor(proj[:, tt, ATTN2[2]:ATTN2[2] + 512], gla_o[:, tt, :], proj[:, tt, L_R:L_R + 512], ALU.mult)
                        dve.drain().then_inc(gla_ready, 1)
                dve_xt(t + T_AFTER_MIX2, At(16 * DEPTH + 12, (l, XT_LAYER2)), 1, LAST_BRANCH)
                dve.wait_ge(gate2_ready, 6 * l + 6)
                for blk in range(2):
                    for br in range(3):
                        k = 3 * blk + br
                        ahead(u + 29, k)
                        unit_is_used(dve, u + (29 + k))
                        fence(dve)
                        for tt in range(TT):
                            b = (f + (32 + 6 * blk + 2 * br + tt)).slot(4)
                            g_ = gate2[:, tt, br * DM + blk * 512:br * DM + blk * 512 + 512]
                            m_ = merged2[:, tt, blk * 512:(blk + 1) * 512]
                            tmp = gla_o[:, tt, :]
                            dve.drain()
                            dve.scalar_tensor_tensor(out=m_ if br == 0 else tmp, in0=g_, scalar=1.0, in1=g_bank[b][:, :],
                                                     op0=ALU.add, op1=ALU.mult).then_inc(g_free[b], 1)
                            if br:
                                dve.drain()
                                dve.tensor_tensor(m_, m_, tmp, ALU.add)
                    dve.drain().then_inc(merged2_ready, 1)
                dve_xt(t + (T_AFTER_MIX2 + 2), At(16 * DEPTH + 14, (l, XT_LAYER2)), 2)
                for k in range(4):
                    ahead(u + 35, k)
                unit_is_used(dve, u + 38)
                fence(dve)
                norm_out(mix_y, 6, 6, 1, mix_fills(f), 1.0, times=2)

                feed_forward(second, 8, 10, 2, 1, 18)


def kernel(**inputs):
    import numpy as _np
    import concourse.bacc as _bacc
    from concourse import mybir as _mybir
    from concourse.bass_utils import run_bass_kernel_spmd as _run

    nc = _bacc.Bacc("TRN2", target_bir_lowering=False, num_devices=1)
    table, const_at = shape_constants()
    arrays, d = {}, {}
    for name, a in dict(inputs, shape_constants=table).items():
        a = _np.ascontiguousarray(a)
        arrays[f"in_{name}_dram"] = a
        d[name] = nc.dram_tensor(f"in_{name}_dram", a.shape, _mybir.dt.from_np(a.dtype), kind="ExternalInput").ap()
    d["out_0_dram"] = nc.dram_tensor("out_0_dram", (1, TT * P, DM), F32, kind="ExternalOutput").ap()
    build(nc, d, const_at)
    r = _run(nc, [arrays], core_ids=[0])
    return r.results[0]["out_0_dram"]
```
